# Optimizing a Trainium2 kernel written in Bass

```python
import math, functools
import jax, jax.numpy as jnp
from jax import lax
import numpy as np
import math
import jax
import jax.numpy as jnp

D_MODEL = 1024
BATCH = 1
SEQ = 512
DEPTH = 2

GRID_W = 64
CTX_LEN = 256
HEAD_DIM = 64
ROPE_THETA = 10000.0
ROPE_FREQS = HEAD_DIM // 4
Q_BLOCK = 128
A_HEADS = 8
A_KV_HEADS = 2
B_HEADS = 4
B_V_DIM = 2 * HEAD_DIM
C_HEADS = 8
C_KV_HEADS = 2
C_WINDOW = 128
D_HEADS = 8
NA_ROWS = 8
NA_COLS = 16
EVEN_SPLITS = (A_HEADS * HEAD_DIM, A_KV_HEADS * HEAD_DIM, A_KV_HEADS * HEAD_DIM,
               2 * B_HEADS * HEAD_DIM, 2 * B_HEADS * HEAD_DIM, B_HEADS * B_V_DIM)
ODD_SPLITS = (C_HEADS * HEAD_DIM, C_KV_HEADS * HEAD_DIM, C_KV_HEADS * HEAD_DIM,
              D_HEADS * HEAD_DIM, D_HEADS * HEAD_DIM, D_HEADS * HEAD_DIM)
IN_WIDTH = sum(EVEN_SPLITS)
MIX_WIDTH = A_HEADS * HEAD_DIM + B_HEADS * B_V_DIM
D_FF = 4 * D_MODEL
N_EVEN = (DEPTH + 1) // 2
N_ODD = DEPTH // 2
EPS = 1e-6
NEG = -1e30


def split_cols(p, sizes):
    return jnp.split(p, np.cumsum(sizes)[:-1].tolist(), axis=-1)

def rms_norm(x, g):
    xf = x.astype(jnp.float32)
    y = xf * lax.rsqrt(jnp.mean(jnp.square(xf), axis=-1, keepdims=True) + EPS)
    return (y * g.astype(jnp.float32)).astype(x.dtype)

def modulate(h, shift, scale):
    return h * (1 + scale) + shift

def lambda_init(layer):
    return 0.8 - 0.6 * math.exp(-0.3 * layer)

def axial_rope_tables(T, dtype):
    t = jnp.arange(T, dtype=jnp.int32)
    pos = jnp.stack([t // GRID_W, t % GRID_W], axis=-1).astype(jnp.float32)
    inv = ROPE_THETA ** (-jnp.arange(ROPE_FREQS, dtype=jnp.float32) / ROPE_FREQS)
    ang = pos[..., None] * inv
    return jnp.cos(ang).astype(dtype), jnp.sin(ang).astype(dtype)

def apply_axial_rope(x, cos, sin):
    xs = x.reshape(x.shape[:-1] + (2, 2, ROPE_FREQS))
    x1, x2 = xs[..., 0, :], xs[..., 1, :]
    c, s = cos[:, None], sin[:, None]
    return jnp.stack([x1 * c - x2 * s, x2 * c + x1 * s], axis=-2).reshape(x.shape)

def map_query_blocks(fn, *qs):
    B, T = qs[0].shape[:2]
    nb = T // Q_BLOCK
    blocks = tuple(jnp.moveaxis(a.reshape((B, nb, Q_BLOCK) + a.shape[2:]), 1, 0) for a in qs)
    out = lax.map(lambda args: fn(*args), blocks)
    return jnp.moveaxis(out, 0, 1).reshape((B, T) + out.shape[3:])

def gqa_attend(q, k, v):
    s = jnp.einsum('bqkgd,bskd->bkgqs', q, k).astype(jnp.float32)
    p = jax.nn.softmax(s, axis=-1).astype(v.dtype)
    return jnp.einsum('bkgqs,bskd->bqkgd', p, v)

def diff_attend(q, k, v, lam):
    s = jnp.einsum('bqhjd,bshjd->bhjqs', q, k).astype(jnp.float32)
    p = jax.nn.softmax(s, axis=-1)
    a = (p[:, :, 0] - lam * p[:, :, 1]).astype(v.dtype)
    return jnp.einsum('bhqs,bshe->bqhe', a, v)

def sink_attend(q, k, v, sink):
    s = jnp.einsum('bqkgd,bskd->bkgqs', q, k).astype(jnp.float32)
    sk = jnp.broadcast_to(sink.astype(jnp.float32)[None, :, :, None, None], s.shape[:-1] + (1,))
    p = jax.nn.softmax(jnp.concatenate([sk, s], axis=-1), axis=-1)[..., 1:].astype(v.dtype)
    return jnp.einsum('bkgqs,bskd->bqkgd', p, v)

def windowed_attend(q, k, v, k_ctx, v_ctx, sink):
    B, T = q.shape[:2]
    L = k_ctx.shape[1]
    nb = T // C_WINDOW

    def band(a):
        ap = jnp.pad(a, ((0, 0), (C_WINDOW, C_WINDOW), (0, 0), (0, 0)))
        ap = ap.reshape((B, nb + 2, C_WINDOW) + a.shape[2:])
        return jnp.concatenate([ap[:, :-2], ap[:, 1:-1], ap[:, 2:]], axis=2)

    kb, vb = band(k), band(v)
    qb = q.reshape((B, nb, C_WINDOW) + q.shape[2:])
    i = jnp.arange(C_WINDOW)[:, None]
    j = jnp.arange(3 * C_WINDOW)[None, :]
    kpos = jnp.arange(nb)[:, None, None] * C_WINDOW - C_WINDOW + j
    valid = (jnp.abs(j - C_WINDOW - i) <= C_WINDOW)[None] & (kpos >= 0) & (kpos < T)
    s_loc = jnp.einsum('bnqkgd,bnskd->bnkgqs', qb, kb).astype(jnp.float32)
    s_loc = jnp.where(valid[None, :, None, None], s_loc, NEG)
    s_ctx = jnp.einsum('bnqkgd,bskd->bnkgqs', qb, k_ctx).astype(jnp.float32)
    sk = jnp.broadcast_to(sink.astype(jnp.float32)[None, None, :, :, None, None], s_ctx.shape[:-1] + (1,))
    p = jax.nn.softmax(jnp.concatenate([sk, s_ctx, s_loc], axis=-1), axis=-1)
    p_ctx = p[..., 1:1 + L].astype(v.dtype)
    p_loc = p[..., 1 + L:].astype(v.dtype)
    o = (jnp.einsum('bnkgqs,bskd->bnqkgd', p_ctx, v_ctx)
         + jnp.einsum('bnkgqs,bnskd->bnqkgd', p_loc, vb))
    return o.reshape(q.shape)

def neighborhood_attend(q, k, v, k_ctx, v_ctx, rpb):
    B, T, H, Dh = q.shape
    rows = T // GRID_W
    kh = min(NA_ROWS, rows)
    kw = NA_COLS
    L = k_ctx.shape[1]
    r = jnp.arange(rows)
    rs = jnp.clip(r - kh // 2, 0, rows - kh)
    row_idx = rs[:, None] + jnp.arange(kh)[None, :]

    def gather_rows(a):
        return a.reshape(B, rows, GRID_W, H, Dh)[:, row_idx].reshape(B, rows, kh * GRID_W, H, Dh)

    kg, vg = gather_rows(k), gather_rows(v)
    qg = q.reshape(B, rows, GRID_W, H, Dh)
    cq = jnp.arange(GRID_W)
    cs = jnp.clip(cq - kw // 2, 0, GRID_W - kw)
    ck = jnp.tile(jnp.arange(GRID_W), kh)
    col_valid = (ck[None] >= cs[:, None]) & (ck[None] < cs[:, None] + kw)
    dr = jnp.repeat(row_idx - r[:, None], GRID_W, axis=1)
    dc = jnp.clip(ck[None] - cq[:, None], -(kw - 1), kw - 1)
    bias = rpb[:, dr[:, None, :] + NA_ROWS - 1, dc[None] + NA_COLS - 1]
    bias = jnp.moveaxis(bias, 0, 1).astype(jnp.float32)
    s_loc = jnp.einsum('brqhd,brshd->brhqs', qg, kg).astype(jnp.float32) + bias
    s_loc = jnp.where(col_valid, s_loc, NEG)
    s_ctx = jnp.einsum('brqhd,bshd->brhqs', qg, k_ctx).astype(jnp.float32)
    p = jax.nn.softmax(jnp.concatenate([s_ctx, s_loc], axis=-1), axis=-1)
    p_ctx = p[..., :L].astype(v.dtype)
    p_loc = p[..., L:].astype(v.dtype)
    o = (jnp.einsum('brhqs,bshd->brqhd', p_ctx, v_ctx)
         + jnp.einsum('brhqs,brshd->brqhd', p_loc, vg))
    return o.reshape(B, T, H * Dh)

def even_mixer(h_x, h_c, w_in, w_out, qk_g, lam_p, subln_g, lam0, cos, sin, with_ctx):
    scale = HEAD_DIM ** -0.5
    g_a = A_HEADS // A_KV_HEADS

    def project(h, rope):
        n, s = h.shape[:2]
        qa, ka, va, qb, kb, vb = split_cols(h @ w_in, EVEN_SPLITS)
        qa = rms_norm(qa.reshape(n, s, A_HEADS, HEAD_DIM), qk_g[0])
        ka = rms_norm(ka.reshape(n, s, A_KV_HEADS, HEAD_DIM), qk_g[1])
        qb = qb.reshape(n, s, 2 * B_HEADS, HEAD_DIM)
        kb = kb.reshape(n, s, 2 * B_HEADS, HEAD_DIM)
        if rope:
            qa, ka = apply_axial_rope(qa, cos, sin), apply_axial_rope(ka, cos, sin)
            qb, kb = apply_axial_rope(qb, cos, sin), apply_axial_rope(kb, cos, sin)
        return ((qa * scale).reshape(n, s, A_KV_HEADS, g_a, HEAD_DIM), ka,
                va.reshape(n, s, A_KV_HEADS, HEAD_DIM),
                (qb * scale).reshape(n, s, B_HEADS, 2, HEAD_DIM),
                kb.reshape(n, s, B_HEADS, 2, HEAD_DIM),
                vb.reshape(n, s, B_HEADS, B_V_DIM))

    lam = (jnp.exp(jnp.sum(lam_p[0] * lam_p[1]).astype(jnp.float32))
           - jnp.exp(jnp.sum(lam_p[2] * lam_p[3]).astype(jnp.float32)) + lam0)
    qa_x, ka_x, va_x, qb_x, kb_x, vb_x = project(h_x, True)
    qa_c, ka_c, va_c, qb_c, kb_c, vb_c = project(h_c, False)
    ka_all = jnp.concatenate([ka_c, ka_x], axis=1)
    va_all = jnp.concatenate([va_c, va_x], axis=1)
    kb_all = jnp.concatenate([kb_c, kb_x], axis=1)
    vb_all = jnp.concatenate([vb_c, vb_x], axis=1)
    B, T = h_x.shape[:2]
    o_a = map_query_blocks(lambda q: gqa_attend(q, ka_all, va_all), qa_x).reshape(B, T, -1)
    o_b = map_query_blocks(lambda q: diff_attend(q, kb_all, vb_all, lam), qb_x)
    o_b = (rms_norm(o_b, subln_g) * (1 - lam0)).reshape(B, T, -1)
    out_x = jnp.concatenate([o_a, o_b], axis=-1) @ w_out
    out_c = None
    if with_ctx:
        n, L = h_c.shape[:2]
        oa_c = gqa_attend(qa_c, ka_c, va_c).reshape(n, L, -1)
        ob_c = (rms_norm(diff_attend(qb_c, kb_c, vb_c, lam), subln_g) * (1 - lam0)).reshape(n, L, -1)
        out_c = jnp.concatenate([oa_c, ob_c], axis=-1) @ w_out
    return out_x, out_c

def odd_mixer(h_x, h_c, w_in, w_out, sink, rpb, cos, sin, with_ctx):
    scale = HEAD_DIM ** -0.5
    g_c = C_HEADS // C_KV_HEADS
    sink = sink.reshape(C_KV_HEADS, g_c)

    def project(h, rope):
        n, s = h.shape[:2]
        qc, kc, vc, qd, kd, vd = split_cols(h @ w_in, ODD_SPLITS)
        qc = qc.reshape(n, s, C_HEADS, HEAD_DIM)
        kc = kc.reshape(n, s, C_KV_HEADS, HEAD_DIM)
        if rope:
            qc, kc = apply_axial_rope(qc, cos, sin), apply_axial_rope(kc, cos, sin)
        return ((qc * scale).reshape(n, s, C_KV_HEADS, g_c, HEAD_DIM), kc,
                vc.reshape(n, s, C_KV_HEADS, HEAD_DIM),
                qd.reshape(n, s, D_HEADS, HEAD_DIM) * scale,
                kd.reshape(n, s, D_HEADS, HEAD_DIM),
                vd.reshape(n, s, D_HEADS, HEAD_DIM))

    qc_x, kc_x, vc_x, qd_x, kd_x, vd_x = project(h_x, True)
    qc_c, kc_c, vc_c, qd_c, kd_c, vd_c = project(h_c, False)
    B, T = h_x.shape[:2]
    o_c = windowed_attend(qc_x, kc_x, vc_x, kc_c, vc_c, sink).reshape(B, T, -1)
    o_d = neighborhood_attend(qd_x, kd_x, vd_x, kd_c, vd_c, rpb)
    out_x = jnp.concatenate([o_c, o_d], axis=-1) @ w_out
    out_c = None
    if with_ctx:
        n, L = h_c.shape[:2]
        oc_c = sink_attend(qc_c, kc_c, vc_c, sink).reshape(n, L, -1)
        od_c = gqa_attend(qd_c[:, :, :, None], kd_c, vd_c).reshape(n, L, -1)
        out_c = jnp.concatenate([oc_c, od_c], axis=-1) @ w_out
    return out_x, out_c

def squared_relu_mlp(h, w1, w2):
    return jnp.square(jax.nn.relu(h @ w1)) @ w2

def first_inputs(seed: int = 0) -> dict:
    key = jax.random.key(seed)
    ks = jax.random.split(key, 16)
    f32 = jnp.float32

    def nrm(k, shape, s):
        return jax.random.normal(k, shape, f32) * s

    return {
        "x": nrm(ks[0], (BATCH, SEQ, D_MODEL), 1.0),
        "c": nrm(ks[1], (BATCH, D_MODEL), 1.0),
        "ctx": nrm(ks[2], (BATCH, CTX_LEN, D_MODEL), 1.0),
        "c_ctx": nrm(ks[3], (D_MODEL,), 1.0),
        "w_mod": nrm(ks[4], (DEPTH, D_MODEL, 6 * D_MODEL), D_MODEL ** -0.5),
        "b_mod": nrm(ks[5], (DEPTH, 6 * D_MODEL), 0.02),
        "norm_g": 1.0 + nrm(ks[6], (DEPTH, 4, D_MODEL), 0.02),
        "w_in": nrm(ks[7], (DEPTH, D_MODEL, IN_WIDTH), D_MODEL ** -0.5),
        "w_out": nrm(ks[8], (DEPTH, MIX_WIDTH, D_MODEL), MIX_WIDTH ** -0.5),
        "w_mlp_in": nrm(ks[9], (DEPTH, D_MODEL, D_FF), D_MODEL ** -0.5),
        "w_mlp_out": nrm(ks[10], (DEPTH, D_FF, D_MODEL), D_FF ** -0.5),
        "qk_norm_a": 1.0 + nrm(ks[11], (N_EVEN, 2, HEAD_DIM), 0.02),
        "diff_lambda": nrm(ks[12], (N_EVEN, 4, HEAD_DIM), 0.1),
        "diff_subln": 1.0 + nrm(ks[13], (N_EVEN, B_V_DIM), 0.02),
        "sink_c": nrm(ks[14], (N_ODD, C_HEADS), 0.5),
        "rpb_d": nrm(ks[15], (N_ODD, D_HEADS, 2 * NA_ROWS - 1, 2 * NA_COLS - 1), 0.1),
    }

def first_block(x, c, ctx, c_ctx, w_mod, b_mod, norm_g, w_in, w_out, w_mlp_in, w_mlp_out,
              qk_norm_a, diff_lambda, diff_subln, sink_c, rpb_d):
    T = x.shape[1]
    cos, sin = axial_rope_tables(T, x.dtype)
    s_x = jax.nn.silu(c)
    s_c = jax.nn.silu(c_ctx)
    for l in range(DEPTH):
        last = l == DEPTH - 1
        mod_x = (s_x @ w_mod[l] + b_mod[l])[:, None, :]
        mod_c = s_c @ w_mod[l] + b_mod[l]
        sh1_x, sc1_x, g1_x, sh2_x, sc2_x, g2_x = jnp.split(mod_x, 6, axis=-1)
        sh1_c, sc1_c, g1_c, sh2_c, sc2_c, g2_c = jnp.split(mod_c, 6, axis=-1)
        h_x = modulate(rms_norm(x, norm_g[l, 0]), sh1_x, sc1_x)
        h_c = modulate(rms_norm(ctx, norm_g[l, 0]), sh1_c, sc1_c)
        if l % 2 == 0:
            i = l // 2
            m_x, m_c = even_mixer(h_x, h_c, w_in[l], w_out[l], qk_norm_a[i], diff_lambda[i],
                                  diff_subln[i], lambda_init(l), cos, sin, not last)
        else:
            i = l // 2
            m_x, m_c = odd_mixer(h_x, h_c, w_in[l], w_out[l], sink_c[i], rpb_d[i],
                                 cos, sin, not last)
        x = x + g1_x * rms_norm(m_x, norm_g[l, 1])
        f_x = squared_relu_mlp(modulate(rms_norm(x, norm_g[l, 2]), sh2_x, sc2_x), w_mlp_in[l], w_mlp_out[l])
        x = x + g2_x * rms_norm(f_x, norm_g[l, 3])
        if not last:
            ctx = ctx + g1_c * rms_norm(m_c, norm_g[l, 1])
            f_c = squared_relu_mlp(modulate(rms_norm(ctx, norm_g[l, 2]), sh2_c, sc2_c), w_mlp_in[l], w_mlp_out[l])
            ctx = ctx + g2_c * rms_norm(f_c, norm_g[l, 3])
    return x


DEPTH_2 = 1

MIX_WIDTH_2 = D_MODEL
MLSTM_WIDTH = MIX_WIDTH_2 // 2
MLSTM_HEADS = 4
MLSTM_HEAD_DIM = MLSTM_WIDTH // MLSTM_HEADS
MLSTM_CHUNK = 128
MLSTM_M_INIT = -1e30
HYENA_WIDTH = MIX_WIDTH_2 - MLSTM_WIDTH
HYENA_GROUPS = 4
HYENA_GROUP_DIM = HYENA_WIDTH // HYENA_GROUPS
HYENA_ORDER = 2
HYENA_DIRS = 2
HYENA_BANDS = 16
HYENA_EMB_DIM = 1 + 2 * HYENA_BANDS
HYENA_FILTER_HIDDEN = 64
HYENA_WINDOW_SHIFT = 0.05
HYENA_SLOW_DECAY = -math.log(1e-2) / 1.5
HYENA_FAST_DECAY = -math.log(1e-2) / 0.3
SHORT_CONV = 3
N_GATE_COLS = 4 * MLSTM_HEADS
PROJ_COLS = 4 * MLSTM_WIDTH + N_GATE_COLS + (HYENA_ORDER + 1) * HYENA_WIDTH
N_EXPERTS = 16
EC_CAPACITY_FACTOR = 2
EXPERT_FF = 2 * D_MODEL
RMS_EPS = 1e-6


def rms_norm_2(x, g):
    xf = x.astype(jnp.float32)
    y = xf * lax.rsqrt(jnp.mean(xf * xf, axis=-1, keepdims=True) + RMS_EPS)
    return (y * g.astype(jnp.float32)).astype(x.dtype)

def centred_short_conv(u, w, b):
    S = u.shape[1]
    r = SHORT_CONV // 2
    up = jnp.pad(u, ((0, 0), (r, r), (0, 0)))
    y = b
    for j in range(SHORT_CONV):
        y = y + up[:, j:j + S] * w[j]
    return y

def mlstm_scan(q, k, v, i_pre, logf):
    B, H, S, Dh = q.shape
    nc = S // MLSTM_CHUNK
    qc = q.reshape(B, H, nc, MLSTM_CHUNK, Dh)
    kc = k.reshape(B, H, nc, MLSTM_CHUNK, Dh)
    vc = v.reshape(B, H, nc, MLSTM_CHUNK, Dh)
    ic = i_pre.reshape(B, H, nc, MLSTM_CHUNK)
    b = jnp.cumsum(logf.reshape(B, H, nc, MLSTM_CHUNK), axis=-1)
    g = b[..., -1]
    w_end = g[..., None] - b + ic
    a = jnp.max(w_end, axis=-1)
    e_end = jnp.exp(w_end - a[..., None])
    c_loc = jnp.einsum('bhcsv,bhcsk->bhcvk', vc * e_end[..., None], kc)
    n_loc = jnp.einsum('bhcs,bhcsk->bhck', e_end, kc)

    def step(carry, inp):
        c_st, n_st, m_st = carry
        g_j, a_j, c_j, n_j = inp
        m_new = jnp.maximum(g_j + m_st, a_j)
        s_prev = jnp.exp(g_j + m_st - m_new)
        s_loc = jnp.exp(a_j - m_new)
        c_new = s_prev[..., None, None] * c_st + s_loc[..., None, None] * c_j
        n_new = s_prev[..., None] * n_st + s_loc[..., None] * n_j
        return (c_new, n_new, m_new), (c_st, n_st, m_st)

    init = (jnp.zeros((B, H, Dh, Dh), q.dtype), jnp.zeros((B, H, Dh), q.dtype),
            jnp.full((B, H), MLSTM_M_INIT, q.dtype))
    xs = tuple(jnp.moveaxis(t, 2, 0) for t in (g, a, c_loc, n_loc))
    _, (c_in, n_in, m_in) = lax.scan(step, init, xs)
    c_in = jnp.moveaxis(c_in, 0, 2)
    n_in = jnp.moveaxis(n_in, 0, 2)
    m_in = jnp.moveaxis(m_in, 0, 2)

    tri = jnp.tril(jnp.ones((MLSTM_CHUNK, MLSTM_CHUNK), dtype=bool))
    log_d = jnp.where(tri, b[..., :, None] - b[..., None, :] + ic[..., None, :], -jnp.inf)
    log_inter = b + m_in[..., None]
    m_t = jnp.maximum(log_inter, jnp.max(log_d, axis=-1))
    d = jnp.exp(log_d - m_t[..., None])
    e_inter = jnp.exp(log_inter - m_t)
    s = jnp.einsum('bhctd,bhcsd->bhcts', qc, kc) * d
    num = (jnp.einsum('bhcts,bhcsd->bhctd', s, vc)
           + e_inter[..., None] * jnp.einsum('bhcvk,bhctk->bhctv', c_in, qc))
    den = jnp.sum(s, axis=-1) + e_inter * jnp.einsum('bhck,bhctk->bhct', n_in, qc)
    nrm = jnp.maximum(jnp.abs(den), jnp.exp(-m_t))
    return (num / nrm[..., None]).reshape(B, H, S, Dh)

def mlstm_mixer(q, k, v, o, gates, conv_w, conv_b, norm_g):
    B, S, _ = q.shape
    H, Dh = MLSTM_HEADS, MLSTM_HEAD_DIM
    qk = jax.nn.silu(centred_short_conv(jnp.concatenate([q, k], axis=-1), conv_w, conv_b))
    q, k = jnp.split(qk, 2, axis=-1)

    def heads(t):
        return t.reshape(B, S, H, Dh).transpose(0, 2, 1, 3).astype(jnp.float32)

    qh, kh, vh = heads(q), heads(k) * (MLSTM_HEAD_DIM ** -0.5), heads(v)
    g4 = gates.reshape(B, S, 4, H).transpose(2, 0, 3, 1).astype(jnp.float32)
    i_f, f_f, i_b, f_b = g4[0], g4[1], g4[2], g4[3]
    h_f = mlstm_scan(qh, kh, vh, i_f, jax.nn.log_sigmoid(f_f))

    def fl(t):
        return jnp.flip(t, axis=2)

    h_b = fl(mlstm_scan(fl(qh), fl(kh), fl(vh), fl(i_b), fl(jax.nn.log_sigmoid(f_b))))
    hsum = (h_f + h_b).transpose(0, 2, 1, 3)
    hn = rms_norm_2(hsum, norm_g.reshape(H, Dh)).reshape(B, S, MLSTM_WIDTH)
    return (jax.nn.sigmoid(o.astype(jnp.float32)) * hn).astype(o.dtype)

def hyena_filters(L, w1, b1, w2, b2, w3, freq, deltas):
    f32 = jnp.float32
    t = jnp.linspace(0.0, 1.0, L, dtype=f32)[:, None]
    w = 2.0 * math.pi * jnp.arange(L, dtype=f32)[:, None] / L
    bands = jnp.linspace(1e-4, HYENA_BANDS - 1, HYENA_BANDS, dtype=f32)[None, :]
    z = jnp.concatenate([t, jnp.cos(bands * w), -jnp.sin(bands * w)], axis=-1)
    fr = freq.astype(f32)
    hid = jnp.sin(fr * (z @ w1.astype(f32) + b1.astype(f32)))
    hid = jnp.sin(fr * (hid @ w2.astype(f32) + b2.astype(f32)))
    h = hid @ w3.astype(f32)
    window = jnp.exp(-t * jnp.abs(deltas.astype(f32))) + HYENA_WINDOW_SHIFT
    return (h * window).reshape(L, HYENA_ORDER, HYENA_DIRS, HYENA_WIDTH)

def bidir_long_conv(u, h_fwd, h_bwd, bias):
    L, C = h_fwd.shape
    two_sided = jnp.concatenate([(h_fwd[0] + h_bwd[0])[None], h_fwd[1:],
                                 jnp.zeros((1, C), jnp.float32), jnp.flip(h_bwd[1:], axis=0)], axis=0)
    k_f = jnp.fft.rfft(two_sided, n=2 * L, axis=0)
    uf = u.astype(jnp.float32)
    u_f = jnp.fft.rfft(uf, n=2 * L, axis=1)
    y = jnp.fft.irfft(u_f * k_f[None], n=2 * L, axis=1)[:, :L]
    return (y + uf * bias.astype(jnp.float32)).astype(u.dtype)

def hyena_mixer(hx, conv_w, conv_b, filt, bias, norm_g):
    B, S, _ = hx.shape
    u = centred_short_conv(hx, conv_w, conv_b)
    x1, x2, z = jnp.split(u, HYENA_ORDER + 1, axis=-1)
    z = x1 * bidir_long_conv(z, filt[:, 0, 0], filt[:, 0, 1], bias[0])
    z = x2 * bidir_long_conv(z, filt[:, 1, 0], filt[:, 1, 1], bias[1])
    zg = z.reshape(B, S, HYENA_GROUPS, HYENA_GROUP_DIM)
    return rms_norm_2(zg, norm_g.reshape(HYENA_GROUPS, HYENA_GROUP_DIM)).reshape(B, S, HYENA_WIDTH)

def expert_choice_moe(xn, w_router, w_gate, w_up, w_down):
    B, T, D = xn.shape
    cap = EC_CAPACITY_FACTOR * T // N_EXPERTS
    aff = jax.nn.softmax((xn @ w_router).astype(jnp.float32), axis=-1)
    g, idx = lax.top_k(jnp.swapaxes(aff, 1, 2), cap)
    bidx = jnp.arange(B)[:, None, None]
    xs = xn[bidx, idx]
    hid = jax.nn.silu(jnp.einsum('becd,edf->becf', xs, w_gate)) * jnp.einsum('becd,edf->becf', xs, w_up)
    y = jnp.einsum('becf,efd->becd', hid, w_down) * g[..., None].astype(xn.dtype)
    return jnp.zeros_like(xn).at[bidx, idx].add(y)

def second_inputs(seed: int = 0) -> dict:
    key = jax.random.key(seed)
    ks = jax.random.split(key, 32)
    f32 = jnp.float32
    D, L = D_MODEL, DEPTH_2

    def nrm(k, shape, scale):
        return jax.random.normal(k, shape, f32) * scale

    gate_off = 4 * MLSTM_WIDTH
    H = MLSTM_HEADS
    f_bias = jnp.linspace(3.0, 6.0, H, dtype=f32)
    b_in = nrm(ks[5], (L, PROJ_COLS), 0.02)
    b_in = b_in.at[:, gate_off + H:gate_off + 2 * H].add(f_bias)
    b_in = b_in.at[:, gate_off + 3 * H:gate_off + 4 * H].add(f_bias)
    n_filt = HYENA_ORDER * HYENA_DIRS * HYENA_WIDTH
    base_delta = jnp.tile(jnp.linspace(HYENA_SLOW_DECAY, HYENA_FAST_DECAY, HYENA_WIDTH, dtype=f32),
                          HYENA_ORDER * HYENA_DIRS)
    return {
        'x': nrm(ks[0], (BATCH, SEQ, D), 1.0),
        'c': nrm(ks[1], (BATCH, D), 1.0),
        'w_ada': nrm(ks[2], (L, D, 6 * D), 0.5 * D ** -0.5),
        'b_ada': nrm(ks[3], (L, 6 * D), 0.02),
        'g_mix': 1.0 + nrm(ks[4], (L, D), 0.02),
        'w_in': nrm(ks[6], (L, D, PROJ_COLS), D ** -0.5),
        'b_in': b_in,
        'conv_qk_w': nrm(ks[7], (L, SHORT_CONV, 2 * MLSTM_WIDTH), SHORT_CONV ** -0.5),
        'conv_qk_b': nrm(ks[8], (L, 2 * MLSTM_WIDTH), 0.02),
        'mlstm_norm_g': 1.0 + nrm(ks[9], (L, MLSTM_WIDTH), 0.02),
        'conv_hy_w': nrm(ks[10], (L, SHORT_CONV, (HYENA_ORDER + 1) * HYENA_WIDTH), SHORT_CONV ** -0.5),
        'conv_hy_b': nrm(ks[11], (L, (HYENA_ORDER + 1) * HYENA_WIDTH), 0.02),
        'hy_w1': nrm(ks[12], (L, HYENA_EMB_DIM, HYENA_FILTER_HIDDEN), HYENA_EMB_DIM ** -0.5),
        'hy_b1': nrm(ks[13], (L, HYENA_FILTER_HIDDEN), 0.1),
        'hy_w2': nrm(ks[14], (L, HYENA_FILTER_HIDDEN, HYENA_FILTER_HIDDEN), HYENA_FILTER_HIDDEN ** -0.5),
        'hy_b2': nrm(ks[15], (L, HYENA_FILTER_HIDDEN), 0.1),
        'hy_w3': nrm(ks[16], (L, HYENA_FILTER_HIDDEN, n_filt), 0.1 * HYENA_FILTER_HIDDEN ** -0.5),
        'hy_freq': 1.0 + nrm(ks[17], (L, HYENA_FILTER_HIDDEN), 0.02),
        'hy_deltas': base_delta[None] * (1.0 + nrm(ks[18], (L, n_filt), 0.02)),
        'hy_bias': nrm(ks[19], (L, HYENA_ORDER, HYENA_WIDTH), 0.1),
        'hyena_norm_g': 1.0 + nrm(ks[20], (L, HYENA_WIDTH), 0.02),
        'w_out': nrm(ks[21], (L, MIX_WIDTH_2, D), MIX_WIDTH_2 ** -0.5),
        'g_ffn': 1.0 + nrm(ks[22], (L, D), 0.02),
        'w_router': nrm(ks[23], (L, D, N_EXPERTS), D ** -0.5),
        'w_gate': nrm(ks[24], (L, N_EXPERTS, D, EXPERT_FF), D ** -0.5),
        'w_up': nrm(ks[25], (L, N_EXPERTS, D, EXPERT_FF), D ** -0.5),
        'w_down': nrm(ks[26], (L, N_EXPERTS, EXPERT_FF, D), EXPERT_FF ** -0.5),
        'g_final': 1.0 + nrm(ks[27], (D,), 0.02),
    }

def second_block(x, c, w_ada, b_ada, g_mix, w_in, b_in, conv_qk_w, conv_qk_b, mlstm_norm_g,
              conv_hy_w, conv_hy_b, hy_w1, hy_b1, hy_w2, hy_b2, hy_w3, hy_freq, hy_deltas, hy_bias,
              hyena_norm_g, w_out, g_ffn, w_router, w_gate, w_up, w_down, g_final):
    W = MLSTM_WIDTH
    split_pts = [W, 2 * W, 3 * W, 4 * W, 4 * W + N_GATE_COLS]
    seq_len = x.shape[1]
    for l in range(DEPTH_2):
        mod = (c @ w_ada[l] + b_ada[l])[:, None, :]
        sh1, sc1, gt1, sh2, sc2, gt2 = jnp.split(mod, 6, axis=-1)
        h = rms_norm_2(x, g_mix[l]) * (1 + sc1) + sh1
        p = h @ w_in[l] + b_in[l]
        q, k, v, o, gates, hx = jnp.split(p, split_pts, axis=-1)
        y_m = mlstm_mixer(q, k, v, o, gates, conv_qk_w[l], conv_qk_b[l], mlstm_norm_g[l])
        filt = hyena_filters(seq_len, hy_w1[l], hy_b1[l], hy_w2[l], hy_b2[l], hy_w3[l], hy_freq[l], hy_deltas[l])
        y_h = hyena_mixer(hx, conv_hy_w[l], conv_hy_b[l], filt, hy_bias[l], hyena_norm_g[l])
        mixed = jnp.concatenate([y_m, y_h], axis=-1) @ w_out[l]
        x = x + gt1 * mixed
        hf = rms_norm_2(x, g_ffn[l]) * (1 + sc2) + sh2
        x = x + gt2 * expert_choice_moe(hf, w_router[l], w_gate[l], w_up[l], w_down[l])
    return rms_norm_2(x, g_final)


def setup_inputs(seed=0):
    out = dict(first_inputs(seed))
    for name, value in second_inputs(seed + 1).items():
        if name != "x":
            out[name + "_2"] = value
    return out


def reference(
    x, c, ctx, c_ctx, w_mod, b_mod, norm_g, w_in, w_out, w_mlp_in, w_mlp_out, qk_norm_a,
    diff_lambda, diff_subln, sink_c, rpb_d, c_2, w_ada_2, b_ada_2, g_mix_2, w_in_2, b_in_2,
    conv_qk_w_2, conv_qk_b_2, mlstm_norm_g_2, conv_hy_w_2, conv_hy_b_2, hy_w1_2, hy_b1_2,
    hy_w2_2, hy_b2_2, hy_w3_2, hy_freq_2, hy_deltas_2, hy_bias_2, hyena_norm_g_2, w_out_2,
    g_ffn_2, w_router_2, w_gate_2, w_up_2, w_down_2, g_final_2,
):
    x = first_block(
        x, c, ctx, c_ctx, w_mod, b_mod, norm_g, w_in, w_out, w_mlp_in, w_mlp_out, qk_norm_a,
        diff_lambda, diff_subln, sink_c, rpb_d,
    )
    return second_block(
        x, c_2, w_ada_2, b_ada_2, g_mix_2, w_in_2, b_in_2, conv_qk_w_2, conv_qk_b_2,
        mlstm_norm_g_2, conv_hy_w_2, conv_hy_b_2, hy_w1_2, hy_b1_2, hy_w2_2, hy_b2_2, hy_w3_2,
        hy_freq_2, hy_deltas_2, hy_bias_2, hyena_norm_g_2, w_out_2, g_ffn_2, w_router_2,
        w_gate_2, w_up_2, w_down_2, g_final_2,
    )


_drawn_inputs = setup_inputs


def setup_inputs(seed=0):
    import zlib

    import numpy as np

    out = dict(_drawn_inputs(seed))
    spreads = {}
    factors = {'qk_norm_a': 8.0,
     'diff_subln': 4.898,
     'sink_c': 8.0,
     'rpb_d': 8.0,
     'b_ada_2': 3.183,
     'g_mix_2': 6.528,
     'conv_qk_w_2': 3.163,
     'conv_qk_b_2': 200.0,
     'mlstm_norm_g_2': 8.0,
     'conv_hy_b_2': 3.862,
     'hy_freq_2': 6.868,
     'hyena_norm_g_2': 7.152,
     'g_ffn_2': 5.6,
     'g_final_2': 22.6}
    for name, (base, spread) in spreads.items():
        noise = np.random.default_rng([zlib.crc32(name.encode()), seed]).standard_normal(out[name].shape)
        drawn = base * np.exp(spread * noise) if base else spread * noise
        out[name] = jnp.asarray(drawn.astype(out[name].dtype))
    for name, factor in factors.items():
        out[name] = (out[name] * factor).astype(out[name].dtype)
    return out
```

```python
import math
from contextlib import ExitStack

import numpy as np

import concourse.bass as bass
from concourse import mybir

P = 128
F32 = mybir.dt.float32
ALU = mybir.AluOpType
ACT = mybir.ActivationFunctionType
AX = mybir.AxisListType

D = 1024
DC = D // P
T_X, T_C = 512, 256
TT_X, TT_C = T_X // P, T_C // P
S_ALL = T_C + T_X
GRID = 64
HD = 64
FF = 4 * D
FF_E = 2 * D
N_EXP = 16
CAP = 2 * T_X // N_EXP
MH, MD = 4, 128
HYW = 512
EPS = 1e-6
NEG = -1e30
LAM0 = 0.8 - 0.6 * math.exp(0.0)
SLAB_N = 512
N_SLABS = 3
N_BANKS = 8
BANK = 512
RPB_ROWS, RPB_COLS = 15, 31
QK_SCALE = HD ** -0.5
N_STATS = 1600
REGION = 20700


def flat(tokens):
    if not tokens:
        return []
    if isinstance(tokens, tuple):
        return [tokens]
    return [x for t in tokens for x in flat(t)]


class Queue:

    def __init__(self, sem):
        self.sem, self.count, self.items, self.waited = sem, 0, [], {}

    def hold(self, tokens):
        need = {}
        for sem, value in flat(tokens):
            need[sem] = max(need.get(sem, 0), value)
        for sem, value in need.items():
            if self.waited.get(sem, 0) < value:
                self.items.append((None, sem, value))
                self.waited[sem] = value

    def put(self, issue, wait=(), signal=True):
        self.hold(wait)
        self.items.append((issue, self.sem if signal else None, 1))
        if signal:
            self.count += 1
        return (self.sem, self.count) if signal else None

    def put_dma(self, issue, counter, wait=()):
        self.hold(wait)
        counter[1] += 16
        self.items.append((issue, counter[0], 16))
        return (counter[0], counter[1])

    def last(self):
        return (self.sem, self.count) if self.count else None

    def play(self, engine):
        for issue, sem, value in self.items:
            if issue is None:
                engine.wait_ge(sem, value)
            else:
                made = issue(engine)
                if sem is not None:
                    made.then_inc(sem, value)


class Core:

    def __init__(self, nc, ctx):
        self.nc, self.ctx = nc, ctx
        self.pe = Queue(self.semaphore("pe_done"))
        self.act = Queue(self.semaphore("act_done"))
        self.dve = Queue(self.semaphore("dve_done"))
        self.pool = Queue(self.semaphore("pool_done"))
        self.sp = Queue(self.semaphore("sp_done"))
        self.psum = ctx.enter_context(nc.psum_tensor("psum", [P, N_BANKS * BANK], F32))
        self.bank_free = [None] * N_BANKS
        self.next_bank = 0
        self.slab = [self.tile(f"slab{i}", [P, DC, SLAB_N]) for i in range(N_SLABS)]
        self.slab_loaded = [self.counter(f"slab_loaded{i}") for i in range(N_SLABS)]
        self.slab_free = [None] * N_SLABS
        self.next_slab = 0
        self.stats = self.tile("stats", [P, N_STATS])
        self.used_cols = 0
        self.turn = 0
        self.junk_free = None

    def semaphore(self, name):
        return self.ctx.enter_context(self.nc.semaphore(name))

    def counter(self, name):
        return [self.semaphore(name), 0]

    def tile(self, name, shape):
        return self.ctx.enter_context(self.nc.sbuf_tensor(name, shape, F32))

    def cols(self, n):
        at = self.used_cols
        self.used_cols += n
        assert self.used_cols <= N_STATS
        return self.stats[:, at:at + n]

    def take_bank(self):
        i = self.next_bank
        self.next_bank = (i + 1) % N_BANKS
        return i, self.psum[:, i * BANK:(i + 1) * BANK]

    def load_slab(self, src, k0, kc, n0, nw):
        i = self.next_slab
        self.next_slab = (i + 1) % N_SLABS
        view = self.slab[i][:, 0:kc, 0:nw]
        rows = src[k0:k0 + kc * P, n0:n0 + nw].rearrange("(c p) n -> p c n", p=P)
        loaded = self.sp.put_dma(lambda e, v=view, r=rows: e.dma_start(v, r), self.slab_loaded[i],
                                 wait=self.slab_free[i])
        return i, view, loaded

    def barrier(self):
        queues = (self.pe, self.act, self.dve, self.pool)
        ends = [q.last() for q in queues]
        for q in queues:
            q.hold(ends)

    def mm(self, out, lhsT, rhs, start, stop, wait=(), signal=False):
        return self.pe.put(lambda e: e.matmul(out, lhsT, rhs, start=start, stop=stop), wait, signal)

    def tr(self, out, in_, wait=(), signal=False):
        n = in_.shape[0]
        return self.pe.put(lambda e: e.transpose(out, in_, self.ident[0:n, 0:n]), wait, signal)

    def activate(self, out, in_, func, wait=(), **more):
        return self.act.put(lambda e: e.activation(out, in_, func, **more), wait)

    def tt(self, out, a, b, op, wait=(), q=None):
        return (q or self.dve).put(lambda e: e.tensor_tensor(out, a, b, op), wait)

    def ts(self, out, a, s1, s2, op0, op1=None, wait=(), q=None, accum_out=None):
        def issue(e):
            if accum_out is not None:
                return e.tensor_scalar(out, a, s1, s2, op0, op1, accum_out=accum_out)
            if op1 is None:
                return e.tensor_scalar(out, a, s1, None, op0)
            return e.tensor_scalar(out, a, s1, s2, op0, op1)
        return (q or self.dve).put(issue, wait)

    def stt(self, out, a, s, b, op0, op1, wait=(), **more):
        return self.dve.put(lambda e: e.scalar_tensor_tensor(out, a, s, b, op0, op1, **more), wait)

    def copy(self, out, in_, wait=(), q=None):
        q = q or self.dve
        if q is self.act:
            return q.put(lambda e: e.activation(out, in_, ACT.Copy), wait)
        return q.put(lambda e: e.tensor_copy(out, in_), wait)

    def copy_any(self, out, in_, wait=()):
        self.turn += 1
        return self.copy(out, in_, wait, self.act if self.turn % 2 else self.dve)

    def load(self, out, in_, counter, wait=(), q=None):
        return (q or self.sp).put_dma(lambda e: e.dma_start(out, in_), counter, wait)

    def feature_gemm(self, src, n0, n, act_T, T, ready, evacuate):
        done = 0
        while done < n:
            nw = min(SLAB_N, n - done)
            slot, slab, loaded = self.load_slab(src, 0, DC, n0 + done, nw)
            for j in range(-(-nw // P)):
                m = min(P, nw - j * P)
                b, bank = self.take_bank()
                for kc in range(DC):
                    end = self.mm(bank[0:m, 0:T], slab[:, kc, j * P:j * P + m], act_T[:, kc, 0:T],
                                  kc == 0, kc == DC - 1, signal=kc == DC - 1,
                                  wait=[loaded, ready, self.bank_free[b]] if kc == 0 else ())
                self.bank_free[b] = evacuate((done // P) + j, bank[0:m, 0:T], end)
            self.slab_free[slot] = end
            done += nw

    def token_gemm(self, src, K, ranges, act_T, tiles, ready, evacuate):
        kslabs = K // (DC * P)
        for n0, nw in ranges:
            banks = [self.take_bank() for _ in range(tiles)]
            for ks in range(kslabs):
                slot, slab, loaded = self.load_slab(src, ks * DC * P, DC, n0, nw)
                for t in range(tiles):
                    b, bank = banks[t]
                    for kc in range(DC):
                        end = self.mm(bank[:, 0:nw], act_T[:, ks * DC + kc, t * P:(t + 1) * P],
                                      slab[:, kc, :], ks + kc == 0, ks == kslabs - 1 and kc == DC - 1,
                                      signal=kc == DC - 1,
                                      wait=[loaded, ready, self.bank_free[b]] if kc == 0 else ())
                    if ks == kslabs - 1:
                        self.bank_free[b] = evacuate(t, n0, nw, bank[:, 0:nw], end)
                self.slab_free[slot] = end

    def inv_rms(self, sums, n, width, wait):
        mean, out = self.cols(n), self.cols(n)
        a = self.ts(mean, sums, 1.0 / width, EPS, ALU.mult, ALU.add, wait=wait)
        done = self.tt(out, mean, self.minus_half[:, 0:n], ALU.pow, wait=a, q=self.pool)
        return out, done

    def row_inv_rms(self, src, tiles, width, ready):
        sums = self.cols(tiles)
        ends = []
        for t in range(tiles):
            self.junk_free = self.activate(self.junk[:, 0:width], src[:, t, :], ACT.Square,
                                           wait=[ready, self.junk_free], accum_out=sums[:, t:t + 1])
            ends.append(self.junk_free)
        return self.inv_rms(sums, tiles, width, ends)

    def norm_to_features(self, src, tiles, ready, a_col, b_col, col_ready, y, y_free, dst, dst_free):
        rstd, have = self.row_inv_rms(src, tiles, D, ready)
        scaled = []
        for t in range(tiles):
            if t % 2:
                scaled.append(self.activate(y[:, t, :], src[:, t, :], ACT.Copy, scale=rstd[:, t:t + 1],
                                            wait=[have, y_free]))
            else:
                scaled.append(self.ts(y[:, t, :], src[:, t, :], rstd[:, t:t + 1], None, ALU.mult,
                                      wait=[have, y_free]))
        done = []
        for c in range(DC):
            b, bank = self.take_bank()
            for t in range(tiles):
                end = self.tr(bank[:, t * P:(t + 1) * P], y[:, t, c * P:(c + 1) * P], signal=t == tiles - 1,
                              wait=[scaled[t], self.bank_free[b]])
            view = dst[:, c, 0:tiles * P]
            if c % 2:
                e = self.activate(view, bank[:, 0:tiles * P], ACT.Identity, scale=a_col[:, c:c + 1],
                                  bias=b_col[:, c:c + 1], wait=[end, col_ready, dst_free])
            else:
                e = self.ts(view, bank[:, 0:tiles * P], a_col[:, c:c + 1], b_col[:, c:c + 1], ALU.mult,
                            ALU.add, wait=[end, col_ready, dst_free])
            self.bank_free[b] = e
            done.append(e)
        return done

    def to_features(self, src, tiles, ready, dst, dst_free):
        done = []
        for c in range(DC):
            b, bank = self.take_bank()
            for t in range(tiles):
                end = self.tr(bank[:, t * P:(t + 1) * P], src[:, t, c * P:(c + 1) * P], signal=t == tiles - 1,
                              wait=[ready, self.bank_free[b]])
            e = self.copy_any(dst[:, c, 0:tiles * P], bank[:, 0:tiles * P], wait=[end, dst_free])
            self.bank_free[b] = e
            done.append(e)
        return done

    def columns_to_rows(self, col, n, dst, ready, dst_free):
        done = []
        for g in range(0, n, 4):
            m = min(4, n - g)
            b, bank = self.take_bank()
            for c in range(m):
                end = self.tr(bank[:, c * P:(c + 1) * P], col[:, g + c:g + c + 1].to_broadcast([P, P]),
                              signal=c == m - 1, wait=[ready, self.bank_free[b]])
            e = self.copy_any(dst[:, g * P:(g + m) * P], bank[:, 0:m * P], wait=[end, dst_free])
            self.bank_free[b] = e
            done.append(e)
        return done

    def gated_residual(self, x, tiles, m, m_ready, gate_row, gate_ready):
        rstd, have = self.row_inv_rms(m, tiles, D, m_ready)
        done = []
        for t in range(tiles):
            a = self.stt(m[:, t, :], m[:, t, :], rstd[:, t:t + 1], gate_row, ALU.mult, ALU.mult,
                         wait=[have, gate_ready])
            done.append(self.tt(x[:, t, :], x[:, t, :], m[:, t, :], ALU.add, wait=a,
                                q=self.pool if t % 2 else self.dve))
        return done


def attention(k, units, buf):
    ends = [k.bank_free[b] for b in range(N_BANKS)]
    pair_free = [[ends[0], ends[1]], [ends[2], ends[3]]]
    tr_free = [ends[4], ends[5]]
    out_free = [ends[6], ends[7]]
    p_free = [None, None]
    pt_free = [None, None]
    state = {}

    def scores(i):
        u = units[i]
        S = u["S"]
        base = (i % 2) * 2 * BANK
        s = k.psum[:, base:base + S]
        for n, (p0, c0, w) in enumerate(u["segments"]):
            end = k.mm(s[:, p0:p0 + w], u["q"], u["k"][:, c0:c0 + w], True, True,
                       signal=n == len(u["segments"]) - 1,
                       wait=[u["ready"], pair_free[i % 2]] if n == 0 else ())
        for p0, w, add, have in u.get("bias", ()):
            end = k.tt(s[:, p0:p0 + w], s[:, p0:p0 + w], add, ALU.add, wait=[end, have])
        if "bias_free" in u:
            u["bias_free"](end)
        st = k.cols(4)
        mx, nb, rs, es = (st[:, j:j + 1] for j in range(4))
        a = k.dve.put(lambda e: e.reduce_max(mx, s, AX.X), wait=end)
        if u.get("sink") is not None:
            a = k.ts(mx, mx, QK_SCALE, u["sink"], ALU.mult, ALU.max, wait=[a, u["sink_ready"]])
            a = k.ts(nb, mx, -1.0, None, ALU.mult, wait=a)
        else:
            a = k.ts(nb, mx, -QK_SCALE, None, ALU.mult, wait=a)
        pv = buf["p"][:, i % 2, 0:S]
        e1 = k.activate(pv, s, ACT.Exp, scale=QK_SCALE, bias=nb, accum_out=rs, wait=[a, p_free[i % 2]])
        pair_free[i % 2] = [e1]
        if u.get("sink") is not None:
            e2 = k.activate(es, u["sink"], ACT.Exp, bias=nb, wait=a)
            total = k.tt(rs, rs, es, ALU.add, wait=[e1, e2])
        else:
            total = e1
        inv = k.dve.put(lambda e: e.reciprocal(mx, rs), wait=[total, a])
        state[i] = [e1, inv, mx]

    def transposes(i):
        u = units[i]
        n = u["S"] // P
        for c in range(n):
            end = k.tr(k.psum[:, 4 * BANK + c * P:4 * BANK + (c + 1) * P], buf["p"][:, i % 2, c * P:(c + 1) * P],
                       signal=c == min(3, n - 1) or c == n - 1,
                       wait=[state[i][0], tr_free[0]] if c == 0 else ([tr_free[1]] if c == 4 else ()))
            if c == min(3, n - 1):
                first = end
        p_free[i % 2] = end
        w = min(n, 4) * P
        e1 = k.copy(buf["pt"][:, i % 2, 0:w], k.psum[:, 4 * BANK:4 * BANK + w], wait=[first, pt_free[i % 2]])
        tr_free[0] = e1
        e2 = None
        if n > 4:
            e2 = k.copy(buf["pt"][:, i % 2, w:n * P], k.psum[:, 5 * BANK:5 * BANK + (n - 4) * P],
                        wait=[end, pt_free[i % 2]], q=k.act)
            tr_free[1] = e2
        state[i].append([e1, e2])

    def values(i):
        u = units[i]
        n = u["S"] // P
        o = k.psum[:, (6 + i % 2) * BANK:(6 + i % 2) * BANK + u["dv"]]
        for c in range(n):
            end = k.mm(o, buf["pt"][:, i % 2, c * P:(c + 1) * P], u["v"][c], c == 0, c == n - 1,
                       signal=c == n - 1, wait=[state[i][3], out_free[i % 2]] if c == 0 else ())
        pt_free[i % 2] = end
        out_free[i % 2] = u["finish"](o, state[i][2], [end, state[i][1]])

    n = len(units)
    for i in range(n + 2):
        if i < n:
            scores(i)
        if 1 <= i < n + 1:
            transposes(i - 1)
        if i >= 2:
            values(i - 2)
    for b in range(4):
        k.bank_free[b] = pair_free[b // 2]
    k.bank_free[4], k.bank_free[5] = tr_free
    k.bank_free[6], k.bank_free[7] = out_free


def rope(k, out_view, src, cos, sin, heads, tmp, wait, tmp_free):
    w = heads * HD
    s3 = src.rearrange("p (h d) -> p h d", d=HD)
    t3 = tmp[:, 0:w].rearrange("p (h d) -> p h d", d=HD)
    u3 = tmp[:, 512:512 + w].rearrange("p (h d) -> p h d", d=HD)
    a = [k.tt(t3, s3, cos.unsqueeze(1).to_broadcast([P, heads, HD]), ALU.mult, wait=[wait, tmp_free])]
    for half in range(2):
        for axis in range(2):
            o = u3.rearrange("p h (a b f) -> p h a b f", a=2, b=2)[:, :, axis, half, :]
            i = s3.rearrange("p h (a b f) -> p h a b f", a=2, b=2)[:, :, axis, 1 - half, :]
            c = sin.rearrange("p (a b f) -> p a b f", a=2, b=2)[:, axis, half, :]
            a.append(k.tt(o, i, c.unsqueeze(1).to_broadcast([P, heads, 16]), ALU.mult, wait=[wait, tmp_free]))
    return k.tt(out_view, t3, u3, ALU.add, wait=a), a


def project_heads(k, layer, w_in, act_T, tiles, tok0, is_x, ready, V):
    QT, KT, VV = V["QT"], V["KT"], V["VV"]
    done = []
    normed = layer == 0
    stage_free = V["stage_free"]

    def stage():
        i = V["stage_next"] % 3
        V["stage_next"] += 1
        return i, V["stage"][:, i, :]

    def put_transposed(staged, nchunks, dst, chunk0, tok, have, slot):
        b, bank = k.take_bank()
        for c in range(nchunks):
            end = k.tr(bank[:, c * P:(c + 1) * P], staged[:, c * P:(c + 1) * P], signal=c == nchunks - 1,
                       wait=[have, k.bank_free[b]])
        e = k.copy_any(dst[:, chunk0:chunk0 + nchunks, tok:tok + P],
                       bank[:, 0:nchunks * P].rearrange("p (c t) -> p c t", t=P), wait=end)
        k.bank_free[b] = e
        stage_free[slot] = end
        done.append(e)

    def q_view(staged, perm):
        if perm:
            return staged.rearrange("p (j g d) -> p g j d", g=2, d=HD)
        return staged.rearrange("p (h d) -> p h d", d=HD)

    def group(t, bank, w, roped, norm, which, perm, end, nchunks, dst, chunk0):
        heads = w // HD
        slot, staged = stage()
        staged = staged[:, 0:w]
        tmp, tmp_free = V["tmp"], V["tmp_free"]
        tok = tok0 + t * P
        src, src_ready = bank[:, 0:w], end
        rel = None
        if norm:
            raw = V["raw"][:, 0:w]
            c = k.copy(raw, bank[:, 0:w], wait=[end, V["raw_free"]], q=k.act)
            sq = tmp[:, 0:w]
            a = k.tt(sq, raw, raw, ALU.mult, wait=[c, tmp_free])
            sums = k.cols(heads)
            a = k.dve.put(lambda e, o=sums, i=sq: e.tensor_reduce(o, i.rearrange("p (h d) -> p h d", d=HD),
                                                                 AX.X, ALU.add), wait=a)
            rstd, have = k.inv_rms(sums, heads, HD, a)
            rawh = raw.rearrange("p (h d) -> p h d", d=HD)
            src_ready = k.tt(rawh, rawh, rstd.unsqueeze(2).to_broadcast([P, heads, HD]), ALU.mult,
                             wait=have)
            src, rel, tmp_free = raw, c, src_ready
        shape_src = src.rearrange("p (h d) -> p h d", d=HD)
        view = q_view(staged, perm)

        def each(fn):
            if perm:
                return [fn(view[:, g], g * 4, 4) for g in range(2)]
            return [fn(view, 0, heads)]

        if roped:
            cos, sin = V["tables"][which]
            outs = []
            for g in range(2 if perm else 1):
                h0, hn = (g * 4, 4) if perm else (0, heads)
                o, parts = rope(k, view[:, g] if perm else view, src[:, h0 * HD:(h0 + hn) * HD],
                                cos[:, t, :], sin[:, t, :], hn, tmp,
                                [src_ready, V["tables_ready"], stage_free[slot]], tmp_free)
                tmp_free = o
                outs.append(o)
            rel = rel or outs
            V["tmp_free"] = tmp_free
        elif norm:
            g_row = V["qk_gain"][:, which * HD:(which + 1) * HD]
            outs = each(lambda o, h0, hn: k.tt(o, shape_src[:, h0:h0 + hn, :],
                                               g_row.unsqueeze(1).to_broadcast([P, hn, HD]), ALU.mult,
                                               wait=[src_ready, V["gain_ready"], stage_free[slot]]))
        else:
            outs = each(lambda o, h0, hn: k.copy(o, shape_src[:, h0:h0 + hn, :],
                                                 wait=[src_ready, stage_free[slot]], q=k.act))
            rel = outs
        if norm:
            V["raw_free"] = outs
            if not roped:
                V["tmp_free"] = outs
        put_transposed(staged, nchunks, dst, chunk0, tok, outs, slot)
        return rel

    def evacuate(t, n0, nw, bank, end):
        sc = tok0 // P + t
        if n0 == 0:
            if not V["want_q"]:
                return None
            return group(t, bank, 512, is_x, normed, 0, True, end, 4, QT, 0)
        if n0 == 512:
            v = k.copy(VV[:, sc, 0:P], bank[:, P:2 * P], wait=end, q=k.act)
            done.append(v)
            return [group(t, bank, P, is_x, normed, 1, False, [end, v], 1, KT, 0), v]
        plain_rope = is_x and layer == 0
        if n0 == 768:
            return group(t, bank, 512, plain_rope, False, 2, False, end, 4, QT, 4)
        if n0 == 1280:
            return group(t, bank, 512, plain_rope, False, 2, False, end, 4, KT, 1)
        v = k.copy_any(VV[:, sc, P:P + 512], bank, wait=end)
        done.append(v)
        return v

    ranges = [(0, 512), (512, 256), (768, 512), (1280, 512), (1792, 512)]
    if not V["want_q"]:
        ranges = [ranges[1], ranges[3], ranges[4]]
    k.token_gemm(w_in, D, ranges, act_T, tiles, ready, evacuate)
    return done


def mlp(k, w1, w2, act_T, tiles, ready, uT, m, m_free):
    T = tiles * P
    hidden = []

    def up(j, bank, end):
        a = k.activate(uT[:, j, 0:T], bank, ACT.Relu, wait=end)
        hidden.append(k.tt(uT[:, j, 0:T], uT[:, j, 0:T], uT[:, j, 0:T], ALU.mult, wait=a))
        return a

    k.feature_gemm(w1, 0, FF, act_T, T, ready, up)
    done = []

    def down(t, n0, nw, bank, end):
        e = k.copy_any(m[:, t, n0:n0 + nw], bank, wait=[end, m_free])
        done.append(e)
        return e

    k.token_gemm(w2, FF, [(0, 512), (512, 512)], uT, tiles, hidden, down)
    return done


def build(nc, A, C, out):
    with ExitStack() as ctx:
        k = Core(nc, ctx)
        k.junk = k.tile("junk", [P, D])
        k.ident = k.tile("ident", [P, P])
        k.minus_half = k.tile("minus_half", [P, 16])
        x = k.tile("x", [P, TT_X, D])
        cx = k.tile("cx", [P, TT_C, D])
        hT = k.tile("hT", [P, DC, T_X])
        y = k.tile("y", [P, TT_X, D])
        gate_row = k.tile("gate_row", [P, D])
        colv = k.tile("colv", [P, 3 * P])
        region = k.tile("region", [P, REGION])
        s_in = k.counter("inputs_loaded")
        s_p = k.counter("pool_loaded")
        scratch = nc.dram_tensor("bias_tables", [8 * RPB_ROWS, GRID * GRID], F32, kind="Internal").ap()
        s_scr = k.counter("bias_tables_written")

        at = [0]

        def carve(*shape):
            n = int(np.prod(shape))
            v = region[:, at[0]:at[0] + n]
            at[0] += n
            assert at[0] <= REGION, at[0]
            if len(shape) == 2:
                v = v.rearrange("p (a b) -> p a b", b=shape[1])
            elif len(shape) == 3:
                v = v.rearrange("p (a b c) -> p a b c", b=shape[1], c=shape[2])
            return v

        def new_phase():
            k.barrier()
            at[0] = 0

        def rewind(to):
            at[0] = to

        t_ident = k.load(k.ident[:, :], C["ident"], s_in)
        rows = [carve(P) for _ in range(3)]
        row_parts = [
            [(A["b_mod"].rearrange("l (r q) -> (l r) q", q=P), 96), (A["c"].rearrange("b (r q) -> (b r) q", q=P), 8),
             (A["c_ctx"].rearrange("(r q) -> r q", q=P), 8), (A["c_2"].rearrange("b (r q) -> (b r) q", q=P), 8),
             (A["conv_qk_b_2"].rearrange("b (r q) -> (b r) q", q=P), 8)],
            [(A["norm_g"].rearrange("l i (r q) -> (l i r) q", q=P), 64),
             (A["b_ada_2"].rearrange("b (r q) -> (b r) q", q=P), 48),
             (A["g_mix_2"].rearrange("b (r q) -> (b r) q", q=P), 8),
             (A["g_ffn_2"].rearrange("b (r q) -> (b r) q", q=P), 8)],
            [(A["conv_qk_w_2"].rearrange("b j (r q) -> (b j r) q", q=P), 24),
             (A["conv_hy_w_2"].rearrange("b j (r q) -> (b j r) q", q=P), 36),
             (A["conv_hy_b_2"].rearrange("b (r q) -> (b r) q", q=P), 12),
             (A["b_in_2"][0, 0:1024].rearrange("(r q) -> r q", q=P), 8),
             (A["b_in_2"][0, 2064:3600].rearrange("(r q) -> r q", q=P), 12)],
        ]
        row_counts = []
        for v, parts in zip(rows, row_parts):
            r = 0
            for src, n in parts:
                k.load(v[r:r + n, :], src, s_in)
                r += n
            row_counts.append(r)
        t_in = (s_in[0], s_in[1])
        s_x = k.counter("x_loaded")
        k.load(x[:, :, :], A["x"][0].rearrange("(t p) d -> p t d", p=P), s_x)
        t_x = k.load(cx[:, :, :], A["ctx"][0].rearrange("(t p) d -> p t d", p=P), s_x)
        t_half = k.dve.put(lambda e: e.memset(k.minus_half[:, :], -0.5))
        k.pool.hold(t_half)

        cols_ready = []
        for i, (v, n) in enumerate(zip(rows, row_counts)):
            b, bank = k.take_bank()
            end = k.tr(bank[:, 0:n], v[0:n, :], wait=t_in, signal=True)
            e = k.copy(colv[:, i * P:i * P + n], bank[:, 0:n], wait=end)
            k.bank_free[b] = e
            cols_ready.append(e)
        b_modT = colv[:, 0:96]
        cT = colv[:, 96:120]
        conv_qk_bT = colv[:, 120:128]
        norm_gT = colv[:, 128:192]
        b_adaT = colv[:, 192:240]
        g_mixT, g_ffnT = colv[:, 240:248], colv[:, 248:256]
        conv_qk_wT, conv_hy_wT = colv[:, 256:280], colv[:, 280:316]
        conv_hy_bT, b_qkT, b_hxT = colv[:, 316:328], colv[:, 328:336], colv[:, 336:348]

        sT = k.tile("sT", [P, DC, 2])
        a = [k.activate(sT[:, :, i], cT[:, i * 8:(i + 1) * 8], ACT.Silu, wait=cols_ready) for i in range(2)]
        mods = k.tile("mods", [P, 2, 48, 2])
        mod2 = k.tile("mod2", [P, 48, 1])

        def modulation(w, vec, n, dst, bias, ready):
            b, bank = k.take_bank()
            pv = bank[:, 0:48 * n].rearrange("p (c s) -> p c s", s=n)
            for s in range(12):
                slot, slab, loaded = k.load_slab(w, 0, DC, s * 512, 512)
                for j in range(4):
                    for kc in range(DC):
                        end = k.mm(pv[:, s * 4 + j, :], slab[:, kc, j * P:(j + 1) * P], vec[:, kc, :],
                                   kc == 0, kc == DC - 1, signal=kc == DC - 1,
                                   wait=[loaded, ready, k.bank_free[b]] if kc == 0 else ())
                k.slab_free[slot] = end
            e = k.tt(dst, pv, bias.unsqueeze(2).to_broadcast([P, 48, n]), ALU.add, wait=end)
            k.bank_free[b] = e
            return e

        mod_ready = [None, None]

        def scale_cols(mod, stream, chunk, gain, ready):
            dst = k.cols(8)
            e = k.stt(dst, mod[:, chunk:chunk + 8, stream], 1.0, gain, ALU.add, ALU.mult, wait=ready)
            return dst, e

        def gate_cols(mod, stream, chunk, gain, ready):
            dst = k.cols(8)
            return dst, k.tt(dst, mod[:, chunk:chunk + 8, stream], gain, ALU.mult, wait=ready)

        mod_ready[0] = modulation(A["w_mod"][0], sT, 2, mods[:, 0], b_modT[:, 0:48], [a, cols_ready])

        new_phase()
        rpb_rows, rpb_T = carve(32), carve(120)
        onehot = carve(GRID * GRID)
        stage_b = carve(8, 512)
        s_rpb = k.counter("rpb_loaded")
        k.load(onehot[0:32, :], C["neighbour_onehot"], s_rpb, q=k.pool)
        k.load(rpb_rows[0:120, 0:RPB_COLS], A["rpb_d"][0].rearrange("h r c -> (h r) c"), s_rpb, q=k.pool)
        ones_col = k.dve.put(lambda e: e.memset(rpb_rows[0:120, 31:32], 1.0))
        t_rpb = (s_rpb[0], s_rpb[1])
        b, bank = k.take_bank()
        end = k.tr(bank[0:32, 0:120], rpb_rows[0:120, 0:32], wait=[t_rpb, ones_col, k.bank_free[b]], signal=True)
        have = k.copy(rpb_T[0:32, :], bank[0:32, 0:120], wait=end)
        k.bank_free[b] = have
        for j in range(8):
            b, bank = k.take_bank()
            end = k.mm(bank[0:120, :], rpb_T[0:32, :], onehot[0:32, j * 512:(j + 1) * 512], True, True,
                       wait=[have, k.bank_free[b]], signal=True)
            e = k.ts(stage_b[0:120, j, :], bank[0:120, :], 1.0 / QK_SCALE, None, ALU.mult, wait=end)
            k.bank_free[b] = e
            k.load(scratch[:, j * 512:(j + 1) * 512], stage_b[0:120, j, :], s_scr, wait=e, q=k.pool)
        t_scr = (s_scr[0], s_scr[1])
        k.pool.hold(t_scr)

        s_tab = k.counter("rope_loaded")
        x_ready, c_ready = t_x, t_x
        for layer in range(2):
            mod = mods[:, layer]
            if layer == 1:
                mod_ready[1] = modulation(A["w_mod"][1], sT, 2, mods[:, 1], b_modT[:, 48:96], cols_ready)
            ready = [mod_ready[layer], cols_ready]
            gains = [norm_gT[:, layer * 32 + i * 8:layer * 32 + i * 8 + 8] for i in range(4)]
            new_phase()
            V = {"QT": carve(8, S_ALL), "KT": carve(5, S_ALL), "VV": carve(6, 640), "stage": carve(3, 512),
                 "tmp": carve(1024), "raw": carve(512), "stage_free": [None] * 3, "stage_next": 0,
                 "tmp_free": None, "raw_free": None, "want_q": True}
            p_buf = V["stage"].rearrange("p a b -> p (a b)").rearrange("p (a b) -> p a b", b=S_ALL)
            pt_buf = carve(2, S_ALL)
            cos, sin = carve(TT_X, HD), carve(TT_X, HD)
            small = carve(640)
            k.load(cos, C["rope_cos"].rearrange("(t p) d -> p t d", p=P), s_tab, q=k.pool)
            k.load(sin, C["rope_sin"].rearrange("(t p) d -> p t d", p=P), s_tab, q=k.pool)
            if layer == 0:
                qk_gain, lam_rows, subln = small[:, 0:128], small[:, 128:384], small[:, 384:512]
                cg, sg = carve(2 * TT_X, HD), carve(2 * TT_X, HD)
                k.load(qk_gain, A["qk_norm_a"][0].rearrange("i d -> (i d)").partition_broadcast(P), s_tab, q=k.pool)
                k.load(lam_rows, A["diff_lambda"][0].rearrange("i d -> (i d)").partition_broadcast(P), s_tab,
                       q=k.pool)
                t_tab = k.load(subln, A["diff_subln"][0].partition_broadcast(P), s_tab, q=k.pool)
                V["qk_gain"], V["gain_ready"] = qk_gain, t_tab
                made = []
                for w in range(2):
                    g = qk_gain[:, w * HD:(w + 1) * HD]
                    made.append(k.tt(cg[:, w * 4:w * 4 + 4, :], cos, g.unsqueeze(1).to_broadcast([P, 4, HD]),
                                     ALU.mult, wait=t_tab))
                    for h in range(2):
                        for ax in range(2):
                            o, i = ax * 32 + h * 16, ax * 32 + (1 - h) * 16
                            made.append(k.tt(sg[:, w * 4:w * 4 + 4, o:o + 16], sin[:, :, o:o + 16],
                                             g[:, i:i + 16].unsqueeze(1).to_broadcast([P, 4, 16]), ALU.mult,
                                             wait=t_tab))
                V["tables"] = [(cg[:, 0:4, :], sg[:, 0:4, :]), (cg[:, 4:8, :], sg[:, 4:8, :]), (cos, sin)]
                V["tables_ready"] = [made, t_tab]
                prod = small[:, 512:640]
                lr = lam_rows.rearrange("p (a b d) -> p a b d", a=2, b=2)
                e = k.tt(prod.rearrange("p (a d) -> p a d", d=HD), lr[:, :, 0, :], lr[:, :, 1, :], ALU.mult,
                         wait=t_tab)
                dots, neg_lam = k.cols(2), k.cols(1)
                e = k.dve.put(lambda en, o=dots, i=prod: en.tensor_reduce(
                    o, i.rearrange("p (a d) -> p a d", d=HD), AX.X, ALU.add), wait=e)
                e = k.activate(dots, dots, ACT.Exp, wait=e)
                e = k.tt(neg_lam, dots[:, 1:2], dots[:, 0:1], ALU.subtract, wait=e)
                lam_ready = k.ts(neg_lam, neg_lam, LAM0, None, ALU.subtract, wait=e)
                e = k.ts(subln, subln, 1.0 - LAM0, None, ALU.mult, wait=t_tab)
                subln_ready = e
            else:
                sink = small[:, 0:8]
                masks = small[:, 8:264]
                more = carve(2, 512)
                bias_ring = [V["tmp"][:, 0:512], V["tmp"][:, 512:1024], V["raw"], more[:, 0, :], more[:, 1, :]]
                k.load(masks, C["window_masks"], s_tab, q=k.pool)
                t_tab = k.load(sink, A["sink_c"][0].partition_broadcast(P), s_tab, q=k.pool)
                V["tables"] = [(cos, sin)] * 3
                V["tables_ready"] = t_tab
            stash = []
            for stream in (1, 0):
                src, tiles, src_ready = ((x, TT_X, x_ready), (cx, TT_C, c_ready))[stream]
                A1, e1 = scale_cols(mod, stream, 8, gains[0], ready)
                normed = k.norm_to_features(src, tiles, src_ready, A1, mod[:, 0:8, stream], [e1, ready], y,
                                            k.pe.last(), hT, k.pe.last())
                V["want_q"] = layer == 0 or stream == 0
                stash.append(project_heads(k, layer, A["w_in"][layer], hT, tiles, 0 if stream else T_C,
                                           stream == 0, normed, V))
            QT, KT, VV = V["QT"], V["KT"], V["VV"]
            k.barrier()
            mixed = {}
            for stream in ((1, 0) if layer == 0 else (0,)):
                tiles = TT_C if stream else TT_X
                mix_done = []
                units = []
                full = [(0, 0, 256)] if stream else [(0, 0, 512), (512, 512, 256)]
                S = T_C if stream else S_ALL
                qtok = 0 if stream else T_C
                half_o = V["raw"].rearrange("p (a b) -> p a b", b=P)
                half_token = {}
                free_y = k.pe.last()

                def finish_plain(t, col, inv_only=None):
                    def f(o, inv, end):
                        e = k.ts(y[:, t, col:col + HD], o, inv, None, ALU.mult, wait=end)
                        mix_done.append(e)
                        return e
                    return f

                def finish_diff(t, h, j):
                    def f(o, inv, end):
                        if j == 0:
                            e = k.ts(half_o[:, t, :], o, inv, None, ALU.mult, wait=[end, half_token.get(t)])
                            half_token[t] = e
                            return e
                        c = k.cols(1)
                        a = k.tt(c, inv, neg_lam, ALU.mult, wait=[end, lam_ready])
                        e = k.stt(y[:, t, 512 + h * P:512 + (h + 1) * P], o, c, half_o[:, t, :], ALU.mult, ALU.add,
                                  wait=[a, half_token[t]])
                        half_token[t] = e
                        mix_done.append(e)
                        return e
                    return f

                bias_state = {"n": 0}
                s_bias = [k.counter(f"bias_loaded{layer}{stream}{i}") for i in range(5)] if layer == 1 else None
                for h in range(8):
                    j, kv = h % 4, h // 4
                    pb = 64 * kv
                    for t in range(tiles):
                        q = QT[pb:pb + 64, j, qtok + t * P:qtok + (t + 1) * P]
                        u = {"q": q, "dv": HD, "ready": None, "finish": finish_plain(t, h * HD)}
                        if layer == 0:
                            u.update(S=S, segments=full, k=KT[pb:pb + 64, 0, :],
                                     v=[VV[:, c, kv * HD:(kv + 1) * HD] for c in range(S // P)])
                        else:
                            lo, hi = max(0, t - 1), min(TT_X - 1, t + 1)
                            n = hi - lo + 1
                            segs = [(0, 0, 256), (256, T_C + lo * P, min(n, 2) * P)]
                            if n == 3:
                                segs.append((512, T_C + (lo + 2) * P, P))
                            bias = []
                            if t > 0:
                                bias.append((256, P, masks[:, 0:P], t_tab))
                            if t < TT_X - 1:
                                bias.append((256 + (n - 1) * P, P, masks[:, P:2 * P], t_tab))
                            u.update(S=T_C + n * P, segments=segs, k=KT[pb:pb + 64, 0, :], bias=bias,
                                     sink=sink[:, h:h + 1], sink_ready=t_tab,
                                     v=[VV[:, c, kv * HD:(kv + 1) * HD] for c in [0, 1] + [2 + lo + i for i in range(n)]])
                        units.append(u)
                heads = [(h, t) for h in range(8) for t in range(tiles)] if layer == 1 else \
                        [(2 * hh + jj, t) for hh in range(4) for t in range(tiles) for jj in range(2)]
                for h, t in heads:
                    c, pb = h // 2, 64 * (h % 2)
                    u = {"q": QT[pb:pb + 64, 4 + c, qtok + t * P:qtok + (t + 1) * P], "S": S, "segments": full,
                         "k": KT[pb:pb + 64, 1 + c, :], "ready": None}
                    if layer == 0:
                        u.update(dv=P, finish=finish_diff(t, c, h % 2),
                                 v=[VV[:, s, P + c * P:P + (c + 1) * P] for s in range(S // P)])
                    else:
                        i = bias_state["n"] % 5
                        bias_state["n"] += 1
                        u.update(dv=HD, finish=finish_plain(t, 512 + h * HD),
                                 v=[VV[:, s, P + h * HD:P + (h + 1) * HD] for s in range(S // P)])
                        u["load_bias"] = (i, h, t)
                    units.append(u)
                if layer == 1:
                    free = [None] * 5

                    def with_bias(u):
                        i, h, t = u["load_bias"]

                        def start():
                            for rs in range(2):
                                r = 2 * t + rs
                                src = scratch[h * RPB_ROWS + 7 - r:h * RPB_ROWS + 15 - r, :].rearrange(
                                    "r (q c) -> q r c", c=GRID)
                                dst = bias_ring[i][64 * rs:64 * rs + 64, :].rearrange("p (r c) -> p r c", c=GRID)
                                tok = k.load(dst, src, s_bias[i], wait=[free[i], t_scr], q=k.pool)
                            return tok
                        have = start()
                        u["bias"] = [(256, 256, bias_ring[i][:, 0:256], have),
                                     (512, 256, bias_ring[i][:, 256:512], have)]

                        def release(tok):
                            free[i] = tok
                        u["bias_free"] = release
                    u_list = UnitStream(units, with_bias)
                else:
                    u_list = units
                attention(k, u_list, {"p": p_buf, "pt": pt_buf})
                if layer == 0:
                    sq = k.junk[:, 0:512]
                    for t in range(tiles):
                        o = y[:, t, 512:1024]
                        e = k.tt(V["tmp"][:, 0:512], o, o, ALU.mult, wait=[mix_done, k.dve.last()])
                        sums = k.cols(4)
                        e = k.dve.put(lambda en, s=sums: en.tensor_reduce(
                            s, V["tmp"][:, 0:512].rearrange("p (h d) -> p h d", d=P), AX.X, ALU.add), wait=e)
                        rstd, have = k.inv_rms(sums, 4, P, e)
                        o3 = o.rearrange("p (h d) -> p h d", d=P)
                        e = k.tt(o3, o3, rstd.unsqueeze(2).to_broadcast([P, 4, P]), ALU.mult, wait=have)
                        e = k.tt(o3, o3, subln.unsqueeze(1).to_broadcast([P, 4, P]), ALU.mult,
                                 wait=[e, subln_ready])
                        mix_done.append(e)
                tr_done = k.to_features(y, tiles, mix_done, hT, k.pe.last())
                g1, e = gate_cols(mod, stream, 16, gains[1], ready)
                g_ready = k.columns_to_rows(g1, 8, gate_row, e, [k.dve.last(), k.pool.last()])
                tr_end = k.pe.last()
                m_done = []

                def out_evac(t, n0, nw, bank, end):
                    e = k.copy_any(y[:, t, n0:n0 + nw], bank, wait=[end, tr_end])
                    m_done.append(e)
                    return e

                k.token_gemm(A["w_out"][layer], D, [(0, 512), (512, 512)], hT, tiles, tr_done, out_evac)
                r = k.gated_residual(cx if stream else x, tiles, y, m_done, gate_row[:, :], g_ready)
                mixed[stream] = r
                k.barrier()
            new_phase()
            uT = carve(FF // P, T_X)
            for stream in ((1, 0) if layer == 0 else (0,)):
                src, tiles = ((x, TT_X), (cx, TT_C))[stream]
                A2, e1 = scale_cols(mod, stream, 32, gains[2], ready)
                normed = k.norm_to_features(src, tiles, mixed[stream], A2, mod[:, 24:32, stream], [e1, ready], y,
                                            [k.pe.last(), k.dve.last(), k.pool.last()], hT, k.pe.last())
                g2, e = gate_cols(mod, stream, 40, gains[3], ready)
                g_ready = k.columns_to_rows(g2, 8, gate_row, e, [k.dve.last(), k.pool.last()])
                m_done = mlp(k, A["w_mlp_in"][layer], A["w_mlp_out"][layer], hT, tiles, normed, uT, y,
                             k.pe.last())
                r = k.gated_residual(src, tiles, y, m_done, gate_row[:, :], g_ready)
                if stream:
                    c_ready = r
                else:
                    x_ready = r
                k.barrier()

        second_block(k, nc, A, C, out, x, x_ready, hT, y, gate_row, carve, new_phase,
                     dict(cT=cT, cols_ready=cols_ready, b_adaT=b_adaT, g_mixT=g_mixT, g_ffnT=g_ffnT,
                          conv_qk_wT=conv_qk_wT, conv_qk_bT=conv_qk_bT, conv_hy_wT=conv_hy_wT,
                          conv_hy_bT=conv_hy_bT, b_qkT=b_qkT, b_hxT=b_hxT, mod2=mod2, modulation=modulation,
                          scale_cols=scale_cols, rewind=rewind, cx=cx, scratch_done=t_scr))

        with nc.Block() as block:
            @block.sync
            def _(e):
                k.sp.play(e)

            @block.tensor
            def _(e):
                k.pe.play(e)

            @block.scalar
            def _(e):
                k.act.play(e)

            @block.vector
            def _(e):
                k.dve.play(e)

            @block.gpsimd
            def _(e):
                k.pool.play(e)


class UnitStream:

    def __init__(self, units, prepare):
        self.units, self.prepare, self.made = units, prepare, set()

    def __len__(self):
        return len(self.units)

    def __getitem__(self, i):
        if i not in self.made:
            self.made.add(i)
            if "load_bias" in self.units[i]:
                self.prepare(self.units[i])
        return self.units[i]


def short_conv(k, out, raw, w, b, T, wait):
    e = k.ts(out, raw, w[1], b, ALU.mult, ALU.add, wait=wait)
    e = k.stt(out[:, 1:T], raw[:, 0:T - 1], w[0], out[:, 1:T], ALU.mult, ALU.add, wait=e)
    return k.stt(out[:, 0:T - 1], raw[:, 1:T], w[2], out[:, 0:T - 1], ALU.mult, ALU.add, wait=e)


def group_rms(k, view, groups, width, gain, gain_ready, tmp, ready):
    n = groups * width
    e = k.tt(tmp[:, 0:n], view, view, ALU.mult, wait=[ready, k.dve.last()])
    sums = k.cols(groups)
    e = k.dve.put(lambda en: en.tensor_reduce(sums, tmp[:, 0:n].rearrange("p (h d) -> p h d", d=width),
                                              AX.X, ALU.add), wait=e)
    rstd, have = k.inv_rms(sums, groups, width, e)
    v3 = view.rearrange("p (h d) -> p h d", d=width)
    e = k.tt(v3, v3, rstd.unsqueeze(2).to_broadcast([P, groups, width]), ALU.mult, wait=have)
    return k.tt(view, view, gain, ALU.mult, wait=[e, gain_ready])


def mlstm(k, qkT, vpad, gates, rows, w, hT, y, consts, ready, carve):
    J, ones, masks = consts["J"], consts["ones"], consts["tri"]
    c_ready = consts["ready"]
    NC_ = T_X // P
    R = 2 * MH
    k_tok = y[:, :, MH * MD:2 * MH * MD]
    kt_done = []
    for c in range(NC_):
        b, bank = k.take_bank()
        for h in range(MH):
            end = k.tr(bank[:, h * P:(h + 1) * P], qkT[:, MH + h, c * P:(c + 1) * P], signal=h == MH - 1,
                       wait=[ready, k.bank_free[b]])
        e = k.copy_any(k_tok[:, c, :], bank, wait=end)
        k.bank_free[b] = e
        kt_done.append(e)
    gsel = carve(NC_ * 4, 8)
    g4 = gsel.rearrange("p (c n d) r -> p c n d r", n=2, d=2)
    e = k.dve.put(lambda en: en.memset(gsel, 0.0))
    sel = []
    for kind in range(2):
        for d in range(2):
            src = gates[:, :, (2 * d + kind) * 4:(2 * d + kind) * 4 + 4]
            sel.append(k.copy(g4[:, :, kind, d, d * 4:d * 4 + 4], src, wait=[e, ready]))
    row = [hT[0:R, i, :] for i in range(8)]
    W, LF, B, CM, M, E_END, E_INT, E_NM = row
    raw_rows = []
    for kind in range(2):
        b, bank = k.take_bank()
        for c in range(NC_):
            k.mm(bank[0:R, c * P:(c + 1) * P], g4[:, c, kind, 0, :], k.ident[:, :], True, False,
                 wait=[sel, k.bank_free[b], c_ready])
            end = k.mm(bank[0:R, c * P:(c + 1) * P], g4[:, NC_ - 1 - c, kind, 1, :], J, False, True,
                       signal=c == NC_ - 1)
        e = k.copy(row[kind], bank[0:R, :], wait=end)
        k.bank_free[b] = e
        raw_rows.append(e)
    e = k.stt(B, LF, -1.0, LF, ALU.mult, ALU.max, wait=raw_rows[1])
    e = k.activate(B, B, ACT.Exp, scale=-1.0, wait=e)
    e = k.activate(B, B, ACT.Ln, bias=1.0, wait=e)
    lf = k.stt(LF, LF, 0.0, B, ALU.min, ALU.subtract, wait=e)
    one = k.dve.put(lambda en: en.memset(E_END, 1.0))
    sc = []
    for c in range(NC_):
        s = slice(c * P, (c + 1) * P)
        sc.append(k.dve.put(lambda en, s=s: en.tensor_tensor_scan(B[:, s], E_END[:, s], LF[:, s], 0.0, ALU.mult,
                                                                  ALU.add), wait=[lf, one]))
    e = k.tt(W, W, B, ALU.subtract, wait=[sc, raw_rows[0]])
    cm = []
    for c in range(NC_):
        s = slice(c * P, (c + 1) * P)
        cm.append(k.dve.put(lambda en, s=s: en.tensor_tensor_scan(CM[:, s], W[:, s], W[:, s], -3.0e38, ALU.max,
                                                                  ALU.max), wait=e))
    sm = carve(64)[0:R, :]
    m_in, g_m, a_c, spl, ncml = sm[:, 0:5], sm[:, 8:12], sm[:, 12:16], sm[:, 16:24], sm[:, 24:28]
    last = slice(P - 1, T_X, P)
    e0 = k.dve.put(lambda en: en.memset(m_in[:, 0:1], NEG))
    e1 = k.tt(a_c, B[:, last], CM[:, last], ALU.add, wait=cm)
    ncml_ready = k.ts(ncml, CM[:, last], -1.0, None, ALU.mult, wait=cm)
    e = [e0, e1]
    for c in range(NC_):
        e = k.tt(g_m[:, c:c + 1], B[:, c * P + P - 1:c * P + P], m_in[:, c:c + 1], ALU.add, wait=e)
        e = k.tt(m_in[:, c + 1:c + 2], g_m[:, c:c + 1], a_c[:, c:c + 1], ALU.max, wait=e)
    e1 = k.tt(spl[:, 0:4], g_m, m_in[:, 1:5], ALU.subtract, wait=e)
    e2 = k.tt(spl[:, 4:8], a_c, m_in[:, 1:5], ALU.subtract, wait=e)
    spl_ready = k.activate(spl, spl, ACT.Exp, wait=[e1, e2])
    m_done, q_done = [], []
    for c in range(NC_):
        s = slice(c * P, (c + 1) * P)
        m_done.append(k.ts(M[:, s], CM[:, s], m_in[:, c:c + 1], None, ALU.max, wait=e))
        q_done.append(k.activate(E_END[:, s], W[:, s], ACT.Exp, bias=ncml[:, c:c + 1], wait=[ncml_ready, sc]))
        q_done.append(k.activate(E_INT[:, s], M[:, s], ACT.Exp, scale=-1.0, bias=m_in[:, c:c + 1],
                                 wait=m_done[-1]))
    e = k.tt(E_NM, B, M, ALU.add, wait=m_done)
    q_done.append(k.activate(E_NM, E_NM, ACT.Exp, scale=-1.0, wait=e))
    Q = [W, M, E_END, E_INT, E_NM]
    nq = len(Q)
    craw, colsq = carve(NC_ * nq, R), carve(NC_ * nq, R)
    b, bank = k.take_bank()
    for c in range(NC_):
        for i, q in enumerate(Q):
            end = k.tr(bank[:, (c * nq + i) * R:(c * nq + i + 1) * R], q[:, c * P:(c + 1) * P],
                       wait=[q_done, m_done, k.bank_free[b]], signal=True)
    n = NC_ * nq * R
    e1 = k.copy(craw, bank[:, 0:n].rearrange("p (n r) -> p n r", r=R), wait=end)
    k.bank_free[b] = e1
    e2 = k.copy(colsq[:, :, 0:4], craw[:, :, 0:4], wait=e1)
    b, bank = k.take_bank()
    end = k.mm(bank[:, 0:n // 2].rearrange("p (n r) -> p n r", r=4), J, craw[:, :, 4:8], True, True,
               wait=[e1, k.bank_free[b], c_ready], signal=True)
    cols_done = [e2]
    for c in range(NC_):
        o = (NC_ - 1 - c) * nq
        cols_done.append(k.copy(colsq[:, o:o + nq, 4:8],
                                bank[:, c * nq * 4:(c + 1) * nq * 4].rearrange("p (n r) -> p n r", r=4), wait=end))
    k.bank_free[b] = cols_done[-1]

    def col(c, q, r):
        return colsq[:, c * nq + q, r:r + 1]

    diag = carve(8, 8)[0:R, :, :]
    e = k.tt(diag, spl.unsqueeze(2).to_broadcast([R, 8, 8]),
             k.ident[0:R, 0:R].unsqueeze(1).to_broadcast([R, 8, 8]), ALU.mult, wait=spl_ready)
    sB = carve(8, 8)
    b, bank = k.take_bank()
    end = k.mm(bank[:, 0:64].rearrange("p (n r) -> p n r", r=8), ones[0:R, :], diag, True, True,
               wait=[e, k.bank_free[b], c_ready], signal=True)
    sB_ready = k.copy(sB, bank[:, 0:64].rearrange("p (n r) -> p n r", r=8), wait=end)
    k.bank_free[b] = sB_ready
    DT = carve(2, T_X)
    PT = carve(2, T_X)
    ve = carve(2, NC_ * 129)
    st = carve(2, 3 * 129)
    num = carve(2, 129)
    tmp = carve(2, 129)
    free = [None, None]
    num_free = [None, None]
    y_tok = {}
    step = 0
    for r in range(R):
        d, h, i = r // MH, r % MH, r % 2
        b, bank = k.take_bank()
        for c in range(NC_):
            end = k.tr(bank[:, c * P:(c + 1) * P], col(c, 1, r).to_broadcast([P, P]), signal=c == NC_ - 1,
                       wait=[cols_done, k.bank_free[b]])
        e = []
        for c in range(NC_):
            e.append(k.ts(DT[:, i, c * P:(c + 1) * P], bank[:, c * P:(c + 1) * P], col(c, 0, r), 0.0,
                          ALU.subtract, ALU.max, wait=[end, free[i]]))
        k.bank_free[b] = e[-1]
        e = k.activate(DT[:, i, :], DT[:, i, :], ACT.Exp, scale=-1.0, wait=e)
        d3 = DT[:, i, :].rearrange("p (c t) -> p c t", t=P)
        dm = k.tt(d3, d3, masks[:, d, :].unsqueeze(1).to_broadcast([P, NC_, P]), ALU.mult, wait=[e, c_ready],
                  q=k.pool)
        b, bank = k.take_bank()
        for c in range(NC_):
            s = slice(c * P, (c + 1) * P)
            end = k.mm(bank[:, s], qkT[:, MH + h, s], qkT[:, h, s], True, True, signal=c == NC_ - 1,
                       wait=[ready, k.bank_free[b]])
        pt_ready = k.tt(PT[:, i, :], bank, DT[:, i, :], ALU.mult, wait=[end, dm, free[i]])
        k.bank_free[b] = pt_ready
        order = list(range(NC_)) if d == 0 else list(range(NC_ - 1, -1, -1))
        v3 = ve[:, i, :].rearrange("p (c n) -> p c n", n=129)
        s3 = st[:, i, :].rearrange("p (c n) -> p c n", n=129)
        state_ready = None
        ends = []
        for n_, c in enumerate(order):
            if n_ < NC_ - 1:
                a = k.activate(v3[:, c, :], vpad[:, c * MH + h, :], ACT.Copy, scale=col(c, 2, r),
                               wait=[cols_done, ready, free[i]])
                b, bank = k.take_bank()
                end = k.mm(bank[:, 0:129], k_tok[:, c, h * P:(h + 1) * P], v3[:, c, :], True, True,
                           wait=[a, kt_done, k.bank_free[b]], signal=True)
                loc = k.activate(s3[:, n_, :], bank[:, 0:129], ACT.Copy, scale=sB[:, 4 + n_, r:r + 1],
                                 wait=[end, sB_ready, free[i]])
                k.bank_free[b] = loc
                if n_ == 0:
                    nxt = loc
                else:
                    nxt = k.stt(s3[:, n_, :], s3[:, n_ - 1, :], sB[:, n_, r:r + 1], s3[:, n_, :], ALU.mult,
                                ALU.add, wait=[loc, state_ready])
            b, bank = k.take_bank()
            end = k.mm(bank[:, 0:129], PT[:, i, c * P:(c + 1) * P], vpad[:, c * MH + h, :], True, True,
                       wait=[pt_ready, k.bank_free[b]], signal=True)
            j = step % 2
            step += 1
            if n_ > 0:
                end2 = k.mm(bank[:, 256:385], qkT[:, h, c * P:(c + 1) * P], s3[:, n_ - 1, :], True, True,
                            wait=state_ready, signal=True)
                e = k.activate(tmp[:, j, :], bank[:, 256:385], ACT.Copy, scale=col(c, 3, r),
                               wait=[end2, num_free[j]])
                e = k.tt(num[:, j, :], bank[:, 0:129], tmp[:, j, :], ALU.add, wait=[e, num_free[j]])
                end = end2
            else:
                e = k.copy(num[:, j, :], bank[:, 0:129], wait=[end, num_free[j]])
            k.bank_free[b] = e
            den = k.cols(2)
            e = k.ts(den[:, 0:1], num[:, j, 128:129], col(c, 4, r), None, ALU.max, wait=e)
            e = k.stt(den[:, 0:1], num[:, j, 128:129], -1.0, den[:, 0:1], ALU.mult, ALU.max, wait=e)
            e = k.dve.put(lambda en, den=den: en.reciprocal(den[:, 1:2], den[:, 0:1]), wait=e)
            o = y[:, c, h * P:(h + 1) * P]
            if d == 0:
                e = k.ts(o, num[:, j, 0:128], den[:, 1:2], None, ALU.mult, wait=e)
            else:
                e = k.stt(o, num[:, j, 0:128], den[:, 1:2], o, ALU.mult, ALU.add, wait=[e, y_tok[(c, h)]])
            y_tok[(c, h)] = e
            num_free[j] = e
            ends += [e, end]
            if n_ < NC_ - 1:
                state_ready = nxt
        free[i] = ends
    return list(y_tok.values())


def hyena(k, u_tok, A, C, cx, hT, y, gate_row, carve, consts, ready):
    N_F = 2 * T_X
    TC = T_X // P
    dft, alt_re, alt_im, alt_g = carve(TC, N_F), carve(TC, P), carve(TC, P), carve(T_X)
    U = carve(2 * TC, HYW)
    Kr, Ki, KrB, hid2_all, bias_row = carve(TC, HYW), y[:, :, HYW:2 * HYW], carve(HYW), carve(HYW), carve(HYW)
    s_bias = k.counter("hyena_bias_loaded")
    s_dft = k.counter("dft_loaded")
    tp = "(t p) f -> p t f"
    k.load(dft, C["dft"].rearrange(tp, p=P), s_dft, q=k.pool)
    k.load(alt_re, C["dft_alt_re"].rearrange(tp, p=P), s_dft, q=k.pool)
    k.load(alt_im, C["dft_alt_im"].rearrange(tp, p=P), s_dft, q=k.pool)
    t_dft = k.load(alt_g, C["dft_alt_back"], s_dft, q=k.pool)
    s_f = k.counter("filter_loaded")
    z0, w1, w2, fcol, tcol = U[0:33, 0, :], U[0:33, 1, 0:64], U[0:64, 1, 64:128], U[0:64, 1, 128:136], k.cols(8)
    deltas = cx[:, :, :].rearrange("p t d -> p (t d)")
    hid2 = hid2_all[0:64, :]
    k.load(z0, C["hyena_z"], s_f, q=k.pool)
    k.load(w1, A["hy_w1_2"][0], s_f, q=k.pool)
    k.load(w2, A["hy_w2_2"][0], s_f, q=k.pool)
    for i, n in enumerate(("hy_b1_2", "hy_b2_2", "hy_freq_2")):
        k.load(fcol[:, i:i + 1], A[n][0].rearrange("(p a) -> p a", a=1), s_f, q=k.pool)
    k.load(tcol[:, 0:6], C["hyena_cols"], s_f, q=k.pool)
    t_f = k.load(deltas, A["hy_deltas_2"][0].partition_broadcast(P), s_f, q=k.pool)
    d_ready = k.stt(deltas, deltas, -1.0, deltas, ALU.mult, ALU.max, wait=t_f)
    arg, turns = U[0:64, 2, :], U[0:64, 3, :]

    def sine_layer(w, z, n, bias, out, wait):
        b, bank = k.take_bank()
        end = k.mm(bank[0:64, :], w, z, True, True, wait=[wait, t_f, k.bank_free[b]], signal=True)
        e = k.ts(arg, bank[0:64, :], bias, fcol[:, 2:3], ALU.add, ALU.mult, wait=end)
        k.bank_free[b] = e
        e = k.ts(turns, arg, 1.0 / (2.0 * math.pi), ROUND, ALU.mult, ALU.add, wait=e)
        e = k.ts(turns, turns, ROUND, None, ALU.subtract, wait=e)
        for part in TWO_PI:
            e = k.stt(arg, turns, -part, arg, ALU.mult, ALU.add, wait=e)
        e = k.ts(arg, arg, 3.1415925, -3.1415925, ALU.min, ALU.max, wait=e)
        return k.activate(out, arg, ACT.Sin, wait=e)

    hid1 = U[0:64, 4, :]
    e = sine_layer(w1, z0, 33, fcol[:, 0:1], hid1, None)
    hid_ready = sine_layer(w2, hid1, 64, fcol[:, 1:2], hid2, e)
    s_w3 = k.counter("filter_w3_loaded")
    conv_done = ready
    win, hbuf = k.junk[:, 0:512], k.junk[:, 512:1024]
    w3_free = [None]
    back_end = None
    for order in range(2):
        w3 = gate_row[0:64, 0:1024]
        t_w3 = k.load(w3, A["hy_w3_2"][0, :, order * 1024:(order + 1) * 1024], s_w3,
                      wait=[w3_free, hid_ready], q=k.pool)
        t_bias = k.load(bias_row, A["hy_bias_2"][0, order].partition_broadcast(P), s_bias,
                        wait=conv_done, q=k.pool)
        HS, HDIF = U[:, 0:TC, :], U[:, TC:2 * TC, :]
        sum_done = []
        prev = back_end and last
        for c in range(TC):
            parts = []
            for dr in range(2):
                b, bank = k.take_bank()
                end = k.mm(bank, hid2[:, c * P:(c + 1) * P], w3[:, dr * 512:(dr + 1) * 512], True, True,
                           wait=[t_w3, hid_ready, k.bank_free[b]], signal=True)
                dst = (HS, HDIF)[dr][:, c, :]
                n0 = order * 1024 + dr * 512
                e = k.activate(win, deltas[:, n0:n0 + 512], ACT.Exp, scale=tcol[:, c:c + 1],
                               wait=[d_ready, prev, t_f])
                prev = k.stt(dst, win, 0.05, bank, ALU.add, ALU.mult, wait=[e, end, back_end])
                k.bank_free[b] = prev
                parts.append(prev)
            w3_free[0] = end
            e = k.tt(hbuf, HS[:, c, :], HDIF[:, c, :], ALU.add, wait=[parts, sum_done])
            e2 = k.tt(HDIF[:, c, :], HS[:, c, :], HDIF[:, c, :], ALU.subtract, wait=e)
            sum_done = [k.copy(HS[:, c, :], hbuf, wait=[e, e2]), e2]
        k_ready = []
        for j in range(2 * TC + 1):
            b, bank = k.take_bank()
            for t in range(TC):
                if j < TC:
                    lhs, rhs = dft[:, t, j * P:(j + 1) * P], HS[:, t, :]
                elif j < 2 * TC:
                    lhs, rhs = dft[:, t, j * P:(j + 1) * P], HDIF[:, t, :]
                else:
                    lhs, rhs = alt_re[:, t, :], HS[:, t, :]
                end = k.mm(bank, lhs, rhs, t == 0, t == TC - 1, signal=t == TC - 1,
                           wait=[sum_done, t_dft, k.bank_free[b]] if t == 0 else ())
            dst = Kr[:, j, :] if j < TC else Ki[:, j - TC, :] if j < 2 * TC else KrB
            scale = tcol[:, 4:5] if j in (0, 2 * TC) else 2.0 / N_F
            e = k.ts(dst, bank, scale, None, ALU.mult, wait=[end, conv_done])
            k.bank_free[b] = e
            k_ready.append(e)
        filters_read = end
        z = [u_tok[:, t, 2 * HYW:3 * HYW] for t in range(TC)]
        u_ready = []
        for j in range(2 * TC):
            b, bank = k.take_bank()
            for t in range(TC):
                lhs = alt_im[:, t, :] if j == TC else dft[:, t, j * P:(j + 1) * P]
                end = k.mm(bank, lhs, z[t], t == 0, t == TC - 1, signal=t == TC - 1,
                           wait=[conv_done, k.bank_free[b], t_dft] if t == 0 else ())
            e = k.copy(U[:, j, :], bank, wait=[end, filters_read], q=k.act)
            k.bank_free[b] = e
            u_ready.append(e)
        Y = hT
        prod = []
        t2 = hbuf
        last = k.dve.last()
        for j in range(TC):
            r, i = U[:, j, :], U[:, TC + j, :]
            krb = KrB if j == 0 else Kr[:, j, :]
            w = [u_ready, k_ready, last]
            a = k.tt(Y[:, j, :], r, Kr[:, j, :], ALU.mult, wait=w + [back_end])
            b_ = k.tt(t2, i, Ki[:, j, :], ALU.mult, wait=w)
            c_ = k.tt(Y[:, j, :], Y[:, j, :], t2, ALU.subtract, wait=[a, b_])
            d_ = k.tt(Y[:, TC + j, :], r, Ki[:, j, :], ALU.mult, wait=w + [back_end])
            e_ = k.tt(win, i, krb, ALU.mult, wait=w)
            f_ = k.tt(Y[:, TC + j, :], Y[:, TC + j, :], win, ALU.add, wait=[d_, e_])
            last = [c_, f_]
            prod += [c_, f_]
        new = []
        for t in range(TC):
            b, bank = k.take_bank()
            for j in range(2 * TC):
                lhs = alt_g[:, t * P:(t + 1) * P] if j == TC else dft[:, j % TC, (j // TC) * T_X + t * P:(j // TC) * T_X + (t + 1) * P]
                end = k.mm(bank, lhs, Y[:, j, :], j == 0, j == 2 * TC - 1, signal=j == 2 * TC - 1,
                           wait=[prod, k.bank_free[b]] if j == 0 else ())
            e = k.tt(z[t], z[t], bias_row, ALU.mult, wait=[end, u_ready, t_bias])
            e = k.tt(z[t], z[t], bank, ALU.add, wait=e)
            k.bank_free[b] = e
            dst = z[t] if order == 0 else y[:, t, HYW:2 * HYW]
            new.append(k.tt(dst, z[t], u_tok[:, t, order * HYW:(order + 1) * HYW], ALU.mult,
                            wait=[e, hid_ready, w3_free[0]]))
        back_end = end
        conv_done = new
    return new


def experts(k, A, x, y, y_ready, hT, h_ready, A2, B2, B2_ready, consts, carve):
    TC = T_X // P
    aff, ex = carve(TC, N_EXP), carve(TC, N_EXP)
    c_ready = consts["ready"]
    logit_done = []

    def logits(t, n0, nw, bank, end):
        e = k.copy(ex[:, t, :], bank, wait=end)
        logit_done.append(e)
        return e

    k.token_gemm(A["w_router_2"][0], D, [(0, N_EXP)], hT, TC, h_ready, logits)
    mx = k.cols(8)
    e = k.dve.put(lambda en: en.tensor_reduce(mx[:, 0:4], ex, AX.X, ALU.max), wait=logit_done)
    e = k.tt(ex, ex, mx[:, 0:4].unsqueeze(2).to_broadcast([P, TC, N_EXP]), ALU.subtract, wait=e)
    e = k.activate(ex, ex, ACT.Exp, wait=e)
    e = k.dve.put(lambda en: en.tensor_reduce(mx[:, 4:8], ex, AX.X, ALU.add), wait=e)
    e = k.dve.put(lambda en: en.reciprocal(mx[:, 0:4], mx[:, 4:8]), wait=e)
    aff_ready = k.tt(aff, ex, mx[:, 0:4].unsqueeze(2).to_broadcast([P, TC, N_EXP]), ALU.mult, wait=e)
    moe = carve(TC, D)
    counts = carve(2, TC * 3)
    scrap = carve(T_X)
    hot = carve(2, TC * CAP)
    wgt = carve(2, TC * 2 * CAP)
    wT = carve(2, T_X)
    xs = carve(2, DC * CAP)
    hid = carve(2, (FF_E // P) * CAP)
    act_g = carve(2, 4 * CAP)
    ye = carve(2, D)
    zero = k.dve.put(lambda en: en.memset(counts, 0.0))
    hot_free, wgt_free, wT_free, xs_free, hid_free, ye_free = ([None, None] for _ in range(6))
    g_free = [None, None]
    prepared = {}
    wT_ready = {}
    moe_done = {}

    def prepare(e_):
        i = e_ % 2
        b, bank = k.take_bank()
        for c in range(TC):
            end = k.tr(bank[:, c * P:(c + 1) * P], aff[:, c, e_:e_ + 1].to_broadcast([P, P]), signal=c == TC - 1,
                       wait=[aff_ready, k.bank_free[b]])
        cnt = counts[:, i, :].rearrange("p (t n) -> p t n", n=3)
        got = []
        for t in range(TC):
            a = aff[:, t, e_:e_ + 1]
            w = [end, zero, k.dve.last()]
            if t:
                e = k.ts(scrap[:, 0:t * P], bank[:, 0:t * P], a, None, ALU.is_ge, ALU.add, wait=w,
                         accum_out=cnt[:, t, 0:1])
                got.append(e)
                w = e
            e = k.ts(scrap[:, t * P:T_X], bank[:, t * P:T_X], a, None, ALU.is_gt, ALU.add, wait=w,
                     accum_out=cnt[:, t, 1:2])
            e2 = k.stt(scrap[:, 0:P], bank[:, t * P:(t + 1) * P], a, consts["before"], ALU.is_equal, ALU.mult,
                       accum_out=cnt[:, t, 2:3], wait=[e, c_ready])
            got += [e, e2]
        k.bank_free[b] = got[-1]
        rank = k.cols(4)
        e = k.dve.put(lambda en: en.tensor_reduce(rank, cnt, AX.X, ALU.add), wait=got)
        pair, j = e_ // 2, e_ % 2
        hots, wgts = [], []
        for t in range(TC):
            hots.append(k.ts(hot[:, i, t * CAP:(t + 1) * CAP], consts["iota"], rank[:, t:t + 1], None,
                             ALU.is_equal, wait=[e, c_ready, hot_free[i]]))
            o = (t * 2 + j) * CAP
            wgts.append(k.ts(wgt[:, pair % 2, o:o + CAP], consts["iota"], rank[:, t:t + 1],
                             aff[:, t, e_:e_ + 1], ALU.is_equal, ALU.mult,
                             wait=[e, c_ready, wgt_free[pair % 2]]))
        b, bank = k.take_bank()
        for dc in range(DC):
            for t in range(TC):
                end = k.mm(bank[:, dc * CAP:(dc + 1) * CAP], y[:, t, dc * P:(dc + 1) * P],
                           hot[:, i, t * CAP:(t + 1) * CAP], t == 0, t == TC - 1,
                           signal=t == TC - 1 and dc == DC - 1,
                           wait=[hots, y_ready, k.bank_free[b]] if t + dc == 0 else ())
        hot_free[i] = end
        x3 = xs[:, i, :].rearrange("p (d r) -> p d r", r=CAP)
        e = k.tt(x3, bank.rearrange("p (d r) -> p d r", r=CAP), A2.unsqueeze(2).to_broadcast([P, DC, CAP]),
                 ALU.mult, wait=[end, xs_free[i], B2_ready])
        k.bank_free[b] = e
        e = k.tt(x3, x3, B2.unsqueeze(2).to_broadcast([P, DC, CAP]), ALU.add, wait=e)
        prepared[e_] = e
        if j == 1:
            b, bank = k.take_bank()
            for t in range(TC):
                end = k.tr(bank[:, t * P:(t + 1) * P], wgt[:, pair % 2, t * 2 * CAP:(t + 1) * 2 * CAP],
                           signal=t == TC - 1, wait=[prepared_w[pair], wgts, k.bank_free[b]])
            wgt_free[pair % 2] = end
            e = k.copy(wT[:, pair % 2, :], bank, wait=[end, wT_free[pair % 2]], q=k.act)
            k.bank_free[b] = e
            wT_ready[pair] = e
        else:
            prepared_w[pair] = wgts

    prepared_w = {}

    def scatter(pair, ye_ready):
        i = pair % 2
        for t in range(TC):
            for n in range(2):
                b, bank = k.take_bank()
                end = k.mm(bank, wT[:, i, t * P:(t + 1) * P], ye[:, i, n * 512:(n + 1) * 512], True, True,
                           wait=[wT_ready[pair], ye_ready, k.bank_free[b]], signal=True)
                o = moe[:, t, n * 512:(n + 1) * 512]
                if pair == 0:
                    e = k.copy(o, bank, wait=end)
                else:
                    e = k.tt(o, o, bank, ALU.add, wait=[end, moe_done[(t, n)]])
                k.bank_free[b] = e
                moe_done[(t, n)] = e
        wT_free[i] = ye_free[i] = end

    prepare(0)
    pending = None
    for e_ in range(N_EXP):
        i, pair = e_ % 2, e_ // 2
        hid_ready = []
        for s in range(FF_E // SLAB_N):
            halves = []
            for w in (A["w_gate_2"], A["w_up_2"]):
                slot, slab, loaded = k.load_slab(w[0, e_], 0, DC, s * SLAB_N, SLAB_N)
                b, bank = k.take_bank()
                for j in range(4):
                    for kc in range(DC):
                        end = k.mm(bank[:, j * CAP:(j + 1) * CAP], slab[:, kc, j * P:(j + 1) * P],
                                   xs[:, i, kc * CAP:(kc + 1) * CAP], kc == 0, kc == DC - 1,
                                   signal=j == 3 and kc == DC - 1,
                                   wait=[loaded, prepared[e_], k.bank_free[b]] if j + kc == 0 else ())
                k.slab_free[slot] = end
                halves.append((b, bank, end))
            (bg, gate, end_g), (bu, up, end_u) = halves
            g = act_g[:, s % 2, :]
            e = k.activate(g, gate[:, 0:4 * CAP], ACT.Silu, wait=[end_g, g_free[s % 2]])
            k.bank_free[bg] = e
            e = k.tt(hid[:, i, s * 4 * CAP:(s + 1) * 4 * CAP], g, up[:, 0:4 * CAP], ALU.mult,
                     wait=[e, end_u, hid_free[i]])
            k.bank_free[bu] = g_free[s % 2] = e
            hid_ready.append(e)
        xs_free[i] = end
        if pending is not None:
            scatter(*pending)
            pending = None
        if e_ + 1 < N_EXP:
            prepare(e_ + 1)
        p0 = CAP * (e_ % 2)
        outs = []
        for n in range(2):
            b, bank = k.take_bank()
            for ks in range(2):
                slot, slab, loaded = k.load_slab(A["w_down_2"][0, e_], ks * DC * P, DC, n * 512, 512)
                for kc in range(DC):
                    f = ks * DC + kc
                    end = k.mm(bank[p0:p0 + CAP, :], hid[:, i, f * CAP:(f + 1) * CAP], slab[:, kc, :], f == 0,
                               f == 2 * DC - 1, signal=kc == DC - 1,
                               wait=[loaded, hid_ready, k.bank_free[b]] if kc == 0 else ())
                k.slab_free[slot] = end
            e = k.copy(ye[p0:p0 + CAP, pair % 2, n * 512:(n + 1) * 512], bank[p0:p0 + CAP, :],
                       wait=[end, ye_free[pair % 2]], q=k.act)
            k.bank_free[b] = e
            outs.append(e)
        hid_free[i] = end
        if e_ % 2 == 0:
            first_half = outs
        else:
            pending = (pair, [first_half, outs])
    scatter(*pending)
    return moe, moe_done


def second_block(k, nc, A, C, out, x, x_ready, hT, y, gate_row, carve, new_phase, S):
    ready = S["cols_ready"]
    mod2 = S["mod2"]
    mod_ready = S["modulation"](A["w_ada_2"][0], S["cT"][:, 16:24].unsqueeze(2), 1, mod2[:, :, :], S["b_adaT"], ready)
    new_phase()
    TC = T_X // P
    u_tok = carve(TC, 3 * HYW)
    consts_t = carve(6, P)
    J, ones, tri, before = consts_t[:, 0, :], consts_t[:, 1, :], consts_t[:, 2:4, :], consts_t[:, 4, :]
    iota = consts_t[:, 5, 0:CAP]
    s_c = k.counter("mixer_consts_loaded")
    k.load(J, C["flip"], s_c, q=k.pool)
    k.load(tri, C["tri"].rearrange("a p b -> p a b"), s_c, q=k.pool)
    k.load(before, C["before"], s_c, q=k.pool)
    k.load(iota, C["iota"].partition_broadcast(P), s_c, q=k.pool)
    after_u = 6144 + 768
    qkT = carve(2 * MH, T_X)
    vpad = carve(TC * MH, 129)
    o_sig = carve(TC, 512)
    gates = carve(TC, 16)
    after_gates = after_u + sum(int(np.prod(v.shape[1:])) for v in (qkT, vpad, o_sig, gates))
    b_row = carve(1040)
    raw = carve(2, T_X)
    conv = carve(2, T_X)
    t_c = k.load(b_row, A["b_in_2"][0, 1024:2064].partition_broadcast(P), s_c, q=k.pool)
    e1 = k.dve.put(lambda e: e.memset(ones, 1.0))
    e2 = k.dve.put(lambda e: e.memset(vpad[:, :, 128:129], 1.0))
    consts = {"J": J, "ones": ones, "tri": tri, "before": before, "iota": iota, "ready": [t_c, e1]}
    gmix, e = S["scale_cols"](mod2, 0, 8, S["g_mixT"], [mod_ready, ready])
    normed = k.norm_to_features(x, TC, x_ready, gmix, mod2[:, 0:8, 0], [e, mod_ready], y, None, hT, None)
    state = {"raw_free": [None, None], "conv_free": [None, None], "n": 0}
    W_in = A["w_in_2"][0]

    qk_done = []

    def qk_evac(j, bank, end):
        i = state["n"] % 2
        state["n"] += 1
        r = raw[:, i, :]
        e0 = k.activate(r, bank, ACT.Identity, bias=S["b_qkT"][:, j:j + 1], wait=[end, state["raw_free"][i]])
        w = [S["conv_qk_wT"][:, 8 * n + j:8 * n + j + 1] for n in range(3)]
        e = short_conv(k, conv[:, i, :], r, w, S["conv_qk_bT"][:, j:j + 1], T_X, [e0, state["conv_free"][i]])
        state["raw_free"][i] = e
        e = k.activate(qkT[:, j, :], conv[:, i, :], ACT.Silu, wait=e)
        state["conv_free"][i] = e
        if j >= MH:
            e = k.ts(qkT[:, j, :], qkT[:, j, :], MD ** -0.5, None, ALU.mult, wait=e)
        qk_done.append(e)
        return e0

    k.feature_gemm(W_in, 0, 1024, hT, T_X, normed, qk_evac)
    vo_done = []

    def vo_evac(t, n0, nw, bank, end):
        row = b_row[:, n0 - 1024:n0 - 1024 + nw]
        if n0 == 1024:
            o = vpad[:, t * MH:(t + 1) * MH, 0:128]
            e = k.tt(o, bank.rearrange("p (h d) -> p h d", d=128), row.rearrange("p (h d) -> p h d", d=128),
                     ALU.add, wait=[end, t_c])
        else:
            e = k.tt(o_sig[:, t, :] if n0 == 1536 else gates[:, t, :], bank, row, ALU.add, wait=[end, t_c])
        vo_done.append(e)
        return e

    k.token_gemm(W_in, D, [(1024, 512), (1536, 512), (2048, 16)], hT, TC, normed, vo_evac)
    u_done = []

    def hx_evac(j, bank, end):
        i = state["n"] % 2
        state["n"] += 1
        r = raw[:, i, :]
        e0 = k.activate(r, bank, ACT.Identity, bias=S["b_hxT"][:, j:j + 1], wait=[end, state["raw_free"][i]])
        w = [S["conv_hy_wT"][:, 12 * n + j:12 * n + j + 1] for n in range(3)]
        e = short_conv(k, conv[:, i, :], r, w, S["conv_hy_bT"][:, j:j + 1], T_X, [e0, state["conv_free"][i]])
        state["raw_free"][i] = e
        hx_pending.append((j, i, e))
        if len(hx_pending) > 1:
            hx_transpose(*hx_pending.pop(0))
        return e0

    hx_pending = []

    def hx_transpose(j, i, have):
        b, bank = k.take_bank()
        for t in range(TC):
            end = k.tr(bank[:, t * P:(t + 1) * P], conv[:, i, t * P:(t + 1) * P], signal=t == TC - 1,
                       wait=[have, k.bank_free[b]])
        state["conv_free"][i] = end
        e = k.copy(u_tok[:, :, j * P:(j + 1) * P], bank.rearrange("p (t c) -> p t c", c=P), wait=end, q=k.act)
        k.bank_free[b] = e
        u_done.append(e)

    k.feature_gemm(W_in, 2064, 1536, hT, T_X, normed, hx_evac)
    while hx_pending:
        hx_transpose(*hx_pending.pop(0))
    k.barrier()
    S["rewind"](after_gates)
    h_done = mlstm(k, qkT, vpad, gates, None, None, hT, y, consts, [qk_done, vo_done, e2], carve)
    s_g = k.counter("mixer_gains_loaded")
    t_g = k.load(k.junk[:, 0:512], A["mlstm_norm_g_2"][0].partition_broadcast(P), s_g, q=k.pool)
    sg = [k.activate(o_sig[:, t, :], o_sig[:, t, :], ACT.Sigmoid, wait=vo_done) for t in range(TC)]
    m_done = []
    for t in range(TC):
        v = y[:, t, 0:512]
        e = group_rms(k, v, MH, MD, k.junk[:, 0:512], t_g, k.junk[:, 512:1024], h_done)
        m_done.append(k.tt(v, v, o_sig[:, t, :], ALU.mult, wait=[e, sg]))
    k.barrier()
    S["rewind"](after_u)
    hy_done = hyena(k, u_tok, A, C, S["cx"], hT, y, gate_row, carve, consts, u_done)
    k.barrier()
    s_g2 = k.counter("hyena_gain_loaded")
    t_g = k.load(k.junk[:, 0:512], A["hyena_norm_g_2"][0].partition_broadcast(P), s_g2, q=k.pool)
    for t in range(TC):
        m_done.append(group_rms(k, y[:, t, 512:1024], 4, P, k.junk[:, 0:512], t_g, k.junk[:, 512:1024], hy_done))
    tr_done = k.to_features(y, TC, m_done, hT, None)
    g_ready = k.columns_to_rows(mod2[:, 16:24, 0], 8, gate_row, mod_ready, None)
    tr_end = k.pe.last()
    res = []

    def out_evac(t, n0, nw, bank, end):
        e = k.tt(y[:, t, n0:n0 + nw], bank, gate_row[:, n0:n0 + nw], ALU.mult, wait=[end, tr_end, g_ready])
        res.append(k.tt(x[:, t, n0:n0 + nw], x[:, t, n0:n0 + nw], y[:, t, n0:n0 + nw], ALU.add, wait=e))
        return e

    k.token_gemm(A["w_out_2"][0], D, [(0, 512), (512, 512)], hT, TC, tr_done, out_evac)
    k.barrier()
    S["rewind"](after_u)
    gffn, e = S["scale_cols"](mod2, 0, 32, S["g_ffnT"], [mod_ready, ready])
    normed = k.norm_to_features(x, TC, res, gffn, mod2[:, 24:32, 0], [e, mod_ready], y, k.pe.last(), hT,
                                k.pe.last())
    y_ready = [k.act.last(), k.dve.last()]
    moe, moe_done = experts(k, A, x, y, y_ready, hT, normed, gffn, mod2[:, 24:32, 0], [e, mod_ready], consts,
                            carve)
    g_ready = k.columns_to_rows(mod2[:, 40:48, 0], 8, gate_row, mod_ready, None)
    fin_row = y[:, 0, :]
    s_fin = k.counter("final_gain_loaded")
    t_fin = k.load(fin_row, A["g_final_2"].partition_broadcast(P), s_fin, wait=k.pe.last(), q=k.pool)
    s_out = k.counter("output_written")
    for t in range(TC):
        m = moe[:, t, :]
        e = k.tt(m, m, gate_row[:, :], ALU.mult, wait=[moe_done[(t, 0)], moe_done[(t, 1)], g_ready])
        e = k.tt(m, m, x[:, t, :], ALU.add, wait=e)
        sums = k.cols(1)
        e = k.activate(k.junk[:, :], m, ACT.Square, accum_out=sums, wait=e)
        rstd, have = k.inv_rms(sums, 1, D, e)
        e = k.stt(m, m, rstd, fin_row, ALU.mult, ALU.mult, wait=[have, t_fin])
        done = k.load(out[t * P:(t + 1) * P, :], m, s_out, wait=e)
    k.sp.hold(done)
    k.sp.hold(S["scratch_done"])


ROUND = 1.5 * 2.0 ** 23
TWO_PI = (6.28125, 0.0019350051879882812, 3.0199159819567e-07)


def tables():
    f = np.float32
    C = {"ident": np.eye(P, dtype=f), "flip": np.eye(P, dtype=f)[::-1].copy()}
    t = np.arange(T_X)
    pos = np.stack([t // GRID, t % GRID], -1).astype(f)
    inv = (f(10000.0) ** (-np.arange(16, dtype=f) / f(16))).astype(f)
    ang = (pos[:, :, None] * inv).astype(f)
    cos, sin = np.cos(ang).astype(f), np.sin(ang).astype(f)
    C["rope_cos"] = np.stack([cos, cos], 2).reshape(T_X, HD)
    C["rope_sin"] = np.stack([-sin, sin], 2).reshape(T_X, HD)
    q, c = np.arange(GRID)[:, None], np.arange(GRID)[None, :]
    start = np.clip(q - 8, 0, GRID - 16)
    valid = (c >= start) & (c < start + 16)
    off = np.clip(c - q, -15, 15) + 15
    hot = np.zeros((32, GRID, GRID), f)
    for d in range(RPB_COLS):
        hot[d] = (off == d) & valid
    hot[31] = np.where(valid, 0.0, NEG)
    C["neighbour_onehot"] = hot.reshape(32, GRID * GRID)
    i, j = np.arange(P)[:, None], np.arange(P)[None, :]
    C["window_masks"] = np.concatenate([np.where(j >= i, 0.0, NEG), np.where(j <= i, 0.0, NEG)], 1).astype(f)
    C["tri"] = np.stack([i <= j, i >= j]).astype(f)
    C["before"] = (j < i).astype(f)
    C["iota"] = np.arange(CAP, dtype=f)
    L = T_X
    tl = np.linspace(0.0, 1.0, L, dtype=f)[:, None]
    w = (f(2.0 * math.pi) * np.arange(L, dtype=f)[:, None] / f(L)).astype(f)
    bands = np.linspace(1e-4, 15, 16, dtype=f)[None, :]
    C["hyena_z"] = np.concatenate([tl, np.cos(bands * w), -np.sin(bands * w)], -1).astype(f).T.copy()
    cols = np.zeros((P, 6), f)
    cols[:, 0:4] = -tl.reshape(4, P).T
    cols[:, 4] = 2.0 / (2 * L)
    cols[0, 4] = 1.0 / (2 * L)
    C["hyena_cols"] = cols
    n = np.arange(L)
    ph = 2.0 * np.pi * ((n[:, None] * n[None, :]) % (2 * L)) / (2 * L)
    re, im = np.cos(ph), -np.sin(ph)
    alt = np.where(n % 2 == 0, 1.0, -1.0)
    C["dft"] = np.concatenate([re, im], 1).astype(f)
    are, aim = re[:, 0:P].copy(), im[:, 0:P].copy()
    are[:, 0] = alt
    aim[:, 0] = alt
    C["dft_alt_re"], C["dft_alt_im"] = are.astype(f), aim.astype(f)
    C["dft_alt_back"] = aim.T.astype(f).copy()
    return C


_INS = ["x", "c", "ctx", "c_ctx", "w_mod", "b_mod", "norm_g", "w_in", "w_out", "w_mlp_in", "w_mlp_out",
        "qk_norm_a", "diff_lambda", "diff_subln", "sink_c", "rpb_d", "c_2", "w_ada_2", "b_ada_2", "g_mix_2",
        "w_in_2", "b_in_2", "conv_qk_w_2", "conv_qk_b_2", "mlstm_norm_g_2", "conv_hy_w_2", "conv_hy_b_2",
        "hy_w1_2", "hy_b1_2", "hy_w2_2", "hy_b2_2", "hy_w3_2", "hy_freq_2", "hy_deltas_2", "hy_bias_2",
        "hyena_norm_g_2", "w_out_2", "g_ffn_2", "w_router_2", "w_gate_2", "w_up_2", "w_down_2", "g_final_2"]


def kernel(**inputs):
    import numpy as _np
    import concourse.bacc as _bacc
    from concourse import mybir as _mybir
    from concourse.bass_utils import run_bass_kernel_spmd as _run

    nc = _bacc.Bacc("TRN2", target_bir_lowering=False, num_devices=1)
    arrays, A, C = {}, {}, {}
    for group, named in ((A, {n: inputs[n] for n in _INS}), (C, tables())):
        for name, value in named.items():
            a = _np.ascontiguousarray(value)
            full = f"in_{name}" if group is A else f"table_{name}"
            arrays[full] = a
            group[name] = nc.dram_tensor(full, a.shape, _mybir.dt.from_np(a.dtype), kind="ExternalInput").ap()
    out = nc.dram_tensor("out", (T_X, D), F32, kind="ExternalOutput").ap()
    build(nc, A, C, out)
    r = _run(nc, [arrays], core_ids=[0])
    return r.results[0]["out"].reshape(1, T_X, D)
```

```python
import math
from contextlib import ExitStack

import numpy as np

import concourse.bass as bass
from concourse import mybir

P = 128
F32 = mybir.dt.float32
ALU = mybir.AluOpType
ACT = mybir.ActivationFunctionType
AX = mybir.AxisListType

D = 1024
DC = D // P
T_X, T_C = 512, 256
TT_X, TT_C = T_X // P, T_C // P
S_ALL = T_C + T_X
GRID = 64
HD = 64
FF = 4 * D
FF_E = 2 * D
N_EXP = 16
CAP = 2 * T_X // N_EXP
MH, MD = 4, 128
HYW = 512
EPS = 1e-6
NEG = -1e30
LAM0 = 0.8 - 0.6 * math.exp(0.0)
SLAB_N = 512
N_SLABS = 3
N_BANKS = 8
BANK = 512
RPB_ROWS, RPB_COLS = 15, 31
QK_SCALE = HD ** -0.5
N_STATS = 1600
REGION = 20480


def flat(tokens):
    if not tokens:
        return []
    if isinstance(tokens, tuple):
        return [tokens]
    return [x for t in tokens for x in flat(t)]


class Queue:

    def __init__(self, sem):
        self.sem, self.count, self.items, self.waited = sem, 0, [], {}

    def hold(self, tokens):
        need = {}
        for sem, value in flat(tokens):
            need[sem] = max(need.get(sem, 0), value)
        for sem, value in need.items():
            if self.waited.get(sem, 0) < value:
                self.items.append((None, sem, value))
                self.waited[sem] = value

    def put(self, issue, wait=(), signal=True):
        self.hold(wait)
        self.items.append((issue, self.sem if signal else None, 1))
        if signal:
            self.count += 1
        return (self.sem, self.count) if signal else None

    def put_dma(self, issue, counter, wait=()):
        self.hold(wait)
        counter[1] += 16
        self.items.append((issue, counter[0], 16))
        return (counter[0], counter[1])

    def last(self):
        return (self.sem, self.count) if self.count else None

    def play(self, engine):
        for issue, sem, value in self.items:
            if issue is None:
                engine.wait_ge(sem, value)
            else:
                made = issue(engine)
                if sem is not None:
                    made.then_inc(sem, value)


class Core:

    def __init__(self, nc, ctx):
        self.nc, self.ctx = nc, ctx
        self.pe = Queue(self.semaphore("pe_done"))
        self.act = Queue(self.semaphore("act_done"))
        self.dve = Queue(self.semaphore("dve_done"))
        self.pool = Queue(self.semaphore("pool_done"))
        self.sp = Queue(self.semaphore("sp_done"))
        self.psum = ctx.enter_context(nc.psum_tensor("psum", [P, N_BANKS * BANK], F32))
        self.bank_free = [None] * N_BANKS
        self.next_bank = 0
        self.held_banks = set()
        self.background = None
        self.slab = [self.tile(f"slab{i}", [P, DC, SLAB_N]) for i in range(N_SLABS)]
        self.slab_loaded = [self.counter(f"slab_loaded{i}") for i in range(N_SLABS)]
        self.slab_free = [None] * N_SLABS
        self.next_slab = 0
        self.stats = self.tile("stats", [P, N_STATS])
        self.used_cols = 0
        self.turn = 0
        self.junk_free = None

    def semaphore(self, name):
        return self.ctx.enter_context(self.nc.semaphore(name))

    def counter(self, name):
        return [self.semaphore(name), 0]

    def tile(self, name, shape):
        return self.ctx.enter_context(self.nc.sbuf_tensor(name, shape, F32))

    def cols(self, n):
        at = self.used_cols
        self.used_cols += n
        assert self.used_cols <= N_STATS
        return self.stats[:, at:at + n]

    def take_bank(self):
        while self.next_bank in self.held_banks:
            self.next_bank = (self.next_bank + 1) % N_BANKS
        i = self.next_bank
        self.next_bank = (i + 1) % N_BANKS
        return i, self.psum[:, i * BANK:(i + 1) * BANK]

    def load_slab(self, src, k0, kc, n0, nw):
        i = self.next_slab
        self.next_slab = (i + 1) % N_SLABS
        view = self.slab[i][:, 0:kc, 0:nw]
        rows = src[k0:k0 + kc * P, n0:n0 + nw].rearrange("(c p) n -> p c n", p=P)
        loaded = self.sp.put_dma(lambda e, v=view, r=rows: e.dma_start(v, r), self.slab_loaded[i],
                                 wait=self.slab_free[i])
        return i, view, loaded

    def step_background(self):
        if self.background is not None:
            next(self.background, None)

    def finish(self, steps):
        for _ in steps:
            pass

    def barrier(self):
        queues = (self.pe, self.act, self.dve, self.pool)
        ends = [q.last() for q in queues]
        for q in queues:
            q.hold(ends)

    def mm(self, out, lhsT, rhs, start, stop, wait=(), signal=False):
        return self.pe.put(lambda e: e.matmul(out, lhsT, rhs, start=start, stop=stop), wait, signal)

    def tr(self, out, in_, wait=(), signal=False):
        n = in_.shape[0]
        return self.pe.put(lambda e: e.transpose(out, in_, self.ident[0:n, 0:n]), wait, signal)

    def activate(self, out, in_, func, wait=(), **more):
        return self.act.put(lambda e: e.activation(out, in_, func, **more), wait)

    def tt(self, out, a, b, op, wait=(), q=None):
        return (q or self.dve).put(lambda e: e.tensor_tensor(out, a, b, op), wait)

    def ts(self, out, a, s1, s2, op0, op1=None, wait=(), q=None, accum_out=None):
        def issue(e):
            if accum_out is not None:
                return e.tensor_scalar(out, a, s1, s2, op0, op1, accum_out=accum_out)
            if op1 is None:
                return e.tensor_scalar(out, a, s1, None, op0)
            return e.tensor_scalar(out, a, s1, s2, op0, op1)
        return (q or self.dve).put(issue, wait)

    def stt(self, out, a, s, b, op0, op1, wait=(), **more):
        return self.dve.put(lambda e: e.scalar_tensor_tensor(out, a, s, b, op0, op1, **more), wait)

    def copy(self, out, in_, wait=(), q=None):
        q = q or self.dve
        if q is self.act:
            return q.put(lambda e: e.activation(out, in_, ACT.Copy), wait)
        return q.put(lambda e: e.tensor_copy(out, in_), wait)

    def copy_any(self, out, in_, wait=()):
        self.turn += 1
        return self.copy(out, in_, wait, self.act if self.turn % 2 else self.dve)

    def load(self, out, in_, counter, wait=(), q=None):
        return (q or self.sp).put_dma(lambda e: e.dma_start(out, in_), counter, wait)

    def feature_gemm(self, src, n0, n, act_T, T, ready, evacuate):
        done = 0
        while done < n:
            nw = min(SLAB_N, n - done)
            slot, slab, loaded = self.load_slab(src, 0, DC, n0 + done, nw)
            for j in range(-(-nw // P)):
                m = min(P, nw - j * P)
                b, bank = self.take_bank()
                for kc in range(DC):
                    end = self.mm(bank[0:m, 0:T], slab[:, kc, j * P:j * P + m], act_T[:, kc, 0:T],
                                  kc == 0, kc == DC - 1, signal=kc == DC - 1,
                                  wait=[loaded, ready, self.bank_free[b]] if kc == 0 else ())
                self.bank_free[b] = evacuate((done // P) + j, bank[0:m, 0:T], end)
            self.slab_free[slot] = end
            done += nw
            self.step_background()

    def token_gemm(self, src, K, ranges, act_T, tiles, ready, evacuate):
        kslabs = K // (DC * P)
        for n0, nw in ranges:
            banks = [self.take_bank() for _ in range(tiles)]
            self.held_banks = {b for b, _ in banks}
            for ks in range(kslabs):
                slot, slab, loaded = self.load_slab(src, ks * DC * P, DC, n0, nw)
                for t in range(tiles):
                    b, bank = banks[t]
                    for kc in range(DC):
                        end = self.mm(bank[:, 0:nw], act_T[:, ks * DC + kc, t * P:(t + 1) * P],
                                      slab[:, kc, :], ks + kc == 0, ks == kslabs - 1 and kc == DC - 1,
                                      signal=kc == DC - 1,
                                      wait=[loaded, ready, self.bank_free[b]] if kc == 0 else ())
                    if ks == kslabs - 1:
                        self.bank_free[b] = evacuate(t, n0, nw, bank[:, 0:nw], end)
                self.slab_free[slot] = end
                if ks == kslabs - 1:
                    self.held_banks = set()
                self.step_background()

    def inv_rms(self, sums, n, width, wait):
        mean, out = self.cols(n), self.cols(n)
        a = self.ts(mean, sums, 1.0 / width, EPS, ALU.mult, ALU.add, wait=wait)
        done = self.tt(out, mean, self.minus_half[:, 0:n], ALU.pow, wait=a, q=self.pool)
        return out, done

    def row_inv_rms(self, src, tiles, width, ready):
        sums = self.cols(tiles)
        ends = []
        for t in range(tiles):
            self.junk_free = self.activate(self.junk[:, 0:width], src[:, t, :], ACT.Square,
                                           wait=[ready, self.junk_free], accum_out=sums[:, t:t + 1])
            ends.append(self.junk_free)
        return self.inv_rms(sums, tiles, width, ends)

    def norm_to_features(self, src, tiles, ready, a_col, b_col, col_ready, y, y_free, dst, dst_free):
        rstd, have = self.row_inv_rms(src, tiles, D, ready)
        scaled = []
        for t in range(tiles):
            if t % 2:
                scaled.append(self.activate(y[:, t, :], src[:, t, :], ACT.Copy, scale=rstd[:, t:t + 1],
                                            wait=[have, y_free]))
            else:
                scaled.append(self.ts(y[:, t, :], src[:, t, :], rstd[:, t:t + 1], None, ALU.mult,
                                      wait=[have, y_free]))
        done = []
        for c in range(DC):
            b, bank = self.take_bank()
            for t in range(tiles):
                end = self.tr(bank[:, t * P:(t + 1) * P], y[:, t, c * P:(c + 1) * P], signal=t == tiles - 1,
                              wait=[scaled[t], self.bank_free[b]])
            view = dst[:, c, 0:tiles * P]
            if c % 2:
                e = self.activate(view, bank[:, 0:tiles * P], ACT.Identity, scale=a_col[:, c:c + 1],
                                  bias=b_col[:, c:c + 1], wait=[end, col_ready, dst_free])
            else:
                e = self.ts(view, bank[:, 0:tiles * P], a_col[:, c:c + 1], b_col[:, c:c + 1], ALU.mult,
                            ALU.add, wait=[end, col_ready, dst_free])
            self.bank_free[b] = e
            done.append(e)
        return done

    def to_features(self, src, tiles, ready, dst, dst_free, chunks=range(DC)):
        done = []
        for c in chunks:
            b, bank = self.take_bank()
            for t in range(tiles):
                end = self.tr(bank[:, t * P:(t + 1) * P], src[:, t, c * P:(c + 1) * P], signal=t == tiles - 1,
                              wait=[ready, self.bank_free[b]])
            e = self.copy_any(dst[:, c, 0:tiles * P], bank[:, 0:tiles * P], wait=[end, dst_free])
            self.bank_free[b] = e
            done.append(e)
        return done

    def columns_to_rows(self, col, n, dst, ready, dst_free):
        done = []
        for g in range(0, n, 4):
            m = min(4, n - g)
            b, bank = self.take_bank()
            for c in range(m):
                end = self.tr(bank[:, c * P:(c + 1) * P], col[:, g + c:g + c + 1].to_broadcast([P, P]),
                              signal=c == m - 1, wait=[ready, self.bank_free[b]])
            e = self.copy_any(dst[:, g * P:(g + m) * P], bank[:, 0:m * P], wait=[end, dst_free])
            self.bank_free[b] = e
            done.append(e)
        return done

    def gated_residual(self, x, tiles, m, m_ready, gate_row, gate_ready):
        rstd, have = self.row_inv_rms(m, tiles, D, m_ready)
        done = []
        for t in range(tiles):
            a = self.stt(m[:, t, :], m[:, t, :], rstd[:, t:t + 1], gate_row, ALU.mult, ALU.mult,
                         wait=[have, gate_ready])
            done.append(self.tt(x[:, t, :], x[:, t, :], m[:, t, :], ALU.add, wait=a,
                                q=self.pool if t % 2 else self.dve))
        return done


def attention(k, units, p_ring, pt_ring):
    ends = [k.bank_free[b] for b in range(N_BANKS)]
    pair_free = [[ends[0], ends[1]], [ends[2], ends[3]]]
    tr_free = [ends[4], ends[5]]
    out_free = [ends[6], ends[7]]
    p_free = [None] * 4
    pt_free = [None] * 4
    soft, moved = {}, {}

    def scores(i):
        u = units[i]
        S = u["S"]
        base = (i % 2) * 2 * BANK
        s = k.psum[:, base:base + S]
        for n, (p0, c0, w) in enumerate(u["segments"]):
            end = k.mm(s[:, p0:p0 + w], u["q"], u["k"][:, c0:c0 + w], True, True,
                       signal=n == len(u["segments"]) - 1,
                       wait=pair_free[i % 2] if n == 0 else ())
        for p0, w, add, have in u.get("bias", ()):
            end = k.tt(s[:, p0:p0 + w], s[:, p0:p0 + w], add, ALU.add, wait=[end, have])
        if "bias_free" in u:
            u["bias_free"](end)
        st = k.cols(4)
        mx, nb, rs, es = (st[:, j:j + 1] for j in range(4))
        a = k.dve.put(lambda e: e.reduce_max(mx, s, AX.X), wait=end)
        if u.get("sink") is not None:
            a = k.ts(mx, mx, QK_SCALE, u["sink"], ALU.mult, ALU.max, wait=[a, u["sink_ready"]])
            a = k.ts(nb, mx, -1.0, None, ALU.mult, wait=a)
        else:
            a = k.ts(nb, mx, -QK_SCALE, None, ALU.mult, wait=a)
        pv = p_ring[:, i % 4, 0:S]
        e1 = k.activate(pv, s, ACT.Exp, scale=QK_SCALE, bias=nb, accum_out=rs, wait=[a, p_free[i % 4]])
        pair_free[i % 2] = [e1]
        total = e1
        if u.get("sink") is not None:
            e2 = k.activate(es, u["sink"], ACT.Exp, bias=nb, wait=a)
            total = k.tt(rs, rs, es, ALU.add, wait=[e1, e2])
        soft[i] = (pv, rs, mx, total)

    def normalise(i):
        pv, rs, inv, total = soft[i]
        e = k.dve.put(lambda e: e.reciprocal(inv, rs), wait=total)
        u = units[i]
        if u["kind"] == "diff" and u["pos"] == 1:
            e = k.tt(inv, inv, u["neg_lam"], ALU.mult, wait=[e, u["lam_ready"]])
            e = k.stt(pv, pv, inv, soft[i - 1][0], ALU.mult, ALU.add, wait=[e, soft[i - 1][3]])
            p_free[(i - 1) % 4] = e
        else:
            e = k.ts(pv, pv, inv, None, ALU.mult, wait=e)
        soft[i] = (pv, rs, inv, e)

    def transposes(i):
        u = units[i]
        if u["kind"] == "diff" and u["pos"] == 0:
            return
        n = u["S"] // P
        lo, hi = pt_ring(i % 4)
        for c in range(n):
            end = k.tr(k.psum[:, 4 * BANK + c * P:4 * BANK + (c + 1) * P], p_ring[:, i % 4, c * P:(c + 1) * P],
                       signal=c == min(3, n - 1) or c == n - 1,
                       wait=[soft[i][3], tr_free[0]] if c == 0 else ([tr_free[1]] if c == 4 else ()))
            if c == min(3, n - 1):
                first = end
        p_free[i % 4] = end
        w = min(n, 4) * P
        e1 = k.copy(lo[:, 0:w], k.psum[:, 4 * BANK:4 * BANK + w], wait=[first, pt_free[i % 4]], q=k.act)
        tr_free[0] = e1
        e2 = None
        if n > 4:
            e2 = k.copy(hi[:, 0:(n - 4) * P], k.psum[:, 5 * BANK:5 * BANK + (n - 4) * P],
                        wait=[end, pt_free[i % 4]])
            tr_free[1] = e2
        moved[i] = ([e1, e2], [(lo if c < 4 else hi)[:, c % 4 * P:(c % 4 + 1) * P] for c in range(n)])

    def values(i):
        u = units[i]
        if u["pos"] == 0:
            return
        j = (i // 2) % 2
        o = k.psum[:, (6 + j) * BANK:(6 + j) * BANK + P]
        n = u["S"] // P
        for c in range(n):
            first, last = c == 0, c == n - 1
            if u["kind"] == "diff":
                end = k.mm(o, moved[i][1][c], u["v"][c], first, last, signal=last,
                           wait=[moved[i][0], out_free[j]] if first else ())
            else:
                for g in range(2):
                    have, pt = moved[i - 1 + g]
                    end = k.mm(o[g * HD:(g + 1) * HD, :], units[i - 1 + g]["v"][c], pt[c], first, last,
                               signal=last and g == 1, wait=[have, out_free[j]] if first else ())
        pt_free[i % 4] = end
        if u["kind"] != "diff":
            pt_free[(i - 1) % 4] = end
        out_free[j] = u["finish"](o, end)

    n = len(units)
    for i in range(n + 3):
        if i < n:
            scores(i)
        if 1 <= i < n + 1:
            normalise(i - 1)
        if 2 <= i < n + 2:
            transposes(i - 2)
        if i >= 3:
            values(i - 3)
    for b in range(4):
        k.bank_free[b] = pair_free[b // 2]
    k.bank_free[4], k.bank_free[5] = tr_free
    k.bank_free[6], k.bank_free[7] = out_free


def rope(k, out_view, src, cos, sin, heads, tmp, wait, tmp_free):
    w = heads * HD
    s3 = src.rearrange("p (h d) -> p h d", d=HD)
    t3 = tmp[:, 0:w].rearrange("p (h d) -> p h d", d=HD)
    u3 = tmp[:, 512:512 + w].rearrange("p (h d) -> p h d", d=HD)
    a = [k.tt(t3, s3, cos.unsqueeze(1).to_broadcast([P, heads, HD]), ALU.mult, wait=[wait, tmp_free])]
    for half in range(2):
        for axis in range(2):
            o = u3.rearrange("p h (a b f) -> p h a b f", a=2, b=2)[:, :, axis, half, :]
            i = s3.rearrange("p h (a b f) -> p h a b f", a=2, b=2)[:, :, axis, 1 - half, :]
            c = sin.rearrange("p (a b f) -> p a b f", a=2, b=2)[:, axis, half, :]
            a.append(k.tt(o, i, c.unsqueeze(1).to_broadcast([P, heads, 16]), ALU.mult, wait=[wait, tmp_free]))
    return k.tt(out_view, t3, u3, ALU.add, wait=a), a


def project_heads(k, layer, w_in, act_T, tiles, tok0, is_x, ready, V):
    QT, KT, VV = V["QT"], V["KT"], V["VV"]
    done = []
    normed = layer == 0
    stage_free = V["stage_free"]

    def stage():
        i = V["stage_next"] % 3
        V["stage_next"] += 1
        return i, V["stage"][:, i, :]

    def put_transposed(staged, nchunks, dst, chunk0, tok, have, slot):
        b, bank = k.take_bank()
        for c in range(nchunks):
            end = k.tr(bank[:, c * P:(c + 1) * P], staged[:, c * P:(c + 1) * P], signal=c == nchunks - 1,
                       wait=[have, k.bank_free[b]])
        e = k.copy_any(dst[:, chunk0:chunk0 + nchunks, tok:tok + P],
                       bank[:, 0:nchunks * P].rearrange("p (c t) -> p c t", t=P), wait=end)
        k.bank_free[b] = e
        stage_free[slot] = end
        done.append(e)

    def group(t, bank, w, roped, norm, which, twice, end, nchunks, dst, chunk0):
        heads = w // HD
        slot, staged = stage()
        staged = staged[:, 0:(2 if twice else 1) * w]
        tmp, tmp_free = V["tmp"], V["tmp_free"]
        tok = tok0 + t * P
        src, src_ready = bank[:, 0:w], end
        rel = None
        if norm:
            raw = V["raw"][:, 0:w]
            c = k.copy(raw, bank[:, 0:w], wait=[end, V["raw_free"]], q=k.act)
            sq = tmp[:, 0:w]
            a = k.tt(sq, raw, raw, ALU.mult, wait=[c, tmp_free])
            sums = k.cols(heads)
            a = k.dve.put(lambda e, o=sums, i=sq: e.tensor_reduce(o, i.rearrange("p (h d) -> p h d", d=HD),
                                                                 AX.X, ALU.add), wait=a)
            rstd, have = k.inv_rms(sums, heads, HD, a)
            rawh = raw.rearrange("p (h d) -> p h d", d=HD)
            src_ready = k.tt(rawh, rawh, rstd.unsqueeze(2).to_broadcast([P, heads, HD]), ALU.mult,
                             wait=have)
            src, rel, tmp_free = raw, c, src_ready
        shape_src = src.rearrange("p (h d) -> p h d", d=HD)
        if twice:
            view, second = (staged.rearrange("p (h r d) -> p h r d", r=2, d=HD)[:, :, i, :] for i in range(2))
        else:
            view = staged.rearrange("p (h d) -> p h d", d=HD)

        if roped:
            cos, sin = V["tables"][which]
            o, parts = rope(k, view, src, cos[:, t, :], sin[:, t, :], heads, tmp,
                            [src_ready, V["tables_ready"], stage_free[slot]], tmp_free)
            tmp_free = o
            outs = [o]
            rel = rel or outs
            V["tmp_free"] = tmp_free
        elif norm:
            g_row = V["qk_gain"][:, which * HD:(which + 1) * HD]
            outs = [k.tt(view, shape_src, g_row.unsqueeze(1).to_broadcast([P, heads, HD]), ALU.mult,
                         wait=[src_ready, V["gain_ready"], stage_free[slot]])]
        else:
            outs = [k.copy(view, shape_src, wait=[src_ready, stage_free[slot]], q=k.act)]
            rel = outs
        if norm:
            V["raw_free"] = outs
            if not roped:
                V["tmp_free"] = outs
        if twice:
            outs = outs + [k.copy(second, view, wait=outs, q=k.pool)]
        put_transposed(staged, nchunks, dst, chunk0, tok, outs, slot)
        return rel

    def evacuate(t, n0, nw, bank, end):
        sc = tok0 // P + t
        if n0 == 0:
            if not V["want_q"]:
                return None
            return group(t, bank, 512, is_x, normed, 0, False, end, 4, QT, 0)
        if n0 == 512:
            v = k.copy(VV[:, sc, 0:P], bank[:, P:2 * P], wait=end, q=k.act)
            done.append(v)
            return [group(t, bank, P, is_x, normed, 1, True, [end, v], 2, KT, 0), v]
        plain_rope = is_x and layer == 0
        if n0 == 768:
            return group(t, bank, 512, plain_rope, False, 2, False, end, 4, QT, 4)
        if n0 == 1280:
            return group(t, bank, 512, plain_rope, False, 2, False, end, 4, KT, 2)
        v = k.copy_any(VV[:, sc, P:P + 512], bank, wait=end)
        done.append(v)
        return v

    ranges = [(0, 512), (512, 256), (768, 512), (1280, 512), (1792, 512)]
    if not V["want_q"]:
        ranges = [ranges[1], ranges[3], ranges[4]]
    k.token_gemm(w_in, D, ranges, act_T, tiles, ready, evacuate)
    return done


def mlp(k, w1, w2, act_T, tiles, ready, uT, m, m_free):
    T = tiles * P
    hidden = []

    def up(j, bank, end):
        a = k.activate(uT[:, j, 0:T], bank, ACT.Relu, wait=end)
        hidden.append(k.tt(uT[:, j, 0:T], uT[:, j, 0:T], uT[:, j, 0:T], ALU.mult, wait=a))
        return a

    k.feature_gemm(w1, 0, FF, act_T, T, ready, up)
    done = []

    def down(t, n0, nw, bank, end):
        e = k.copy_any(m[:, t, n0:n0 + nw], bank, wait=[end, m_free])
        done.append(e)
        return e

    k.token_gemm(w2, FF, [(0, 512), (512, 512)], uT, tiles, hidden, down)
    return done


def build(nc, A, C, out):
    with ExitStack() as ctx:
        k = Core(nc, ctx)
        k.junk = k.tile("junk", [P, D])
        k.ident = k.tile("ident", [P, P])
        k.minus_half = k.tile("minus_half", [P, 16])
        x = k.tile("x", [P, TT_X, D])
        cx = k.tile("cx", [P, TT_C, D])
        hT = k.tile("hT", [P, DC, T_X])
        y = k.tile("y", [P, TT_X, D])
        gate_row = k.tile("gate_row", [P, D])
        colv = k.tile("colv", [P, 3 * P])
        region = k.tile("region", [P, REGION])
        s_in = k.counter("inputs_loaded")
        s_p = k.counter("pool_loaded")
        scratch = nc.dram_tensor("bias_tables", [8 * RPB_ROWS, GRID * GRID], F32, kind="Internal").ap()
        s_scr = k.counter("bias_tables_written")

        at = [0]

        def carve(*shape):
            n = int(np.prod(shape))
            v = region[:, at[0]:at[0] + n]
            at[0] += n
            assert at[0] <= REGION, at[0]
            if len(shape) == 2:
                v = v.rearrange("p (a b) -> p a b", b=shape[1])
            elif len(shape) == 3:
                v = v.rearrange("p (a b c) -> p a b c", b=shape[1], c=shape[2])
            return v

        def new_phase():
            k.barrier()
            at[0] = 0

        def rewind(to):
            at[0] = to

        t_ident = k.load(k.ident[:, :], C["ident"], s_in)
        rows = [carve(P) for _ in range(3)]
        row_parts = [
            [(A["b_mod"].rearrange("l (r q) -> (l r) q", q=P), 96), (A["c"].rearrange("b (r q) -> (b r) q", q=P), 8),
             (A["c_ctx"].rearrange("(r q) -> r q", q=P), 8), (A["c_2"].rearrange("b (r q) -> (b r) q", q=P), 8),
             (A["conv_qk_b_2"].rearrange("b (r q) -> (b r) q", q=P), 8)],
            [(A["norm_g"].rearrange("l i (r q) -> (l i r) q", q=P), 64),
             (A["b_ada_2"].rearrange("b (r q) -> (b r) q", q=P), 48),
             (A["g_mix_2"].rearrange("b (r q) -> (b r) q", q=P), 8),
             (A["g_ffn_2"].rearrange("b (r q) -> (b r) q", q=P), 8)],
            [(A["conv_qk_w_2"].rearrange("b j (r q) -> (b j r) q", q=P), 24),
             (A["conv_hy_w_2"].rearrange("b j (r q) -> (b j r) q", q=P), 36),
             (A["conv_hy_b_2"].rearrange("b (r q) -> (b r) q", q=P), 12),
             (A["b_in_2"][0, 0:1024].rearrange("(r q) -> r q", q=P), 8),
             (A["b_in_2"][0, 2064:3600].rearrange("(r q) -> r q", q=P), 12)],
        ]
        row_counts = []
        for v, parts in zip(rows, row_parts):
            r = 0
            for src, n in parts:
                k.load(v[r:r + n, :], src, s_in)
                r += n
            row_counts.append(r)
        t_in = (s_in[0], s_in[1])
        s_x = k.counter("x_loaded")
        k.load(x[:, :, :], A["x"][0].rearrange("(t p) d -> p t d", p=P), s_x)
        t_x = k.load(cx[:, :, :], A["ctx"][0].rearrange("(t p) d -> p t d", p=P), s_x)
        t_half = k.dve.put(lambda e: e.memset(k.minus_half[:, :], -0.5))
        k.pool.hold(t_half)

        cols_ready = []
        for i, (v, n) in enumerate(zip(rows, row_counts)):
            b, bank = k.take_bank()
            end = k.tr(bank[:, 0:n], v[0:n, :], wait=t_in, signal=True)
            e = k.copy(colv[:, i * P:i * P + n], bank[:, 0:n], wait=end)
            k.bank_free[b] = e
            cols_ready.append(e)
        b_modT = colv[:, 0:96]
        cT = colv[:, 96:120]
        conv_qk_bT = colv[:, 120:128]
        norm_gT = colv[:, 128:192]
        b_adaT = colv[:, 192:240]
        g_mixT, g_ffnT = colv[:, 240:248], colv[:, 248:256]
        conv_qk_wT, conv_hy_wT = colv[:, 256:280], colv[:, 280:316]
        conv_hy_bT, b_qkT, b_hxT = colv[:, 316:328], colv[:, 328:336], colv[:, 336:348]

        vecs = k.tile("vecs", [P, DC, 32])
        pick = k.tile("pick", [P, 3])
        t_pick = k.load(pick[:, :], C["pick"], k.counter("pick_loaded"))
        e = k.dve.put(lambda e: e.memset(vecs[:, :, :], 0.0))
        a = [k.activate(vecs[:, :, i], cT[:, i * 8:(i + 1) * 8], ACT.Silu, wait=[e, cols_ready]) for i in range(2)]
        vecs_ready = a + [k.copy(vecs[:, :, 2], cT[:, 16:24], wait=[e, cols_ready])]
        mods = k.tile("mods", [P, 2, 48, 2])
        mod2 = k.tile("mod2", [P, 48, 1])

        def modulation(w, first, n, dst, bias, done):
            def to_columns(s, half, have):
                b, bank = k.take_bank()
                pv = bank[:, 0:4 * n].rearrange("p (c s) -> p c s", s=n)
                for j in range(4):
                    end = k.mm(pv[:, j, :], k.junk[:, half + j * P:half + (j + 1) * P], pick[:, first:first + n],
                               True, True, signal=j == 3, wait=[have, t_pick, k.bank_free[b]] if j == 0 else ())
                k.junk_free = [k.junk_free, end]
                e = k.tt(dst[:, 4 * s:4 * s + 4, :], pv,
                         bias[:, 4 * s:4 * s + 4].unsqueeze(2).to_broadcast([P, 4, n]), ALU.add, wait=end)
                k.bank_free[b] = e
                done.append(e)

            last = None
            for s in range(12):
                slot, slab, loaded = k.load_slab(w, 0, DC, s * SLAB_N, SLAB_N)
                b, bank = k.take_bank()
                for kc in range(DC):
                    g = 32 * (kc % 4)
                    end = k.mm(bank[g:g + 32, :], vecs[:, kc, :], slab[:, kc, :], kc < 4, kc >= 4,
                               signal=kc == DC - 1,
                               wait=[loaded, vecs_ready, k.bank_free[b]] if kc == 0 else ())
                k.slab_free[slot] = end
                if last is not None:
                    to_columns(*last)
                half = s % 2 * SLAB_N
                e = k.activate(k.junk[:, half:half + SLAB_N], bank, ACT.Copy, wait=[end, k.junk_free])
                k.bank_free[b] = e
                last = (s, half, e)
                yield
            to_columns(*last)

        mod_ready, mod2_ready = [[], []], []

        def scale_cols(mod, stream, chunk, gain, ready):
            dst = k.cols(8)
            e = k.stt(dst, mod[:, chunk:chunk + 8, stream], 1.0, gain, ALU.add, ALU.mult, wait=ready)
            return dst, e

        def gate_cols(mod, stream, chunk, gain, ready):
            dst = k.cols(8)
            return dst, k.tt(dst, mod[:, chunk:chunk + 8, stream], gain, ALU.mult, wait=ready)

        rpb_rows, rpb_T = carve(32), carve(120)
        onehot = carve(GRID * GRID)
        stage_b = carve(8, 512)
        s_rpb = k.counter("rpb_loaded")
        k.load(onehot[0:32, :], C["neighbour_onehot"], s_rpb, q=k.pool)
        k.load(rpb_rows[0:120, 0:RPB_COLS], A["rpb_d"][0].rearrange("h r c -> (h r) c"), s_rpb, q=k.pool)
        ones_col = k.dve.put(lambda e: e.memset(rpb_rows[0:120, 31:32], 1.0))
        t_rpb = (s_rpb[0], s_rpb[1])
        b, bank = k.take_bank()
        end = k.tr(bank[0:32, 0:120], rpb_rows[0:120, 0:32], wait=[t_rpb, ones_col, k.bank_free[b]], signal=True)
        have = k.copy(rpb_T[0:32, :], bank[0:32, 0:120], wait=end)
        k.bank_free[b] = have
        for j in range(8):
            b, bank = k.take_bank()
            end = k.mm(bank[0:120, :], rpb_T[0:32, :], onehot[0:32, j * 512:(j + 1) * 512], True, True,
                       wait=[have, k.bank_free[b]], signal=True)
            e = k.ts(stage_b[0:120, j, :], bank[0:120, :], 1.0 / QK_SCALE, None, ALU.mult, wait=end)
            k.bank_free[b] = e
            k.load(scratch[:, j * 512:(j + 1) * 512], stage_b[0:120, j, :], s_scr, wait=e, q=k.pool)
        t_scr = (s_scr[0], s_scr[1])
        k.finish(modulation(A["w_mod"][0], 0, 2, mods[:, 0], b_modT[:, 0:48], mod_ready[0]))
        for q in (k.pe, k.act, k.dve, k.pool):
            q.hold(t_scr)

        s_tab = k.counter("rope_loaded")
        x_ready, c_ready = t_x, t_x
        for layer in range(2):
            mod = mods[:, layer]
            ready = [mod_ready[layer], cols_ready]
            gains = [norm_gT[:, layer * 32 + i * 8:layer * 32 + i * 8 + 8] for i in range(4)]
            new_phase()
            V = {"QT": carve(8, S_ALL), "KT": carve(6, S_ALL), "VV": carve(6, 640), "stage": carve(3, 512),
                 "tmp": carve(1024), "raw": carve(512), "gained": carve(4 * TT_X, HD), "stage_free": [None] * 3, "stage_next": 0,
                 "tmp_free": None, "raw_free": None, "want_q": True}
            cos, sin = carve(TT_X, HD), carve(TT_X, HD)
            small = carve(640)
            late = region[:, 14592:14592 + 4096]
            p_ring = late[:, 0:4 * S_ALL].rearrange("p (a b) -> p a b", b=S_ALL)

            def pt_ring(i):
                return y[:, i, 0:512], late[:, 4 * S_ALL + i * 256:4 * S_ALL + (i + 1) * 256]
            k.load(cos, C["rope_cos"].rearrange("(t p) d -> p t d", p=P), s_tab, q=k.pool)
            k.load(sin, C["rope_sin"].rearrange("(t p) d -> p t d", p=P), s_tab, q=k.pool)
            if layer == 0:
                qk_gain, lam_rows, subln = small[:, 0:128], small[:, 128:384], small[:, 384:512]
                cg, sg = V["gained"][:, 0:2 * TT_X, :], V["gained"][:, 2 * TT_X:, :]
                k.load(qk_gain, A["qk_norm_a"][0].rearrange("i d -> (i d)").partition_broadcast(P), s_tab, q=k.pool)
                k.load(lam_rows, A["diff_lambda"][0].rearrange("i d -> (i d)").partition_broadcast(P), s_tab,
                       q=k.pool)
                t_tab = k.load(subln, A["diff_subln"][0].partition_broadcast(P), s_tab, q=k.pool)
                V["qk_gain"], V["gain_ready"] = qk_gain, t_tab
                made = []
                for w in range(2):
                    g = qk_gain[:, w * HD:(w + 1) * HD]
                    made.append(k.tt(cg[:, w * 4:w * 4 + 4, :], cos, g.unsqueeze(1).to_broadcast([P, 4, HD]),
                                     ALU.mult, wait=t_tab))
                    for h in range(2):
                        for ax in range(2):
                            o, i = ax * 32 + h * 16, ax * 32 + (1 - h) * 16
                            made.append(k.tt(sg[:, w * 4:w * 4 + 4, o:o + 16], sin[:, :, o:o + 16],
                                             g[:, i:i + 16].unsqueeze(1).to_broadcast([P, 4, 16]), ALU.mult,
                                             wait=t_tab))
                V["tables"] = [(cg[:, 0:4, :], sg[:, 0:4, :]), (cg[:, 4:8, :], sg[:, 4:8, :]), (cos, sin)]
                V["tables_ready"] = [made, t_tab]
                prod = small[:, 512:640]
                lr = lam_rows.rearrange("p (a b d) -> p a b d", a=2, b=2)
                e = k.tt(prod.rearrange("p (a d) -> p a d", d=HD), lr[:, :, 0, :], lr[:, :, 1, :], ALU.mult,
                         wait=t_tab)
                dots, neg_lam = k.cols(2), k.cols(1)
                e = k.dve.put(lambda en, o=dots, i=prod: en.tensor_reduce(
                    o, i.rearrange("p (a d) -> p a d", d=HD), AX.X, ALU.add), wait=e)
                e = k.activate(dots, dots, ACT.Exp, wait=e)
                e = k.tt(neg_lam, dots[:, 1:2], dots[:, 0:1], ALU.subtract, wait=e)
                lam_ready = k.ts(neg_lam, neg_lam, LAM0, None, ALU.subtract, wait=e)
                e = k.ts(subln, subln, 1.0 - LAM0, None, ALU.mult, wait=t_tab)
                subln_ready = e
            else:
                sink = small[:, 0:8]
                masks = small[:, 8:264]
                bias_ring = [y[:, i, 512:1024] for i in range(4)]
                k.load(masks, C["window_masks"], s_tab, q=k.pool)
                t_tab = k.load(sink, A["sink_c"][0].partition_broadcast(P), s_tab, q=k.pool)
                V["tables"] = [(cos, sin)] * 3
                V["tables_ready"] = t_tab
            stash = []
            for stream in (1, 0):
                src, tiles, src_ready = ((x, TT_X, x_ready), (cx, TT_C, c_ready))[stream]
                A1, e1 = scale_cols(mod, stream, 8, gains[0], ready)
                normed = k.norm_to_features(src, tiles, src_ready, A1, mod[:, 0:8, stream], [e1, ready], y,
                                            k.pe.last(), hT, k.pe.last())
                V["want_q"] = layer == 0 or stream == 0
                stash.append(project_heads(k, layer, A["w_in"][layer], hT, tiles, 0 if stream else T_C,
                                           stream == 0, normed, V))
            QT, KT, VV = V["QT"], V["KT"], V["VV"]
            k.barrier()
            mixed = {}
            for stream in ((1, 0) if layer == 0 else (0,)):
                tiles = TT_C if stream else TT_X
                mix_done = []
                units = []
                full = [(0, 0, 256)] if stream else [(0, 0, 512), (512, 512, 256)]
                S = T_C if stream else S_ALL
                qtok = 0 if stream else T_C

                def stacked(t, c):
                    def f(o, end):
                        e = k.copy_any(hT[:, c, t * P:(t + 1) * P], o, wait=end)
                        mix_done.append(e)
                        return e
                    return f

                def diff_out(t, h):
                    def f(o, end):
                        e = k.copy_any(y[:, t, 512 + h * P:512 + (h + 1) * P], o, wait=end)
                        diff_done.append(e)
                        return e
                    return f

                diff_done = []
                bias_state = {"n": 0}
                s_bias = [k.counter(f"bias_loaded{layer}{stream}{i}") for i in range(4)] if layer == 1 else None
                for c, t, g in [(c, t, g) for c in range(4) for t in range(tiles) for g in range(2)]:
                        h, kv, pb = 2 * c + g, c // 2, 64 * g
                        q = QT[pb:pb + 64, c, qtok + t * P:qtok + (t + 1) * P]
                        u = {"q": q, "kind": "stack", "pos": g, "finish": stacked(t, c)}
                        if layer == 0:
                            u.update(S=S, segments=full, k=KT[pb:pb + 64, kv, :],
                                     v=[VV[:, c, kv * HD:(kv + 1) * HD] for c in range(S // P)])
                        else:
                            lo, hi = max(0, t - 1), min(TT_X - 1, t + 1)
                            n = hi - lo + 1
                            segs = [(0, 0, 256), (256, T_C + lo * P, min(n, 2) * P)]
                            if n == 3:
                                segs.append((512, T_C + (lo + 2) * P, P))
                            bias = []
                            if t > 0:
                                bias.append((256, P, masks[:, 0:P], t_tab))
                            if t < TT_X - 1:
                                bias.append((256 + (n - 1) * P, P, masks[:, P:2 * P], t_tab))
                            u.update(S=T_C + n * P, segments=segs, k=KT[pb:pb + 64, kv, :], bias=bias,
                                     sink=sink[:, h:h + 1], sink_ready=t_tab,
                                     v=[VV[:, c, kv * HD:(kv + 1) * HD] for c in [0, 1] + [2 + lo + i for i in range(n)]])
                        units.append(u)
                for c, t, g in [(c, t, g) for c in range(4) for t in range(tiles) for g in range(2)]:
                    h, pb = 2 * c + g, 64 * g
                    u = {"q": QT[pb:pb + 64, 4 + c, qtok + t * P:qtok + (t + 1) * P], "S": S, "segments": full,
                         "k": KT[pb:pb + 64, 2 + c, :], "pos": g}
                    if layer == 0:
                        u.update(kind="diff", finish=diff_out(t, c), neg_lam=neg_lam, lam_ready=lam_ready,
                                 v=[VV[:, s, P + c * P:P + (c + 1) * P] for s in range(S // P)])
                    else:
                        i = bias_state["n"] % 4
                        bias_state["n"] += 1
                        u.update(kind="stack", finish=stacked(t, 4 + c), load_bias=(i, h, t),
                                 v=[VV[:, s, P + h * HD:P + (h + 1) * HD] for s in range(S // P)])
                    units.append(u)
                if layer == 1:
                    free = [None] * 4

                    def with_bias(u):
                        i, h, t = u["load_bias"]

                        def start():
                            for rs in range(2):
                                r = 2 * t + rs
                                src = scratch[h * RPB_ROWS + 7 - r:h * RPB_ROWS + 15 - r, :].rearrange(
                                    "r (q c) -> q r c", c=GRID)
                                dst = bias_ring[i][64 * rs:64 * rs + 64, :].rearrange("p (r c) -> p r c", c=GRID)
                                tok = k.load(dst, src, s_bias[i], wait=[free[i], t_scr], q=k.pool)
                            return tok
                        have = start()
                        u["bias"] = [(256, 256, bias_ring[i][:, 0:256], have),
                                     (512, 256, bias_ring[i][:, 256:512], have)]

                        def release(tok):
                            free[i] = tok
                        u["bias_free"] = release
                    u_list = UnitStream(units, with_bias)
                else:
                    u_list = units
                attention(k, u_list, p_ring, pt_ring)
                if layer == 0:
                    for t in range(tiles):
                        o = y[:, t, 512:1024]
                        e = k.tt(V["tmp"][:, 0:512], o, o, ALU.mult, wait=[diff_done, k.dve.last()])
                        sums = k.cols(4)
                        e = k.dve.put(lambda en, s=sums: en.tensor_reduce(
                            s, V["tmp"][:, 0:512].rearrange("p (h d) -> p h d", d=P), AX.X, ALU.add), wait=e)
                        rstd, have = k.inv_rms(sums, 4, P, e)
                        o3 = o.rearrange("p (h d) -> p h d", d=P)
                        e = k.tt(o3, o3, rstd.unsqueeze(2).to_broadcast([P, 4, P]), ALU.mult, wait=have)
                        e = k.tt(o3, o3, subln.unsqueeze(1).to_broadcast([P, 4, P]), ALU.mult,
                                 wait=[e, subln_ready])
                        diff_done.append(e)
                    mix_done += k.to_features(y, tiles, diff_done, hT, k.pe.last(), range(4, DC))
                g1, e = gate_cols(mod, stream, 16, gains[1], ready)
                g_ready = k.columns_to_rows(g1, 8, gate_row, e, [k.dve.last(), k.pool.last()])
                tr_end = k.pe.last()
                m_done = []

                def out_evac(t, n0, nw, bank, end):
                    e = k.copy_any(y[:, t, n0:n0 + nw], bank, wait=[end, tr_end])
                    m_done.append(e)
                    return e

                k.token_gemm(A["w_out"][layer], D, [(0, 512), (512, 512)], hT, tiles, mix_done, out_evac)
                r = k.gated_residual(cx if stream else x, tiles, y, m_done, gate_row[:, :], g_ready)
                mixed[stream] = r
                k.barrier()
            new_phase()
            uT = carve(FF // P, T_X)
            for stream in ((1, 0) if layer == 0 else (0,)):
                src, tiles = ((x, TT_X), (cx, TT_C))[stream]
                A2, e1 = scale_cols(mod, stream, 32, gains[2], ready)
                normed = k.norm_to_features(src, tiles, mixed[stream], A2, mod[:, 24:32, stream], [e1, ready], y,
                                            [k.pe.last(), k.dve.last(), k.pool.last()], hT, k.pe.last())
                g2, e = gate_cols(mod, stream, 40, gains[3], ready)
                g_ready = k.columns_to_rows(g2, 8, gate_row, e, [k.dve.last(), k.pool.last()])
                if layer == 0:
                    later = (modulation(A["w_mod"][1], 0, 2, mods[:, 1], b_modT[:, 48:96], mod_ready[1]) if stream
                             else modulation(A["w_ada_2"][0], 2, 1, mod2[:, :, :], b_adaT, mod2_ready))
                    k.background = later
                m_done = mlp(k, A["w_mlp_in"][layer], A["w_mlp_out"][layer], hT, tiles, normed, uT, y,
                             k.pe.last())
                if layer == 0:
                    k.background = None
                    k.finish(later)
                r = k.gated_residual(src, tiles, y, m_done, gate_row[:, :], g_ready)
                if stream:
                    c_ready = r
                else:
                    x_ready = r
                k.barrier()

        second_block(k, nc, A, C, out, x, x_ready, hT, y, gate_row, carve, new_phase,
                     dict(cT=cT, cols_ready=cols_ready, b_adaT=b_adaT, g_mixT=g_mixT, g_ffnT=g_ffnT,
                          conv_qk_wT=conv_qk_wT, conv_qk_bT=conv_qk_bT, conv_hy_wT=conv_hy_wT,
                          conv_hy_bT=conv_hy_bT, b_qkT=b_qkT, b_hxT=b_hxT, mod2=mod2, mod2_ready=mod2_ready,
                          scale_cols=scale_cols, rewind=rewind, cx=cx, scratch_done=t_scr))

        with nc.Block() as block:
            @block.sync
            def _(e):
                k.sp.play(e)

            @block.tensor
            def _(e):
                k.pe.play(e)

            @block.scalar
            def _(e):
                k.act.play(e)

            @block.vector
            def _(e):
                k.dve.play(e)

            @block.gpsimd
            def _(e):
                k.pool.play(e)


class UnitStream:

    def __init__(self, units, prepare):
        self.units, self.prepare, self.made = units, prepare, set()

    def __len__(self):
        return len(self.units)

    def __getitem__(self, i):
        if i not in self.made:
            self.made.add(i)
            if "load_bias" in self.units[i]:
                self.prepare(self.units[i])
        return self.units[i]


def short_conv(k, out, raw, w, b, T, wait):
    e = k.ts(out, raw, w[1], b, ALU.mult, ALU.add, wait=wait)
    e = k.stt(out[:, 1:T], raw[:, 0:T - 1], w[0], out[:, 1:T], ALU.mult, ALU.add, wait=e)
    return k.stt(out[:, 0:T - 1], raw[:, 1:T], w[2], out[:, 0:T - 1], ALU.mult, ALU.add, wait=e)


def group_rms(k, view, groups, width, gain, gain_ready, tmp, ready):
    n = groups * width
    e = k.tt(tmp[:, 0:n], view, view, ALU.mult, wait=[ready, k.dve.last()])
    sums = k.cols(groups)
    e = k.dve.put(lambda en: en.tensor_reduce(sums, tmp[:, 0:n].rearrange("p (h d) -> p h d", d=width),
                                              AX.X, ALU.add), wait=e)
    rstd, have = k.inv_rms(sums, groups, width, e)
    v3 = view.rearrange("p (h d) -> p h d", d=width)
    e = k.tt(v3, v3, rstd.unsqueeze(2).to_broadcast([P, groups, width]), ALU.mult, wait=have)
    return k.tt(view, view, gain, ALU.mult, wait=[e, gain_ready])


def mlstm(k, qkT, vpad, gates, rows, w, hT, y, consts, ready, carve):
    J, ones, masks = consts["J"], consts["ones"], consts["tri"]
    c_ready = consts["ready"]
    NC_ = T_X // P
    R = 2 * MH
    k_tok = y[:, :, MH * MD:2 * MH * MD]
    kt_done = []
    for c in range(NC_):
        b, bank = k.take_bank()
        for h in range(MH):
            end = k.tr(bank[:, h * P:(h + 1) * P], qkT[:, MH + h, c * P:(c + 1) * P], signal=h == MH - 1,
                       wait=[ready, k.bank_free[b]])
        e = k.copy_any(k_tok[:, c, :], bank, wait=end)
        k.bank_free[b] = e
        kt_done.append(e)
    gsel = carve(NC_ * 4, 8)
    g4 = gsel.rearrange("p (c n d) r -> p c n d r", n=2, d=2)
    e = k.dve.put(lambda en: en.memset(gsel, 0.0))
    sel = []
    for kind in range(2):
        for d in range(2):
            src = gates[:, :, (2 * d + kind) * 4:(2 * d + kind) * 4 + 4]
            sel.append(k.copy(g4[:, :, kind, d, d * 4:d * 4 + 4], src, wait=[e, ready]))
    row = [hT[0:R, i, :] for i in range(8)]
    W, LF, B, CM, M, E_END, E_INT, E_NM = row
    raw_rows = []
    for kind in range(2):
        b, bank = k.take_bank()
        for c in range(NC_):
            k.mm(bank[0:R, c * P:(c + 1) * P], g4[:, c, kind, 0, :], k.ident[:, :], True, False,
                 wait=[sel, k.bank_free[b], c_ready])
            end = k.mm(bank[0:R, c * P:(c + 1) * P], g4[:, NC_ - 1 - c, kind, 1, :], J, False, True,
                       signal=c == NC_ - 1)
        e = k.copy(row[kind], bank[0:R, :], wait=end)
        k.bank_free[b] = e
        raw_rows.append(e)
    e = k.stt(B, LF, -1.0, LF, ALU.mult, ALU.max, wait=raw_rows[1])
    e = k.activate(B, B, ACT.Exp, scale=-1.0, wait=e)
    e = k.activate(B, B, ACT.Ln, bias=1.0, wait=e)
    lf = k.stt(LF, LF, 0.0, B, ALU.min, ALU.subtract, wait=e)
    one = k.dve.put(lambda en: en.memset(E_END, 1.0))
    sc = []
    for c in range(NC_):
        s = slice(c * P, (c + 1) * P)
        sc.append(k.dve.put(lambda en, s=s: en.tensor_tensor_scan(B[:, s], E_END[:, s], LF[:, s], 0.0, ALU.mult,
                                                                  ALU.add), wait=[lf, one]))
    e = k.tt(W, W, B, ALU.subtract, wait=[sc, raw_rows[0]])
    cm = []
    for c in range(NC_):
        s = slice(c * P, (c + 1) * P)
        cm.append(k.dve.put(lambda en, s=s: en.tensor_tensor_scan(CM[:, s], W[:, s], W[:, s], -3.0e38, ALU.max,
                                                                  ALU.max), wait=e))
    sm = carve(64)[0:R, :]
    m_in, g_m, a_c, spl, ncml = sm[:, 0:5], sm[:, 8:12], sm[:, 12:16], sm[:, 16:24], sm[:, 24:28]
    last = slice(P - 1, T_X, P)
    e0 = k.dve.put(lambda en: en.memset(m_in[:, 0:1], NEG))
    e1 = k.tt(a_c, B[:, last], CM[:, last], ALU.add, wait=cm)
    ncml_ready = k.ts(ncml, CM[:, last], -1.0, None, ALU.mult, wait=cm)
    e = [e0, e1]
    for c in range(NC_):
        e = k.tt(g_m[:, c:c + 1], B[:, c * P + P - 1:c * P + P], m_in[:, c:c + 1], ALU.add, wait=e)
        e = k.tt(m_in[:, c + 1:c + 2], g_m[:, c:c + 1], a_c[:, c:c + 1], ALU.max, wait=e)
    e1 = k.tt(spl[:, 0:4], g_m, m_in[:, 1:5], ALU.subtract, wait=e)
    e2 = k.tt(spl[:, 4:8], a_c, m_in[:, 1:5], ALU.subtract, wait=e)
    spl_ready = k.activate(spl, spl, ACT.Exp, wait=[e1, e2])
    m_done, q_done = [], []
    for c in range(NC_):
        s = slice(c * P, (c + 1) * P)
        m_done.append(k.ts(M[:, s], CM[:, s], m_in[:, c:c + 1], None, ALU.max, wait=e))
        q_done.append(k.activate(E_END[:, s], W[:, s], ACT.Exp, bias=ncml[:, c:c + 1], wait=[ncml_ready, sc]))
        q_done.append(k.activate(E_INT[:, s], M[:, s], ACT.Exp, scale=-1.0, bias=m_in[:, c:c + 1],
                                 wait=m_done[-1]))
    e = k.tt(E_NM, B, M, ALU.add, wait=m_done)
    q_done.append(k.activate(E_NM, E_NM, ACT.Exp, scale=-1.0, wait=e))
    Q = [W, M, E_END, E_INT, E_NM]
    nq = len(Q)
    craw, colsq = carve(NC_ * nq, R), carve(NC_ * nq, R)
    b, bank = k.take_bank()
    for c in range(NC_):
        for i, q in enumerate(Q):
            end = k.tr(bank[:, (c * nq + i) * R:(c * nq + i + 1) * R], q[:, c * P:(c + 1) * P],
                       wait=[q_done, m_done, k.bank_free[b]], signal=True)
    n = NC_ * nq * R
    e1 = k.copy(craw, bank[:, 0:n].rearrange("p (n r) -> p n r", r=R), wait=end)
    k.bank_free[b] = e1
    e2 = k.copy(colsq[:, :, 0:4], craw[:, :, 0:4], wait=e1)
    b, bank = k.take_bank()
    end = k.mm(bank[:, 0:n // 2].rearrange("p (n r) -> p n r", r=4), J, craw[:, :, 4:8], True, True,
               wait=[e1, k.bank_free[b], c_ready], signal=True)
    cols_done = [e2]
    for c in range(NC_):
        o = (NC_ - 1 - c) * nq
        cols_done.append(k.copy(colsq[:, o:o + nq, 4:8],
                                bank[:, c * nq * 4:(c + 1) * nq * 4].rearrange("p (n r) -> p n r", r=4), wait=end))
    k.bank_free[b] = cols_done[-1]

    def col(c, q, r):
        return colsq[:, c * nq + q, r:r + 1]

    diag = carve(8, 8)[0:R, :, :]
    e = k.tt(diag, spl.unsqueeze(2).to_broadcast([R, 8, 8]),
             k.ident[0:R, 0:R].unsqueeze(1).to_broadcast([R, 8, 8]), ALU.mult, wait=spl_ready)
    sB = carve(8, 8)
    b, bank = k.take_bank()
    end = k.mm(bank[:, 0:64].rearrange("p (n r) -> p n r", r=8), ones[0:R, :], diag, True, True,
               wait=[e, k.bank_free[b], c_ready], signal=True)
    sB_ready = k.copy(sB, bank[:, 0:64].rearrange("p (n r) -> p n r", r=8), wait=end)
    k.bank_free[b] = sB_ready
    DT = carve(2, T_X)
    PT = carve(2, T_X)
    ve = carve(2, NC_ * 129)
    st = carve(2, 3 * 129)
    num = carve(2, 129)
    tmp = carve(2, 129)
    free = [None, None]
    num_free = [None, None]
    y_tok = {}
    step = 0
    for r in range(R):
        d, h, i = r // MH, r % MH, r % 2
        b, bank = k.take_bank()
        for c in range(NC_):
            end = k.tr(bank[:, c * P:(c + 1) * P], col(c, 1, r).to_broadcast([P, P]), signal=c == NC_ - 1,
                       wait=[cols_done, k.bank_free[b]])
        e = []
        for c in range(NC_):
            e.append(k.ts(DT[:, i, c * P:(c + 1) * P], bank[:, c * P:(c + 1) * P], col(c, 0, r), 0.0,
                          ALU.subtract, ALU.max, wait=[end, free[i]]))
        k.bank_free[b] = e[-1]
        e = k.activate(DT[:, i, :], DT[:, i, :], ACT.Exp, scale=-1.0, wait=e)
        d3 = DT[:, i, :].rearrange("p (c t) -> p c t", t=P)
        dm = k.tt(d3, d3, masks[:, d, :].unsqueeze(1).to_broadcast([P, NC_, P]), ALU.mult, wait=[e, c_ready],
                  q=k.pool)
        b, bank = k.take_bank()
        for c in range(NC_):
            s = slice(c * P, (c + 1) * P)
            end = k.mm(bank[:, s], qkT[:, MH + h, s], qkT[:, h, s], True, True, signal=c == NC_ - 1,
                       wait=[ready, k.bank_free[b]])
        pt_ready = k.tt(PT[:, i, :], bank, DT[:, i, :], ALU.mult, wait=[end, dm, free[i]])
        k.bank_free[b] = pt_ready
        order = list(range(NC_)) if d == 0 else list(range(NC_ - 1, -1, -1))
        v3 = ve[:, i, :].rearrange("p (c n) -> p c n", n=129)
        s3 = st[:, i, :].rearrange("p (c n) -> p c n", n=129)
        state_ready = None
        ends = []
        for n_, c in enumerate(order):
            if n_ < NC_ - 1:
                a = k.activate(v3[:, c, :], vpad[:, c * MH + h, :], ACT.Copy, scale=col(c, 2, r),
                               wait=[cols_done, ready, free[i]])
                b, bank = k.take_bank()
                end = k.mm(bank[:, 0:129], k_tok[:, c, h * P:(h + 1) * P], v3[:, c, :], True, True,
                           wait=[a, kt_done, k.bank_free[b]], signal=True)
                loc = k.activate(s3[:, n_, :], bank[:, 0:129], ACT.Copy, scale=sB[:, 4 + n_, r:r + 1],
                                 wait=[end, sB_ready, free[i]])
                k.bank_free[b] = loc
                if n_ == 0:
                    nxt = loc
                else:
                    nxt = k.stt(s3[:, n_, :], s3[:, n_ - 1, :], sB[:, n_, r:r + 1], s3[:, n_, :], ALU.mult,
                                ALU.add, wait=[loc, state_ready])
            b, bank = k.take_bank()
            end = k.mm(bank[:, 0:129], PT[:, i, c * P:(c + 1) * P], vpad[:, c * MH + h, :], True, True,
                       wait=[pt_ready, k.bank_free[b]], signal=True)
            j = step % 2
            step += 1
            if n_ > 0:
                end2 = k.mm(bank[:, 256:385], qkT[:, h, c * P:(c + 1) * P], s3[:, n_ - 1, :], True, True,
                            wait=state_ready, signal=True)
                e = k.activate(tmp[:, j, :], bank[:, 256:385], ACT.Copy, scale=col(c, 3, r),
                               wait=[end2, num_free[j]])
                e = k.tt(num[:, j, :], bank[:, 0:129], tmp[:, j, :], ALU.add, wait=[e, num_free[j]])
                end = end2
            else:
                e = k.copy(num[:, j, :], bank[:, 0:129], wait=[end, num_free[j]])
            k.bank_free[b] = e
            den = k.cols(2)
            e = k.ts(den[:, 0:1], num[:, j, 128:129], col(c, 4, r), None, ALU.max, wait=e)
            e = k.stt(den[:, 0:1], num[:, j, 128:129], -1.0, den[:, 0:1], ALU.mult, ALU.max, wait=e)
            e = k.dve.put(lambda en, den=den: en.reciprocal(den[:, 1:2], den[:, 0:1]), wait=e)
            o = y[:, c, h * P:(h + 1) * P]
            if d == 0:
                e = k.ts(o, num[:, j, 0:128], den[:, 1:2], None, ALU.mult, wait=e)
            else:
                e = k.stt(o, num[:, j, 0:128], den[:, 1:2], o, ALU.mult, ALU.add, wait=[e, y_tok[(c, h)]])
            y_tok[(c, h)] = e
            num_free[j] = e
            ends += [e, end]
            if n_ < NC_ - 1:
                state_ready = nxt
        free[i] = ends
    return list(y_tok.values())


def hyena(k, u_tok, A, C, cx, hT, y, gate_row, carve, consts, ready):
    N_F = 2 * T_X
    TC = T_X // P
    dft, alt_re, alt_im, alt_g = carve(TC, N_F), carve(TC, P), carve(TC, P), carve(T_X)
    U = carve(2 * TC, HYW)
    Kr, Ki, KrB, hid2_all, bias_row = carve(TC, HYW), y[:, :, HYW:2 * HYW], carve(HYW), carve(HYW), carve(HYW)
    s_bias = k.counter("hyena_bias_loaded")
    s_dft = k.counter("dft_loaded")
    tp = "(t p) f -> p t f"
    k.load(dft, C["dft"].rearrange(tp, p=P), s_dft, q=k.pool)
    k.load(alt_re, C["dft_alt_re"].rearrange(tp, p=P), s_dft, q=k.pool)
    k.load(alt_im, C["dft_alt_im"].rearrange(tp, p=P), s_dft, q=k.pool)
    t_dft = k.load(alt_g, C["dft_alt_back"], s_dft, q=k.pool)
    s_f = k.counter("filter_loaded")
    z0, w1, w2, fcol, tcol = U[0:33, 0, :], U[0:33, 1, 0:64], U[0:64, 1, 64:128], U[0:64, 1, 128:136], k.cols(8)
    deltas = cx[:, :, :].rearrange("p t d -> p (t d)")
    hid2 = hid2_all[0:64, :]
    k.load(z0, C["hyena_z"], s_f, q=k.pool)
    k.load(w1, A["hy_w1_2"][0], s_f, q=k.pool)
    k.load(w2, A["hy_w2_2"][0], s_f, q=k.pool)
    for i, n in enumerate(("hy_b1_2", "hy_b2_2", "hy_freq_2")):
        k.load(fcol[:, i:i + 1], A[n][0].rearrange("(p a) -> p a", a=1), s_f, q=k.pool)
    k.load(tcol[:, 0:6], C["hyena_cols"], s_f, q=k.pool)
    t_f = k.load(deltas, A["hy_deltas_2"][0].partition_broadcast(P), s_f, q=k.pool)
    d_ready = k.stt(deltas, deltas, -1.0, deltas, ALU.mult, ALU.max, wait=t_f)
    arg, turns = U[0:64, 2, :], U[0:64, 3, :]

    def sine_layer(w, z, n, bias, out, wait):
        b, bank = k.take_bank()
        end = k.mm(bank[0:64, :], w, z, True, True, wait=[wait, t_f, k.bank_free[b]], signal=True)
        e = k.ts(arg, bank[0:64, :], bias, fcol[:, 2:3], ALU.add, ALU.mult, wait=end)
        k.bank_free[b] = e
        e = k.ts(turns, arg, 1.0 / (2.0 * math.pi), ROUND, ALU.mult, ALU.add, wait=e)
        e = k.ts(turns, turns, ROUND, None, ALU.subtract, wait=e)
        for part in TWO_PI:
            e = k.stt(arg, turns, -part, arg, ALU.mult, ALU.add, wait=e)
        e = k.ts(arg, arg, 3.1415925, -3.1415925, ALU.min, ALU.max, wait=e)
        return k.activate(out, arg, ACT.Sin, wait=e)

    hid1 = U[0:64, 4, :]
    e = sine_layer(w1, z0, 33, fcol[:, 0:1], hid1, None)
    hid_ready = sine_layer(w2, hid1, 64, fcol[:, 1:2], hid2, e)
    s_w3 = k.counter("filter_w3_loaded")
    conv_done = ready
    win, hbuf = k.junk[:, 0:512], k.junk[:, 512:1024]
    w3_free = [None]
    back_end = None
    for order in range(2):
        w3 = gate_row[0:64, 0:1024]
        t_w3 = k.load(w3, A["hy_w3_2"][0, :, order * 1024:(order + 1) * 1024], s_w3,
                      wait=[w3_free, hid_ready], q=k.pool)
        t_bias = k.load(bias_row, A["hy_bias_2"][0, order].partition_broadcast(P), s_bias,
                        wait=conv_done, q=k.pool)
        HS, HDIF = U[:, 0:TC, :], U[:, TC:2 * TC, :]
        sum_done = []
        prev = back_end and last
        for c in range(TC):
            parts = []
            for dr in range(2):
                b, bank = k.take_bank()
                end = k.mm(bank, hid2[:, c * P:(c + 1) * P], w3[:, dr * 512:(dr + 1) * 512], True, True,
                           wait=[t_w3, hid_ready, k.bank_free[b]], signal=True)
                dst = (HS, HDIF)[dr][:, c, :]
                n0 = order * 1024 + dr * 512
                e = k.activate(win, deltas[:, n0:n0 + 512], ACT.Exp, scale=tcol[:, c:c + 1],
                               wait=[d_ready, prev, t_f])
                prev = k.stt(dst, win, 0.05, bank, ALU.add, ALU.mult, wait=[e, end, back_end])
                k.bank_free[b] = prev
                parts.append(prev)
            w3_free[0] = end
            e = k.tt(hbuf, HS[:, c, :], HDIF[:, c, :], ALU.add, wait=[parts, sum_done])
            e2 = k.tt(HDIF[:, c, :], HS[:, c, :], HDIF[:, c, :], ALU.subtract, wait=e)
            sum_done = [k.copy(HS[:, c, :], hbuf, wait=[e, e2]), e2]
        k_ready = []
        for j in range(2 * TC + 1):
            b, bank = k.take_bank()
            for t in range(TC):
                if j < TC:
                    lhs, rhs = dft[:, t, j * P:(j + 1) * P], HS[:, t, :]
                elif j < 2 * TC:
                    lhs, rhs = dft[:, t, j * P:(j + 1) * P], HDIF[:, t, :]
                else:
                    lhs, rhs = alt_re[:, t, :], HS[:, t, :]
                end = k.mm(bank, lhs, rhs, t == 0, t == TC - 1, signal=t == TC - 1,
                           wait=[sum_done, t_dft, k.bank_free[b]] if t == 0 else ())
            dst = Kr[:, j, :] if j < TC else Ki[:, j - TC, :] if j < 2 * TC else KrB
            scale = tcol[:, 4:5] if j in (0, 2 * TC) else 2.0 / N_F
            e = k.ts(dst, bank, scale, None, ALU.mult, wait=[end, conv_done])
            k.bank_free[b] = e
            k_ready.append(e)
        filters_read = end
        z = [u_tok[:, t, 2 * HYW:3 * HYW] for t in range(TC)]
        u_ready = []
        for j in range(2 * TC):
            b, bank = k.take_bank()
            for t in range(TC):
                lhs = alt_im[:, t, :] if j == TC else dft[:, t, j * P:(j + 1) * P]
                end = k.mm(bank, lhs, z[t], t == 0, t == TC - 1, signal=t == TC - 1,
                           wait=[conv_done, k.bank_free[b], t_dft] if t == 0 else ())
            e = k.copy(U[:, j, :], bank, wait=[end, filters_read], q=k.act)
            k.bank_free[b] = e
            u_ready.append(e)
        Y = hT
        prod = []
        t2 = hbuf
        last = k.dve.last()
        for j in range(TC):
            r, i = U[:, j, :], U[:, TC + j, :]
            krb = KrB if j == 0 else Kr[:, j, :]
            w = [u_ready, k_ready, last]
            a = k.tt(Y[:, j, :], r, Kr[:, j, :], ALU.mult, wait=w + [back_end])
            b_ = k.tt(t2, i, Ki[:, j, :], ALU.mult, wait=w)
            c_ = k.tt(Y[:, j, :], Y[:, j, :], t2, ALU.subtract, wait=[a, b_])
            d_ = k.tt(Y[:, TC + j, :], r, Ki[:, j, :], ALU.mult, wait=w + [back_end])
            e_ = k.tt(win, i, krb, ALU.mult, wait=w)
            f_ = k.tt(Y[:, TC + j, :], Y[:, TC + j, :], win, ALU.add, wait=[d_, e_])
            last = [c_, f_]
            prod += [c_, f_]
        new = []
        for t in range(TC):
            b, bank = k.take_bank()
            for j in range(2 * TC):
                lhs = alt_g[:, t * P:(t + 1) * P] if j == TC else dft[:, j % TC, (j // TC) * T_X + t * P:(j // TC) * T_X + (t + 1) * P]
                end = k.mm(bank, lhs, Y[:, j, :], j == 0, j == 2 * TC - 1, signal=j == 2 * TC - 1,
                           wait=[prod, k.bank_free[b]] if j == 0 else ())
            e = k.tt(z[t], z[t], bias_row, ALU.mult, wait=[end, u_ready, t_bias])
            e = k.tt(z[t], z[t], bank, ALU.add, wait=e)
            k.bank_free[b] = e
            dst = z[t] if order == 0 else y[:, t, HYW:2 * HYW]
            new.append(k.tt(dst, z[t], u_tok[:, t, order * HYW:(order + 1) * HYW], ALU.mult,
                            wait=[e, hid_ready, w3_free[0]]))
        back_end = end
        conv_done = new
    return new


def experts(k, A, x, y, y_ready, hT, h_ready, A2, B2, B2_ready, consts, carve):
    TC = T_X // P
    HALF = SLAB_N // 2
    aff, ex = carve(TC, N_EXP), carve(TC, N_EXP)
    c_ready = consts["ready"]
    logit_done = []

    def logits(t, n0, nw, bank, end):
        e = k.copy(ex[:, t, :], bank, wait=end)
        logit_done.append(e)
        return e

    k.token_gemm(A["w_router_2"][0], D, [(0, N_EXP)], hT, TC, h_ready, logits)
    mx = k.cols(8)
    e = k.dve.put(lambda en: en.tensor_reduce(mx[:, 0:4], ex, AX.X, ALU.max), wait=logit_done)
    e = k.tt(ex, ex, mx[:, 0:4].unsqueeze(2).to_broadcast([P, TC, N_EXP]), ALU.subtract, wait=e)
    e = k.activate(ex, ex, ACT.Exp, wait=e)
    e = k.dve.put(lambda en: en.tensor_reduce(mx[:, 4:8], ex, AX.X, ALU.add), wait=e)
    e = k.dve.put(lambda en: en.reciprocal(mx[:, 0:4], mx[:, 4:8]), wait=e)
    aff_ready = k.tt(aff, ex, mx[:, 0:4].unsqueeze(2).to_broadcast([P, TC, N_EXP]), ALU.mult, wait=e)
    moe = carve(TC, D)
    counts = carve(2, TC * 3)
    scrap = carve(T_X)
    hot = carve(2, TC * CAP)
    wgt = carve(2, TC * P)
    wT = carve(4, T_X)
    xs = carve(2, DC * CAP)
    hid = carve(2, (FF_E // P) * CAP)
    act_g = carve(2, HALF)
    tok_h = carve(2, HALF)
    ye = carve(4, 2 * HALF)
    zero = k.dve.put(lambda en: en.memset(counts, 0.0))
    hot_free, wgt_free, xs_free, hid_free, g_free, h_free = ([None, None] for _ in range(6))
    wT_free, ye_free = [None] * 4, [None] * 4
    prepared = {}
    wT_ready = {}
    moe_done = {}

    def choose(e_):
        i = e_ % 2
        b, bank = k.take_bank()
        for c in range(TC):
            end = k.tr(bank[:, c * P:(c + 1) * P], aff[:, c, e_:e_ + 1].to_broadcast([P, P]), signal=c == TC - 1,
                       wait=[aff_ready, k.bank_free[b]])
        cnt = counts[:, i, :].rearrange("p (t n) -> p t n", n=3)
        got = []
        for t in range(TC):
            a = aff[:, t, e_:e_ + 1]
            w = [end, zero, k.dve.last()]
            if t:
                e = k.ts(scrap[:, 0:t * P], bank[:, 0:t * P], a, None, ALU.is_ge, ALU.add, wait=w,
                         accum_out=cnt[:, t, 0:1])
                got.append(e)
                w = e
            e = k.ts(scrap[:, t * P:T_X], bank[:, t * P:T_X], a, None, ALU.is_gt, ALU.add, wait=w,
                     accum_out=cnt[:, t, 1:2])
            e2 = k.stt(scrap[:, 0:P], bank[:, t * P:(t + 1) * P], a, consts["before"], ALU.is_equal, ALU.mult,
                       accum_out=cnt[:, t, 2:3], wait=[e, c_ready])
            got += [e, e2]
        k.bank_free[b] = got[-1]
        rank = k.cols(4)
        e = k.dve.put(lambda en: en.tensor_reduce(rank, cnt, AX.X, ALU.add), wait=got)
        hots, wgts = [], []
        for t in range(TC):
            hots.append(k.ts(hot[:, i, t * CAP:(t + 1) * CAP], consts["iota"][:, 0:CAP], rank[:, t:t + 1], None,
                             ALU.is_equal, wait=[e, c_ready, hot_free[i]]))
            wgts.append(k.ts(wgt[:, i, t * P:(t + 1) * P], consts["iota"], rank[:, t:t + 1],
                             aff[:, t, e_:e_ + 1], ALU.is_equal, ALU.mult, wait=[e, c_ready, wgt_free[i]]))
        return hots, wgts

    def gather(e_, hots, wgts):
        i = e_ % 2
        b, bank = k.take_bank()
        for dc in range(DC):
            for t in range(TC):
                end = k.mm(bank[:, dc * CAP:(dc + 1) * CAP], y[:, t, dc * P:(dc + 1) * P],
                           hot[:, i, t * CAP:(t + 1) * CAP], t == 0, t == TC - 1,
                           signal=t == TC - 1 and dc == DC - 1,
                           wait=[hots, y_ready, k.bank_free[b]] if t + dc == 0 else ())
        hot_free[i] = end
        x3 = xs[:, i, :].rearrange("p (d r) -> p d r", r=CAP)
        e = k.tt(x3, bank.rearrange("p (d r) -> p d r", r=CAP), A2.unsqueeze(2).to_broadcast([P, DC, CAP]),
                 ALU.mult, wait=[end, xs_free[i], B2_ready])
        k.bank_free[b] = e
        prepared[e_] = k.tt(x3, x3, B2.unsqueeze(2).to_broadcast([P, DC, CAP]), ALU.add, wait=e)
        b, bank = k.take_bank()
        for t in range(TC):
            end = k.tr(bank[:, t * P:(t + 1) * P], wgt[:, i, t * P:(t + 1) * P], signal=t == TC - 1,
                       wait=[wgts, k.bank_free[b]])
        wgt_free[i] = end
        wT_ready[e_] = k.bank_free[b] = k.copy(wT[:, e_ % 4, :], bank, wait=[end, wT_free[e_ % 4]], q=k.act)

    def scatter(pair, t):
        for half in range(2):
            rows = slice(half * CAP, (half + 1) * CAP)
            b, bank = k.take_bank()
            for n in range(2):
                for e_ in (2 * pair, 2 * pair + 1):
                    end = k.mm(bank[:, n * HALF:(n + 1) * HALF], wT[rows, e_ % 4, t * P:(t + 1) * P],
                               ye[rows, e_ % 4, n * HALF:(n + 1) * HALF], e_ % 2 == 0, e_ % 2 == 1,
                               signal=n + e_ % 2 == 2,
                               wait=[wT_ready[e_], ye_ready[e_], k.bank_free[b]])
            o = moe[:, t, :].rearrange("p (n h d) -> p n h d", n=2, h=2)[:, :, half, :]
            rows_in = bank.rearrange("p (n d) -> p n d", n=2)
            if pair == 0:
                e = k.copy(o, rows_in, wait=end)
            else:
                e = k.tt(o, o, rows_in, ALU.add, wait=[end, moe_done[(t, half)]])
            k.bank_free[b] = e
            moe_done[(t, half)] = e
        if t == TC - 1:
            for e_ in (2 * pair, 2 * pair + 1):
                wT_free[e_ % 4] = ye_free[e_ % 4] = end

    def weights_past(act_T, chunk0, slabs, w, ready):
        b, bank = k.take_bank()
        for n, (k0, n0) in enumerate(slabs):
            slot, slab, loaded = k.load_slab(w, k0, DC, n0, SLAB_N)
            for kc in range(DC):
                f = chunk0 + n * DC + kc
                for half in range(2):
                    end = k.mm(bank[half * CAP:(half + 1) * CAP, 0:HALF], act_T[:, f * CAP:(f + 1) * CAP],
                               slab[:, kc, half * HALF:(half + 1) * HALF], n + kc == 0,
                               n == len(slabs) - 1 and kc == DC - 1, signal=kc == DC - 1 and half == 1,
                               wait=[loaded, ready, k.bank_free[b]] if kc + half == 0 else ())
            k.slab_free[slot] = end
        return b, bank[:, 0:HALF], end

    ye_ready = {}
    gather(0, *choose(0))
    for e_ in range(N_EXP):
        i = e_ % 2
        hid_ready = []

        def to_hidden(s, h, have):
            b, bank = k.take_bank()
            for q in range(2):
                end = k.tr(bank[:, q * P:(q + 1) * P], h[:, q * P:(q + 1) * P], signal=q == 1,
                           wait=[have, k.bank_free[b]])
            h_free[s % 2] = end
            dst = hid[:, i, s * 4 * CAP:(s + 1) * 4 * CAP].rearrange("p (h q r) -> p q h r", h=2, q=2)
            src = bank[:, 0:2 * P].rearrange("p (q h r) -> p q h r", q=2, h=2)
            for q in range(2):
                e = k.copy(dst[:, q], src[:, q], wait=[end, hid_free[i]], q=k.act)
                hid_ready.append(e)
            k.bank_free[b] = e

        chosen = choose(e_ + 1) if e_ + 1 < N_EXP else None
        last = None
        for s in range(FF_E // SLAB_N):
            bg, gate, end_g = weights_past(xs[:, i], 0, [(0, s * SLAB_N)], A["w_gate_2"][0, e_], prepared[e_])
            bu, up, end_u = weights_past(xs[:, i], 0, [(0, s * SLAB_N)], A["w_up_2"][0, e_], prepared[e_])
            g, h = act_g[:, s % 2, :], tok_h[:, s % 2, :]
            e = k.activate(g, gate, ACT.Silu, wait=[end_g, g_free[s % 2]])
            k.bank_free[bg] = e
            e = k.tt(h, g, up, ALU.mult, wait=[e, end_u, h_free[s % 2]])
            k.bank_free[bu] = g_free[s % 2] = e
            if last is not None:
                to_hidden(*last)
            last = (s, h, e)
            if e_ % 2 == 0 and e_:
                scatter(e_ // 2 - 1, s)
        xs_free[i] = end_u
        if chosen:
            gather(e_ + 1, *chosen)
        to_hidden(*last)
        outs = []
        for n in range(2):
            b, bank, end = weights_past(hid[:, i], 0, [(0, n * SLAB_N), (DC * P, n * SLAB_N)],
                                        A["w_down_2"][0, e_], hid_ready)
            e = k.copy(ye[:, e_ % 4, n * HALF:(n + 1) * HALF], bank, wait=[end, ye_free[e_ % 4]], q=k.act)
            k.bank_free[b] = e
            outs.append(e)
        hid_free[i] = end
        ye_ready[e_] = outs
    for t in range(TC):
        scatter(N_EXP // 2 - 1, t)
    return moe, moe_done


def second_block(k, nc, A, C, out, x, x_ready, hT, y, gate_row, carve, new_phase, S):
    ready = S["cols_ready"]
    mod2 = S["mod2"]
    mod_ready = S["mod2_ready"]
    new_phase()
    TC = T_X // P
    consts_t = carve(6, P)
    u_tok = carve(TC, 3 * HYW)
    J, ones, tri, before = consts_t[:, 0, :], consts_t[:, 1, :], consts_t[:, 2:4, :], consts_t[:, 4, :]
    iota = consts_t[:, 5, :]
    s_c = k.counter("mixer_consts_loaded")
    k.load(J, C["flip"], s_c, q=k.pool)
    k.load(tri, C["tri"].rearrange("a p b -> p a b"), s_c, q=k.pool)
    k.load(before, C["before"], s_c, q=k.pool)
    k.load(iota, C["iota"].partition_broadcast(P), s_c, q=k.pool)
    after_u = 6 * P + TC * 3 * HYW
    qkT = carve(2 * MH, T_X)
    vpad = carve(TC * MH, 129)
    o_sig = carve(TC, 512)
    gates = carve(TC, 16)
    after_gates = after_u + sum(int(np.prod(v.shape[1:])) for v in (qkT, vpad, o_sig, gates))
    b_row = carve(1040)
    raw = carve(2, T_X)
    conv = carve(2, T_X)
    t_c = k.load(b_row, A["b_in_2"][0, 1024:2064].partition_broadcast(P), s_c, q=k.pool)
    e1 = k.dve.put(lambda e: e.memset(ones, 1.0))
    e2 = k.dve.put(lambda e: e.memset(vpad[:, :, 128:129], 1.0))
    consts = {"J": J, "ones": ones, "tri": tri, "before": before, "iota": iota, "ready": [t_c, e1]}
    gmix, e = S["scale_cols"](mod2, 0, 8, S["g_mixT"], [mod_ready, ready])
    normed = k.norm_to_features(x, TC, x_ready, gmix, mod2[:, 0:8, 0], [e, mod_ready], y, None, hT, None)
    state = {"raw_free": [None, None], "conv_free": [None, None], "n": 0}
    W_in = A["w_in_2"][0]

    qk_done = []

    def qk_evac(j, bank, end):
        i = state["n"] % 2
        state["n"] += 1
        r = raw[:, i, :]
        e0 = k.activate(r, bank, ACT.Identity, bias=S["b_qkT"][:, j:j + 1], wait=[end, state["raw_free"][i]])
        w = [S["conv_qk_wT"][:, 8 * n + j:8 * n + j + 1] for n in range(3)]
        e = short_conv(k, conv[:, i, :], r, w, S["conv_qk_bT"][:, j:j + 1], T_X, [e0, state["conv_free"][i]])
        state["raw_free"][i] = e
        e = k.activate(qkT[:, j, :], conv[:, i, :], ACT.Silu, wait=e)
        state["conv_free"][i] = e
        if j >= MH:
            e = k.ts(qkT[:, j, :], qkT[:, j, :], MD ** -0.5, None, ALU.mult, wait=e)
        qk_done.append(e)
        return e0

    k.feature_gemm(W_in, 0, 1024, hT, T_X, normed, qk_evac)
    vo_done = []

    def vo_evac(t, n0, nw, bank, end):
        row = b_row[:, n0 - 1024:n0 - 1024 + nw]
        if n0 == 1024:
            o = vpad[:, t * MH:(t + 1) * MH, 0:128]
            e = k.tt(o, bank.rearrange("p (h d) -> p h d", d=128), row.rearrange("p (h d) -> p h d", d=128),
                     ALU.add, wait=[end, t_c])
        else:
            e = k.tt(o_sig[:, t, :] if n0 == 1536 else gates[:, t, :], bank, row, ALU.add, wait=[end, t_c])
        vo_done.append(e)
        return e

    k.token_gemm(W_in, D, [(1024, 512), (1536, 512), (2048, 16)], hT, TC, normed, vo_evac)
    u_done = []

    def hx_evac(j, bank, end):
        i = state["n"] % 2
        state["n"] += 1
        r = raw[:, i, :]
        e0 = k.activate(r, bank, ACT.Identity, bias=S["b_hxT"][:, j:j + 1], wait=[end, state["raw_free"][i]])
        w = [S["conv_hy_wT"][:, 12 * n + j:12 * n + j + 1] for n in range(3)]
        e = short_conv(k, conv[:, i, :], r, w, S["conv_hy_bT"][:, j:j + 1], T_X, [e0, state["conv_free"][i]])
        state["raw_free"][i] = e
        hx_pending.append((j, i, e))
        if len(hx_pending) > 1:
            hx_transpose(*hx_pending.pop(0))
        return e0

    hx_pending = []

    def hx_transpose(j, i, have):
        b, bank = k.take_bank()
        for t in range(TC):
            end = k.tr(bank[:, t * P:(t + 1) * P], conv[:, i, t * P:(t + 1) * P], signal=t == TC - 1,
                       wait=[have, k.bank_free[b]])
        state["conv_free"][i] = end
        e = k.copy(u_tok[:, :, j * P:(j + 1) * P], bank.rearrange("p (t c) -> p t c", c=P), wait=end, q=k.act)
        k.bank_free[b] = e
        u_done.append(e)

    k.feature_gemm(W_in, 2064, 1536, hT, T_X, normed, hx_evac)
    while hx_pending:
        hx_transpose(*hx_pending.pop(0))
    k.barrier()
    S["rewind"](after_gates)
    h_done = mlstm(k, qkT, vpad, gates, None, None, hT, y, consts, [qk_done, vo_done, e2], carve)
    s_g = k.counter("mixer_gains_loaded")
    t_g = k.load(k.junk[:, 0:512], A["mlstm_norm_g_2"][0].partition_broadcast(P), s_g, q=k.pool)
    sg = [k.activate(o_sig[:, t, :], o_sig[:, t, :], ACT.Sigmoid, wait=vo_done) for t in range(TC)]
    m_done = []
    for t in range(TC):
        v = y[:, t, 0:512]
        e = group_rms(k, v, MH, MD, k.junk[:, 0:512], t_g, k.junk[:, 512:1024], h_done)
        m_done.append(k.tt(v, v, o_sig[:, t, :], ALU.mult, wait=[e, sg]))
    k.barrier()
    S["rewind"](after_u)
    hy_done = hyena(k, u_tok, A, C, S["cx"], hT, y, gate_row, carve, consts, u_done)
    k.barrier()
    s_g2 = k.counter("hyena_gain_loaded")
    t_g = k.load(k.junk[:, 0:512], A["hyena_norm_g_2"][0].partition_broadcast(P), s_g2, q=k.pool)
    for t in range(TC):
        m_done.append(group_rms(k, y[:, t, 512:1024], 4, P, k.junk[:, 0:512], t_g, k.junk[:, 512:1024], hy_done))
    tr_done = k.to_features(y, TC, m_done, hT, None)
    g_ready = k.columns_to_rows(mod2[:, 16:24, 0], 8, gate_row, mod_ready, None)
    tr_end = k.pe.last()
    res = []

    def out_evac(t, n0, nw, bank, end):
        e = k.tt(y[:, t, n0:n0 + nw], bank, gate_row[:, n0:n0 + nw], ALU.mult, wait=[end, tr_end, g_ready])
        res.append(k.tt(x[:, t, n0:n0 + nw], x[:, t, n0:n0 + nw], y[:, t, n0:n0 + nw], ALU.add, wait=e))
        return e

    k.token_gemm(A["w_out_2"][0], D, [(0, 512), (512, 512)], hT, TC, tr_done, out_evac)
    k.barrier()
    S["rewind"](6 * P)
    gffn, e = S["scale_cols"](mod2, 0, 32, S["g_ffnT"], [mod_ready, ready])
    normed = k.norm_to_features(x, TC, res, gffn, mod2[:, 24:32, 0], [e, mod_ready], y, k.pe.last(), hT,
                                k.pe.last())
    y_ready = [k.act.last(), k.dve.last()]
    moe, moe_done = experts(k, A, x, y, y_ready, hT, normed, gffn, mod2[:, 24:32, 0], [e, mod_ready], consts,
                            carve)
    g_ready = k.columns_to_rows(mod2[:, 40:48, 0], 8, gate_row, mod_ready, None)
    fin_row = y[:, 0, :]
    s_fin = k.counter("final_gain_loaded")
    t_fin = k.load(fin_row, A["g_final_2"].partition_broadcast(P), s_fin, wait=k.pe.last(), q=k.pool)
    s_out = k.counter("output_written")
    for t in range(TC):
        m = moe[:, t, :]
        e = k.tt(m, m, gate_row[:, :], ALU.mult, wait=[moe_done[(t, 0)], moe_done[(t, 1)], g_ready])
        e = k.tt(m, m, x[:, t, :], ALU.add, wait=e)
        sums = k.cols(1)
        e = k.activate(k.junk[:, :], m, ACT.Square, accum_out=sums, wait=e)
        rstd, have = k.inv_rms(sums, 1, D, e)
        e = k.stt(m, m, rstd, fin_row, ALU.mult, ALU.mult, wait=[have, t_fin])
        done = k.load(out[t * P:(t + 1) * P, :], m, s_out, wait=e)
    k.sp.hold(done)
    k.sp.hold(S["scratch_done"])


ROUND = 1.5 * 2.0 ** 23
TWO_PI = (6.28125, 0.0019350051879882812, 3.0199159819567e-07)


def tables():
    f = np.float32
    C = {"ident": np.eye(P, dtype=f), "flip": np.eye(P, dtype=f)[::-1].copy()}
    t = np.arange(T_X)
    pos = np.stack([t // GRID, t % GRID], -1).astype(f)
    inv = (f(10000.0) ** (-np.arange(16, dtype=f) / f(16))).astype(f)
    ang = (pos[:, :, None] * inv).astype(f)
    cos, sin = np.cos(ang).astype(f), np.sin(ang).astype(f)
    C["rope_cos"] = np.stack([cos, cos], 2).reshape(T_X, HD)
    C["rope_sin"] = np.stack([-sin, sin], 2).reshape(T_X, HD)
    q, c = np.arange(GRID)[:, None], np.arange(GRID)[None, :]
    start = np.clip(q - 8, 0, GRID - 16)
    valid = (c >= start) & (c < start + 16)
    off = np.clip(c - q, -15, 15) + 15
    hot = np.zeros((32, GRID, GRID), f)
    for d in range(RPB_COLS):
        hot[d] = (off == d) & valid
    hot[31] = np.where(valid, 0.0, NEG)
    C["neighbour_onehot"] = hot.reshape(32, GRID * GRID)
    i, j = np.arange(P)[:, None], np.arange(P)[None, :]
    C["window_masks"] = np.concatenate([np.where(j >= i, 0.0, NEG), np.where(j <= i, 0.0, NEG)], 1).astype(f)
    C["tri"] = np.stack([i <= j, i >= j]).astype(f)
    C["before"] = (j < i).astype(f)
    C["pick"] = (np.arange(P)[:, None] % 32 == np.arange(3)[None, :]).astype(f)
    C["iota"] = (np.arange(P) % CAP).astype(f)
    L = T_X
    tl = np.linspace(0.0, 1.0, L, dtype=f)[:, None]
    w = (f(2.0 * math.pi) * np.arange(L, dtype=f)[:, None] / f(L)).astype(f)
    bands = np.linspace(1e-4, 15, 16, dtype=f)[None, :]
    C["hyena_z"] = np.concatenate([tl, np.cos(bands * w), -np.sin(bands * w)], -1).astype(f).T.copy()
    cols = np.zeros((P, 6), f)
    cols[:, 0:4] = -tl.reshape(4, P).T
    cols[:, 4] = 2.0 / (2 * L)
    cols[0, 4] = 1.0 / (2 * L)
    C["hyena_cols"] = cols
    n = np.arange(L)
    ph = 2.0 * np.pi * ((n[:, None] * n[None, :]) % (2 * L)) / (2 * L)
    re, im = np.cos(ph), -np.sin(ph)
    alt = np.where(n % 2 == 0, 1.0, -1.0)
    C["dft"] = np.concatenate([re, im], 1).astype(f)
    are, aim = re[:, 0:P].copy(), im[:, 0:P].copy()
    are[:, 0] = alt
    aim[:, 0] = alt
    C["dft_alt_re"], C["dft_alt_im"] = are.astype(f), aim.astype(f)
    C["dft_alt_back"] = aim.T.astype(f).copy()
    return C


_INS = ["x", "c", "ctx", "c_ctx", "w_mod", "b_mod", "norm_g", "w_in", "w_out", "w_mlp_in", "w_mlp_out",
        "qk_norm_a", "diff_lambda", "diff_subln", "sink_c", "rpb_d", "c_2", "w_ada_2", "b_ada_2", "g_mix_2",
        "w_in_2", "b_in_2", "conv_qk_w_2", "conv_qk_b_2", "mlstm_norm_g_2", "conv_hy_w_2", "conv_hy_b_2",
        "hy_w1_2", "hy_b1_2", "hy_w2_2", "hy_b2_2", "hy_w3_2", "hy_freq_2", "hy_deltas_2", "hy_bias_2",
        "hyena_norm_g_2", "w_out_2", "g_ffn_2", "w_router_2", "w_gate_2", "w_up_2", "w_down_2", "g_final_2"]


def kernel(**inputs):
    import numpy as _np
    import concourse.bacc as _bacc
    from concourse import mybir as _mybir
    from concourse.bass_utils import run_bass_kernel_spmd as _run

    nc = _bacc.Bacc("TRN2", target_bir_lowering=False, num_devices=1)
    arrays, A, C = {}, {}, {}
    for group, named in ((A, {n: inputs[n] for n in _INS}), (C, tables())):
        for name, value in named.items():
            a = _np.ascontiguousarray(value)
            full = f"in_{name}" if group is A else f"table_{name}"
            arrays[full] = a
            group[name] = nc.dram_tensor(full, a.shape, _mybir.dt.from_np(a.dtype), kind="ExternalInput").ap()
    out = nc.dram_tensor("out", (T_X, D), F32, kind="ExternalOutput").ap()
    build(nc, A, C, out)
    r = _run(nc, [arrays], core_ids=[0])
    return r.results[0]["out"].reshape(1, T_X, D)
```

```python
import itertools
import math
from contextlib import ExitStack

import numpy as np

import concourse.bass as bass
from concourse import mybir

P = 128
F32 = mybir.dt.float32
ALU = mybir.AluOpType
ACT = mybir.ActivationFunctionType
AX = mybir.AxisListType

D = 1024
DC = D // P
T_X, T_C = 512, 256
TT_X, TT_C = T_X // P, T_C // P
S_ALL = T_C + T_X
GRID = 64
HD = 64
FF = 4 * D
FF_E = 2 * D
N_EXP = 16
CAP = 2 * T_X // N_EXP
MH, MD = 4, 128
HYW = 512
EPS = 1e-6
NEG = -1e30
LAM0 = 0.8 - 0.6 * math.exp(0.0)
SLAB_N = 512
N_SLABS = 3
N_BANKS = 8
BANK = 512
RPB_ROWS, RPB_COLS = 15, 31
QK_SCALE = HD ** -0.5
N_STATS = 1600
REGION = 20480


def flat(tokens):
    if not tokens:
        return []
    if isinstance(tokens, tuple):
        return [tokens]
    return [x for t in tokens for x in flat(t)]


class Queue:

    def __init__(self, sem):
        self.sem, self.count, self.items, self.waited = sem, 0, [], {}

    def hold(self, tokens):
        need = {}
        for sem, value in flat(tokens):
            need[sem] = max(need.get(sem, 0), value)
        for sem, value in need.items():
            if self.waited.get(sem, 0) < value:
                self.items.append((None, sem, value))
                self.waited[sem] = value

    def put(self, issue, wait=(), signal=True):
        self.hold(wait)
        self.items.append((issue, self.sem if signal else None, 1))
        if signal:
            self.count += 1
        return (self.sem, self.count) if signal else None

    def put_dma(self, issue, counter, wait=()):
        self.hold(wait)
        counter[1] += 16
        self.items.append((issue, counter[0], 16))
        return (counter[0], counter[1])

    def last(self):
        return (self.sem, self.count) if self.count else None

    def play(self, engine):
        for issue, sem, value in self.items:
            if issue is None:
                engine.wait_ge(sem, value)
            else:
                made = issue(engine)
                if sem is not None:
                    made.then_inc(sem, value)


class Core:

    def __init__(self, nc, ctx):
        self.nc, self.ctx = nc, ctx
        self.pe = Queue(self.semaphore("pe_done"))
        self.act = Queue(self.semaphore("act_done"))
        self.dve = Queue(self.semaphore("dve_done"))
        self.pool = Queue(self.semaphore("pool_done"))
        self.sp = Queue(self.semaphore("sp_done"))
        self.psum = ctx.enter_context(nc.psum_tensor("psum", [P, N_BANKS * BANK], F32))
        self.bank_free = [None] * N_BANKS
        self.next_bank = 0
        self.held_banks = set()
        self.background = None
        self.slab = [self.tile(f"slab{i}", [P, DC, SLAB_N]) for i in range(N_SLABS)]
        self.slab_loaded = [self.counter(f"slab_loaded{i}") for i in range(N_SLABS)]
        self.slab_free = [None] * N_SLABS
        self.next_slab = 0
        self.stats = self.tile("stats", [P, N_STATS])
        self.used_cols = 0
        self.turn = 0
        self.junk_free = None

    def semaphore(self, name):
        return self.ctx.enter_context(self.nc.semaphore(name))

    def counter(self, name):
        return [self.semaphore(name), 0]

    def tile(self, name, shape):
        return self.ctx.enter_context(self.nc.sbuf_tensor(name, shape, F32))

    def cols(self, n):
        at = self.used_cols
        self.used_cols += n
        assert self.used_cols <= N_STATS
        return self.stats[:, at:at + n]

    def take_bank(self):
        while self.next_bank in self.held_banks:
            self.next_bank = (self.next_bank + 1) % N_BANKS
        i = self.next_bank
        self.next_bank = (i + 1) % N_BANKS
        return i, self.psum[:, i * BANK:(i + 1) * BANK]

    def load_slab(self, src, k0, kc, n0, nw):
        i = self.next_slab
        self.next_slab = (i + 1) % N_SLABS
        view = self.slab[i][:, 0:kc, 0:nw]
        rows = src[k0:k0 + kc * P, n0:n0 + nw].rearrange("(c p) n -> p c n", p=P)
        loaded = self.sp.put_dma(lambda e, v=view, r=rows: e.dma_start(v, r), self.slab_loaded[i],
                                 wait=self.slab_free[i])
        return i, view, loaded

    def step_background(self):
        if self.background is not None:
            next(self.background, None)

    def finish(self, steps):
        for _ in steps:
            pass

    def barrier(self):
        ends = [q.last() for q in (self.pe, self.act, self.dve, self.pool)]
        for q in (self.act, self.dve, self.pool):
            q.hold(ends)

    def mm(self, out, lhsT, rhs, start, stop, wait=(), signal=False):
        return self.pe.put(lambda e: e.matmul(out, lhsT, rhs, start=start, stop=stop), wait, signal)

    def tr(self, out, in_, wait=(), signal=False):
        n = in_.shape[0]
        return self.pe.put(lambda e: e.transpose(out, in_, self.ident[0:n, 0:n]), wait, signal)

    def activate(self, out, in_, func, wait=(), **more):
        return self.act.put(lambda e: e.activation(out, in_, func, **more), wait)

    def tt(self, out, a, b, op, wait=(), q=None):
        return (q or self.dve).put(lambda e: e.tensor_tensor(out, a, b, op), wait)

    def ts(self, out, a, s1, s2, op0, op1=None, wait=(), q=None, accum_out=None):
        def issue(e):
            if accum_out is not None:
                return e.tensor_scalar(out, a, s1, s2, op0, op1, accum_out=accum_out)
            if op1 is None:
                return e.tensor_scalar(out, a, s1, None, op0)
            return e.tensor_scalar(out, a, s1, s2, op0, op1)
        return (q or self.dve).put(issue, wait)

    def stt(self, out, a, s, b, op0, op1, wait=(), **more):
        return self.dve.put(lambda e: e.scalar_tensor_tensor(out, a, s, b, op0, op1, **more), wait)

    def copy(self, out, in_, wait=(), q=None):
        q = q or self.dve
        if q is self.act:
            return q.put(lambda e: e.activation(out, in_, ACT.Copy), wait)
        return q.put(lambda e: e.tensor_copy(out, in_), wait)

    def copy_any(self, out, in_, wait=()):
        self.turn += 1
        return self.copy(out, in_, wait, self.act if self.turn % 2 else self.dve)

    def load(self, out, in_, counter, wait=(), q=None):
        return (q or self.sp).put_dma(lambda e: e.dma_start(out, in_), counter, wait)

    def feature_gemm(self, src, n0, n, act_T, T, ready, evacuate):
        done = 0
        while done < n:
            nw = min(SLAB_N, n - done)
            slot, slab, loaded = self.load_slab(src, 0, DC, n0 + done, nw)
            for j in range(-(-nw // P)):
                m = min(P, nw - j * P)
                b, bank = self.take_bank()
                for kc in range(DC):
                    end = self.mm(bank[0:m, 0:T], slab[:, kc, j * P:j * P + m], act_T[:, kc, 0:T],
                                  kc == 0, kc == DC - 1, signal=kc == DC - 1,
                                  wait=[loaded, ready, self.bank_free[b]] if kc == 0 else ())
                self.bank_free[b] = evacuate((done // P) + j, bank[0:m, 0:T], end)
            self.slab_free[slot] = end
            done += nw
            self.step_background()

    def token_gemm(self, src, K, ranges, act_T, tiles, ready, evacuate):
        kslabs = K // (DC * P)
        for n0, nw in ranges:
            banks = [self.take_bank() for _ in range(tiles)]
            self.held_banks = {b for b, _ in banks}
            for ks in range(kslabs):
                slot, slab, loaded = self.load_slab(src, ks * DC * P, DC, n0, nw)
                for t in range(tiles):
                    b, bank = banks[t]
                    for kc in range(DC):
                        end = self.mm(bank[:, 0:nw], act_T[:, ks * DC + kc, t * P:(t + 1) * P],
                                      slab[:, kc, :], ks + kc == 0, ks == kslabs - 1 and kc == DC - 1,
                                      signal=kc == DC - 1,
                                      wait=[loaded, ready, self.bank_free[b]] if kc == 0 else ())
                    if ks == kslabs - 1:
                        self.bank_free[b] = evacuate(t, n0, nw, bank[:, 0:nw], end)
                self.slab_free[slot] = end
                if ks == kslabs - 1:
                    self.held_banks = set()
                self.step_background()

    def inv_rms(self, sums, n, width, wait):
        mean, out = self.cols(n), self.cols(n)
        a = self.ts(mean, sums, 1.0 / width, EPS, ALU.mult, ALU.add, wait=wait)
        done = self.tt(out, mean, self.minus_half[:, 0:n], ALU.pow, wait=a, q=self.pool)
        return out, done

    def row_inv_rms(self, row, ready):
        sums = self.cols(1)
        self.junk_free = self.activate(self.junk[:, :], row, ACT.Square, wait=[ready, self.junk_free],
                                       accum_out=sums)
        return self.inv_rms(sums, 1, D, self.junk_free)

    def normed_tile(self, src, t, ready, y, y_free):
        rstd, have = self.row_inv_rms(src[:, t, :], ready)
        if t % 2:
            return self.activate(y[:, t, :], src[:, t, :], ACT.Copy, scale=rstd, wait=[have, y_free])
        return self.ts(y[:, t, :], src[:, t, :], rstd, None, ALU.mult, wait=[have, y_free])

    def modulated(self, y, tiles, scaled, a_col, b_col, col_ready, dst, dst_free):
        done = []
        for c in range(DC):
            b, bank = self.take_bank()
            for t in range(tiles):
                end = self.tr(bank[:, t * P:(t + 1) * P], y[:, t, c * P:(c + 1) * P], signal=t == tiles - 1,
                              wait=[scaled[t], self.bank_free[b]])
            view = dst[:, c, 0:tiles * P]
            if c % 2:
                e = self.activate(view, bank[:, 0:tiles * P], ACT.Identity, scale=a_col[:, c:c + 1],
                                  bias=b_col[:, c:c + 1], wait=[end, col_ready, dst_free])
            else:
                e = self.ts(view, bank[:, 0:tiles * P], a_col[:, c:c + 1], b_col[:, c:c + 1], ALU.mult,
                            ALU.add, wait=[end, col_ready, dst_free])
            self.bank_free[b] = e
            done.append(e)
        return done

    def to_features(self, src, tiles, ready, dst, dst_free, chunks=range(DC)):
        done = []
        for c in chunks:
            b, bank = self.take_bank()
            for t in range(tiles):
                end = self.tr(bank[:, t * P:(t + 1) * P], src[:, t, c * P:(c + 1) * P], signal=t == tiles - 1,
                              wait=[ready, self.bank_free[b]])
            e = self.copy_any(dst[:, c, 0:tiles * P], bank[:, 0:tiles * P], wait=[end, dst_free])
            self.bank_free[b] = e
            done.append(e)
        return done

    def columns_to_rows(self, col, n, dst, ready, dst_free):
        done = []
        for g in range(0, n, 4):
            m = min(4, n - g)
            b, bank = self.take_bank()
            for c in range(m):
                end = self.tr(bank[:, c * P:(c + 1) * P], col[:, g + c:g + c + 1].to_broadcast([P, P]),
                              signal=c == m - 1, wait=[ready, self.bank_free[b]])
            e = self.copy_any(dst[:, g * P:(g + m) * P], bank[:, 0:m * P], wait=[end, dst_free])
            self.bank_free[b] = e
            done.append(e)
        return done

    def gated_residual(self, x, t, m, m_ready, gate_row, gate_ready):
        rstd, have = self.row_inv_rms(m[:, t, :], m_ready)
        a = self.stt(m[:, t, :], m[:, t, :], rstd, gate_row, ALU.mult, ALU.mult, wait=[have, gate_ready])
        return self.tt(x[:, t, :], x[:, t, :], m[:, t, :], ALU.add, wait=a, q=self.dve if t % 2 else self.pool)


def attention(k, units, p_ring, pt_ring):
    ends = [k.bank_free[b] for b in range(N_BANKS)]
    pair_free = [[ends[0], ends[1]], [ends[2], ends[3]]]
    tr_free = [ends[4], ends[5]]
    out_free = [ends[6], ends[7]]
    p_free = [None] * 4
    pt_free = [None] * 4
    soft, moved = {}, {}

    def scores(i):
        u = units[i]
        S = u["S"]
        base = (i % 2) * 2 * BANK
        s = k.psum[:, base:base + S]
        for n, (p0, c0, w) in enumerate(u["segments"]):
            end = k.mm(s[:, p0:p0 + w], u["q"], u["k"][:, c0:c0 + w], True, True,
                       signal=n == len(u["segments"]) - 1,
                       wait=pair_free[i % 2] if n == 0 else ())
        for p0, w, add, have in u.get("bias", ()):
            end = k.tt(s[:, p0:p0 + w], s[:, p0:p0 + w], add, ALU.add, wait=[end, have])
        if "bias_free" in u:
            u["bias_free"](end)
        st = k.cols(4)
        mx, nb, rs, es = (st[:, j:j + 1] for j in range(4))
        a = k.dve.put(lambda e: e.reduce_max(mx, s, AX.X), wait=end)
        if u.get("sink") is not None:
            a = k.ts(mx, mx, QK_SCALE, u["sink"], ALU.mult, ALU.max, wait=[a, u["sink_ready"]])
            a = k.ts(nb, mx, -1.0, None, ALU.mult, wait=a)
        else:
            a = k.ts(nb, mx, -QK_SCALE, None, ALU.mult, wait=a)
        pv = p_ring[:, i % 4, 0:S]
        e1 = k.activate(pv, s, ACT.Exp, scale=QK_SCALE, bias=nb, accum_out=rs, wait=[a, p_free[i % 4]])
        pair_free[i % 2] = [e1]
        total = e1
        if u.get("sink") is not None:
            e2 = k.activate(es, u["sink"], ACT.Exp, bias=nb, wait=a)
            total = k.tt(rs, rs, es, ALU.add, wait=[e1, e2])
        soft[i] = (pv, rs, mx, total)

    def normalise(i):
        pv, rs, inv, total = soft[i]
        e = k.dve.put(lambda e: e.reciprocal(inv, rs), wait=total)
        u = units[i]
        if u["kind"] == "diff" and u["pos"] == 1:
            e = k.tt(inv, inv, u["neg_lam"], ALU.mult, wait=[e, u["lam_ready"]])
            e = k.stt(pv, pv, inv, soft[i - 1][0], ALU.mult, ALU.add, wait=[e, soft[i - 1][3]])
            p_free[(i - 1) % 4] = e
        else:
            e = k.ts(pv, pv, inv, None, ALU.mult, wait=e)
        soft[i] = (pv, rs, inv, e)

    def transposes(i):
        u = units[i]
        if u["kind"] == "diff" and u["pos"] == 0:
            return
        n = u["S"] // P
        lo, hi = pt_ring(i % 4)
        for c in range(n):
            end = k.tr(k.psum[:, 4 * BANK + c * P:4 * BANK + (c + 1) * P], p_ring[:, i % 4, c * P:(c + 1) * P],
                       signal=c == min(3, n - 1) or c == n - 1,
                       wait=[soft[i][3], tr_free[0]] if c == 0 else ([tr_free[1]] if c == 4 else ()))
            if c == min(3, n - 1):
                first = end
        p_free[i % 4] = end
        w = min(n, 4) * P
        e1 = k.copy(lo[:, 0:w], k.psum[:, 4 * BANK:4 * BANK + w], wait=[first, pt_free[i % 4]], q=k.act)
        tr_free[0] = e1
        e2 = None
        if n > 4:
            e2 = k.copy(hi[:, 0:(n - 4) * P], k.psum[:, 5 * BANK:5 * BANK + (n - 4) * P],
                        wait=[end, pt_free[i % 4]])
            tr_free[1] = e2
        moved[i] = ([e1, e2], [(lo if c < 4 else hi)[:, c % 4 * P:(c % 4 + 1) * P] for c in range(n)])

    def values(i):
        u = units[i]
        if u["pos"] == 0:
            return
        j = (i // 2) % 2
        o = k.psum[:, (6 + j) * BANK:(6 + j) * BANK + P]
        n = u["S"] // P
        for c in range(n):
            first, last = c == 0, c == n - 1
            if u["kind"] == "diff":
                end = k.mm(o, moved[i][1][c], u["v"][c], first, last, signal=last,
                           wait=[moved[i][0], out_free[j]] if first else ())
            else:
                for g in range(2):
                    have, pt = moved[i - 1 + g]
                    end = k.mm(o[g * HD:(g + 1) * HD, :], units[i - 1 + g]["v"][c], pt[c], first, last,
                               signal=last and g == 1, wait=[have, out_free[j]] if first else ())
        pt_free[i % 4] = end
        if u["kind"] != "diff":
            pt_free[(i - 1) % 4] = end
        out_free[j] = u["finish"](o, end)

    n = len(units)
    for i in range(n + 4):
        if i < n:
            scores(i)
        if 2 <= i < n + 2:
            normalise(i - 2)
        if 3 <= i < n + 3:
            transposes(i - 3)
        if i >= 4:
            values(i - 4)
    for b in range(4):
        k.bank_free[b] = pair_free[b // 2]
    k.bank_free[4], k.bank_free[5] = tr_free
    k.bank_free[6], k.bank_free[7] = out_free


def rope(k, out_view, src, cos, sin, heads, tmp, wait, tmp_free):
    w = heads * HD
    s3 = src.rearrange("p (h d) -> p h d", d=HD)
    t3 = tmp[:, 0:w].rearrange("p (h d) -> p h d", d=HD)
    u3 = tmp[:, 512:512 + w].rearrange("p (h d) -> p h d", d=HD)
    a = [k.tt(t3, s3, cos.unsqueeze(1).to_broadcast([P, heads, HD]), ALU.mult, wait=[wait, tmp_free])]
    for half in range(2):
        for axis in range(2):
            o = u3.rearrange("p h (a b f) -> p h a b f", a=2, b=2)[:, :, axis, half, :]
            i = s3.rearrange("p h (a b f) -> p h a b f", a=2, b=2)[:, :, axis, 1 - half, :]
            c = sin.rearrange("p (a b f) -> p a b f", a=2, b=2)[:, axis, half, :]
            a.append(k.tt(o, i, c.unsqueeze(1).to_broadcast([P, heads, 16]), ALU.mult, wait=[wait, tmp_free]))
    return k.tt(out_view, t3, u3, ALU.add, wait=a), a


def project_heads(k, layer, w_in, act_T, tiles, tok0, is_x, ready, V):
    QT, KT, VV = V["QT"], V["KT"], V["VV"]
    done = []
    normed = layer == 0
    stage_free = V["stage_free"]
    pending = []

    def stage():
        i = V["stage_next"] % 3
        V["stage_next"] += 1
        return i, V["stage"][:, i, :]

    def put_transposed(staged, nchunks, dst, chunk0, tok, have, slot):
        b, bank = k.take_bank()
        for c in range(nchunks):
            end = k.tr(bank[:, c * P:(c + 1) * P], staged[:, c * P:(c + 1) * P], signal=c == nchunks - 1,
                       wait=[have, k.bank_free[b]])
        e = k.copy_any(dst[:, chunk0:chunk0 + nchunks, tok:tok + P],
                       bank[:, 0:nchunks * P].rearrange("p (c t) -> p c t", t=P), wait=end)
        k.bank_free[b] = e
        stage_free[slot] = end
        done.append(e)

    def group(t, bank, w, roped, norm, which, twice, end, nchunks, dst, chunk0):
        heads = w // HD
        slot, staged = stage()
        staged = staged[:, 0:(2 if twice else 1) * w]
        tmp, tmp_free = V["tmp"], V["tmp_free"]
        tok = tok0 + t * P
        src, src_ready = bank[:, 0:w], end
        rel = None
        if norm:
            raw = V["raw"][:, 0:w]
            c = k.copy(raw, bank[:, 0:w], wait=[end, V["raw_free"]], q=k.act)
            sq = tmp[:, 0:w]
            a = k.tt(sq, raw, raw, ALU.mult, wait=[c, tmp_free])
            sums = k.cols(heads)
            a = k.dve.put(lambda e, o=sums, i=sq: e.tensor_reduce(o, i.rearrange("p (h d) -> p h d", d=HD),
                                                                 AX.X, ALU.add), wait=a)
            rstd, have = k.inv_rms(sums, heads, HD, a)
            rawh = raw.rearrange("p (h d) -> p h d", d=HD)
            src_ready = k.tt(rawh, rawh, rstd.unsqueeze(2).to_broadcast([P, heads, HD]), ALU.mult,
                             wait=have)
            src, rel, tmp_free = raw, c, src_ready
        shape_src = src.rearrange("p (h d) -> p h d", d=HD)
        if twice:
            view, second = (staged.rearrange("p (h r d) -> p h r d", r=2, d=HD)[:, :, i, :] for i in range(2))
        else:
            view = staged.rearrange("p (h d) -> p h d", d=HD)

        if roped:
            cos, sin = V["tables"][which]
            o, parts = rope(k, view, src, cos[:, t, :], sin[:, t, :], heads, tmp,
                            [src_ready, V["tables_ready"], stage_free[slot]], tmp_free)
            tmp_free = o
            outs = [o]
            rel = rel or outs
            V["tmp_free"] = tmp_free
        elif norm:
            g_row = V["qk_gain"][:, which * HD:(which + 1) * HD]
            outs = [k.tt(view, shape_src, g_row.unsqueeze(1).to_broadcast([P, heads, HD]), ALU.mult,
                         wait=[src_ready, V["gain_ready"], stage_free[slot]])]
        else:
            outs = [k.copy(view, shape_src, wait=[src_ready, stage_free[slot]], q=k.act)]
            rel = outs
        if norm:
            V["raw_free"] = outs
            if not roped:
                V["tmp_free"] = outs
        if twice:
            outs = outs + [k.copy(second, view, wait=outs, q=k.pool)]
        pending.append((staged, nchunks, dst, chunk0, tok, outs, slot))
        if len(pending) > 1:
            put_transposed(*pending.pop(0))
        return rel

    def evacuate(t, n0, nw, bank, end):
        sc = tok0 // P + t
        if n0 == 0:
            if not V["want_q"]:
                return None
            return group(t, bank, 512, is_x, normed, 0, False, end, 4, QT, 0)
        if n0 == 512:
            v = k.copy(VV[:, sc, 0:P], bank[:, P:2 * P], wait=end, q=k.act)
            done.append(v)
            return [group(t, bank, P, is_x, normed, 1, True, [end, v], 2, KT, 0), v]
        plain_rope = is_x and layer == 0
        if n0 == 768:
            return group(t, bank, 512, plain_rope, False, 2, False, end, 4, QT, 4)
        if n0 == 1280:
            return group(t, bank, 512, plain_rope, False, 2, False, end, 4, KT, 2)
        v = k.copy_any(VV[:, sc, P:P + 512], bank, wait=end)
        done.append(v)
        return v

    ranges = [(0, 512), (512, 256), (768, 512), (1280, 512), (1792, 512)]
    if not V["want_q"]:
        ranges = [ranges[1], ranges[3], ranges[4]]
    k.token_gemm(w_in, D, ranges, act_T, tiles, ready, evacuate)
    while pending:
        put_transposed(*pending.pop(0))
    return done


def mlp_up(k, w1, act_T, tiles, ready, uT):
    T = tiles * P
    hidden = []

    def up(j, bank, end):
        a = k.activate(uT[:, j, 0:T], bank, ACT.Relu, wait=end)
        hidden.append(k.tt(uT[:, j, 0:T], uT[:, j, 0:T], uT[:, j, 0:T], ALU.mult, wait=a))
        return a

    k.feature_gemm(w1, 0, FF, act_T, T, ready, up)
    return hidden


def project_residual(k, w, K, act_T, x, tiles, ready, m, m_free, gate_row, gate_ready, then):
    m_done = {t: [] for t in range(tiles)}

    def evacuate(t, n0, nw, bank, end):
        e = k.copy_any(m[:, t, n0:n0 + nw], bank, wait=[end, m_free])
        m_done[t].append(e)
        if n0 + nw == D:
            then(t, k.gated_residual(x, t, m, m_done[t], gate_row, gate_ready))
        return e

    k.token_gemm(w, K, [(0, 512), (512, 512)], act_T, tiles, ready, evacuate)


def build(nc, A, C, out):
    with ExitStack() as ctx:
        k = Core(nc, ctx)
        k.junk = k.tile("junk", [P, D])
        k.ident = k.tile("ident", [P, P])
        k.minus_half = k.tile("minus_half", [P, 16])
        x = k.tile("x", [P, TT_X, D])
        cx = k.tile("cx", [P, TT_C, D])
        hT = k.tile("hT", [P, DC, T_X])
        y = k.tile("y", [P, TT_X, D])
        gate_row = k.tile("gate_row", [P, D])
        colv = k.tile("colv", [P, 3 * P])
        region = k.tile("region", [P, REGION])
        s_in = k.counter("inputs_loaded")
        scratch = nc.dram_tensor("bias_tables", [8 * RPB_ROWS, GRID * GRID], F32, kind="Internal").ap()
        s_scr = k.counter("bias_tables_written")

        at = [0]

        def carve(*shape):
            n = int(np.prod(shape))
            v = region[:, at[0]:at[0] + n]
            at[0] += n
            assert at[0] <= REGION, at[0]
            if len(shape) == 2:
                v = v.rearrange("p (a b) -> p a b", b=shape[1])
            elif len(shape) == 3:
                v = v.rearrange("p (a b c) -> p a b c", b=shape[1], c=shape[2])
            return v

        def new_phase():
            k.barrier()
            at[0] = 0

        def rewind(to):
            at[0] = to

        k.load(k.ident[:, :], C["ident"], s_in)
        rows = [carve(P) for _ in range(3)]
        row_parts = [
            [(A["b_mod"].rearrange("l (r q) -> (l r) q", q=P), 96), (A["c"].rearrange("b (r q) -> (b r) q", q=P), 8),
             (A["c_ctx"].rearrange("(r q) -> r q", q=P), 8), (A["c_2"].rearrange("b (r q) -> (b r) q", q=P), 8),
             (A["conv_qk_b_2"].rearrange("b (r q) -> (b r) q", q=P), 8)],
            [(A["norm_g"].rearrange("l i (r q) -> (l i r) q", q=P), 64),
             (A["b_ada_2"].rearrange("b (r q) -> (b r) q", q=P), 48),
             (A["g_mix_2"].rearrange("b (r q) -> (b r) q", q=P), 8),
             (A["g_ffn_2"].rearrange("b (r q) -> (b r) q", q=P), 8)],
            [(A["conv_qk_w_2"].rearrange("b j (r q) -> (b j r) q", q=P), 24),
             (A["conv_hy_w_2"].rearrange("b j (r q) -> (b j r) q", q=P), 36),
             (A["conv_hy_b_2"].rearrange("b (r q) -> (b r) q", q=P), 12),
             (A["b_in_2"][0, 0:1024].rearrange("(r q) -> r q", q=P), 8),
             (A["b_in_2"][0, 2064:3600].rearrange("(r q) -> r q", q=P), 12)],
        ]
        row_counts = []
        for v, parts in zip(rows, row_parts):
            r = 0
            for src, n in parts:
                k.load(v[r:r + n, :], src, s_in)
                r += n
            row_counts.append(r)
        t_in = (s_in[0], s_in[1])
        s_x = k.counter("x_loaded")
        k.load(x[:, :, :], A["x"][0].rearrange("(t p) d -> p t d", p=P), s_x)
        t_x = k.load(cx[:, :, :], A["ctx"][0].rearrange("(t p) d -> p t d", p=P), s_x)
        t_half = k.dve.put(lambda e: e.memset(k.minus_half[:, :], -0.5))
        k.pool.hold(t_half)

        cols_ready = []
        for i, (v, n) in enumerate(zip(rows, row_counts)):
            b, bank = k.take_bank()
            end = k.tr(bank[:, 0:n], v[0:n, :], wait=t_in, signal=True)
            e = k.copy(colv[:, i * P:i * P + n], bank[:, 0:n], wait=end)
            k.bank_free[b] = e
            cols_ready.append(e)
        b_modT = colv[:, 0:96]
        cT = colv[:, 96:120]
        conv_qk_bT = colv[:, 120:128]
        norm_gT = colv[:, 128:192]
        b_adaT = colv[:, 192:240]
        g_mixT, g_ffnT = colv[:, 240:248], colv[:, 248:256]
        conv_qk_wT, conv_hy_wT = colv[:, 256:280], colv[:, 280:316]
        conv_hy_bT, b_qkT, b_hxT = colv[:, 316:328], colv[:, 328:336], colv[:, 336:348]

        vecs = k.tile("vecs", [P, DC, 32])
        pick = k.tile("pick", [P, 3])
        t_pick = k.load(pick[:, :], C["pick"], k.counter("pick_loaded"))
        e = k.dve.put(lambda e: e.memset(vecs[:, :, :], 0.0))
        a = [k.activate(vecs[:, :, i], cT[:, i * 8:(i + 1) * 8], ACT.Silu, wait=[e, cols_ready]) for i in range(2)]
        vecs_ready = a + [k.copy(vecs[:, :, 2], cT[:, 16:24], wait=[e, cols_ready])]
        mods = k.tile("mods", [P, 2, 48, 2])
        mod2 = k.tile("mod2", [P, 48, 1])

        mod_sums = k.tile("modulation_sums", [P, SLAB_N])
        sums_free = [None]

        def modulation(w, first, n, dst, bias, done):
            def to_columns(s, have):
                b, bank = k.take_bank()
                pv = bank[:, 0:4 * n].rearrange("p (c s) -> p c s", s=n)
                for j in range(4):
                    end = k.mm(pv[:, j, :], mod_sums[:, j * P:(j + 1) * P], pick[:, first:first + n],
                               True, True, signal=j == 3, wait=[have, t_pick, k.bank_free[b]] if j == 0 else ())
                sums_free[0] = end
                e = k.tt(dst[:, 4 * s:4 * s + 4, :], pv,
                         bias[:, 4 * s:4 * s + 4].unsqueeze(2).to_broadcast([P, 4, n]), ALU.add, wait=end)
                k.bank_free[b] = e
                done.append(e)

            last = None
            for s in range(12):
                slot, slab, loaded = k.load_slab(w, 0, DC, s * SLAB_N, SLAB_N)
                b, bank = k.take_bank()
                for kc in range(DC):
                    g = 32 * (kc % 4)
                    end = k.mm(bank[g:g + 32, :], vecs[:, kc, :], slab[:, kc, :], kc < 4, kc >= 4,
                               signal=kc == DC - 1,
                               wait=[loaded, vecs_ready, k.bank_free[b]] if kc == 0 else ())
                k.slab_free[slot] = end
                if last is not None:
                    to_columns(*last)
                e = k.activate(mod_sums[:, :], bank, ACT.Copy, wait=[end, sums_free[0]])
                k.bank_free[b] = e
                last = (s, e)
                yield
            to_columns(*last)

        mod_ready, mod2_ready = [[], []], []

        def scale_cols(mod, stream, chunk, gain, ready):
            dst = k.cols(8)
            e = k.stt(dst, mod[:, chunk:chunk + 8, stream], 1.0, gain, ALU.add, ALU.mult, wait=ready)
            return dst, e

        def gate_cols(mod, stream, chunk, gain, ready):
            dst = k.cols(8)
            return dst, k.tt(dst, mod[:, chunk:chunk + 8, stream], gain, ALU.mult, wait=ready)

        rpb_rows, rpb_T = carve(32), carve(120)
        onehot = carve(GRID * GRID)
        stage_b = carve(8, 512)
        s_rpb = k.counter("rpb_loaded")
        k.load(onehot[0:32, :], C["neighbour_onehot"], s_rpb, q=k.pool)
        k.load(rpb_rows[0:120, 0:RPB_COLS], A["rpb_d"][0].rearrange("h r c -> (h r) c"), s_rpb, q=k.pool)
        ones_col = k.dve.put(lambda e: e.memset(rpb_rows[0:120, 31:32], 1.0))
        t_rpb = (s_rpb[0], s_rpb[1])
        b, bank = k.take_bank()
        end = k.tr(bank[0:32, 0:120], rpb_rows[0:120, 0:32], wait=[t_rpb, ones_col, k.bank_free[b]], signal=True)
        have = k.copy(rpb_T[0:32, :], bank[0:32, 0:120], wait=end)
        k.bank_free[b] = have
        for j in range(8):
            b, bank = k.take_bank()
            end = k.mm(bank[0:120, :], rpb_T[0:32, :], onehot[0:32, j * 512:(j + 1) * 512], True, True,
                       wait=[have, k.bank_free[b]], signal=True)
            e = k.ts(stage_b[0:120, j, :], bank[0:120, :], 1.0 / QK_SCALE, None, ALU.mult, wait=end)
            k.bank_free[b] = e
            k.load(scratch[:, j * 512:(j + 1) * 512], stage_b[0:120, j, :], s_scr, wait=e, q=k.pool)
        t_scr = (s_scr[0], s_scr[1])
        first = modulation(A["w_mod"][0], 0, 2, mods[:, 0], b_modT[:, 0:48], mod_ready[0])
        for _ in range(2 * DC * P // SLAB_N + 1):
            next(first)
        for q in (k.pe, k.act, k.dve, k.pool):
            q.hold(t_scr)

        s_tab = k.counter("rope_loaded")
        x_ready, c_ready = t_x, t_x
        for layer in range(2):
            mod = mods[:, layer]
            ready = [mod_ready[layer], cols_ready]
            gains = [norm_gT[:, layer * 32 + i * 8:layer * 32 + i * 8 + 8] for i in range(4)]
            new_phase()
            V = {"QT": carve(8, S_ALL), "KT": carve(6, S_ALL), "VV": carve(6, 640), "stage": carve(3, 512),
                 "tmp": carve(1024), "raw": carve(512), "gained": carve(4 * TT_X, HD), "stage_free": [None] * 3, "stage_next": 0,
                 "tmp_free": None, "raw_free": None, "want_q": True}
            cos, sin = carve(TT_X, HD), carve(TT_X, HD)
            small = carve(640)
            late = region[:, 14592:14592 + 4096]
            p_ring = late[:, 0:4 * S_ALL].rearrange("p (a b) -> p a b", b=S_ALL)

            def pt_ring(i):
                return y[:, i, 0:512], late[:, 4 * S_ALL + i * 256:4 * S_ALL + (i + 1) * 256]
            k.load(cos, C["rope_cos"].rearrange("(t p) d -> p t d", p=P), s_tab, q=k.pool)
            k.load(sin, C["rope_sin"].rearrange("(t p) d -> p t d", p=P), s_tab, q=k.pool)
            if layer == 0:
                qk_gain, lam_rows, subln = small[:, 0:128], small[:, 128:384], small[:, 384:512]
                cg, sg = V["gained"][:, 0:2 * TT_X, :], V["gained"][:, 2 * TT_X:, :]
                k.load(qk_gain, A["qk_norm_a"][0].rearrange("i d -> (i d)").partition_broadcast(P), s_tab, q=k.pool)
                k.load(lam_rows, A["diff_lambda"][0].rearrange("i d -> (i d)").partition_broadcast(P), s_tab,
                       q=k.pool)
                t_tab = k.load(subln, A["diff_subln"][0].partition_broadcast(P), s_tab, q=k.pool)
                V["qk_gain"], V["gain_ready"] = qk_gain, t_tab
                made = []
                for w in range(2):
                    g = qk_gain[:, w * HD:(w + 1) * HD]
                    made.append(k.tt(cg[:, w * 4:w * 4 + 4, :], cos, g.unsqueeze(1).to_broadcast([P, 4, HD]),
                                     ALU.mult, wait=t_tab))
                    for h in range(2):
                        for ax in range(2):
                            o, i = ax * 32 + h * 16, ax * 32 + (1 - h) * 16
                            made.append(k.tt(sg[:, w * 4:w * 4 + 4, o:o + 16], sin[:, :, o:o + 16],
                                             g[:, i:i + 16].unsqueeze(1).to_broadcast([P, 4, 16]), ALU.mult,
                                             wait=t_tab))
                V["tables"] = [(cg[:, 0:4, :], sg[:, 0:4, :]), (cg[:, 4:8, :], sg[:, 4:8, :]), (cos, sin)]
                V["tables_ready"] = [made, t_tab]
                prod = small[:, 512:640]
                lr = lam_rows.rearrange("p (a b d) -> p a b d", a=2, b=2)
                e = k.tt(prod.rearrange("p (a d) -> p a d", d=HD), lr[:, :, 0, :], lr[:, :, 1, :], ALU.mult,
                         wait=t_tab)
                dots, neg_lam = k.cols(2), k.cols(1)
                e = k.dve.put(lambda en, o=dots, i=prod: en.tensor_reduce(
                    o, i.rearrange("p (a d) -> p a d", d=HD), AX.X, ALU.add), wait=e)
                e = k.activate(dots, dots, ACT.Exp, wait=e)
                e = k.tt(neg_lam, dots[:, 1:2], dots[:, 0:1], ALU.subtract, wait=e)
                lam_ready = k.ts(neg_lam, neg_lam, LAM0, None, ALU.subtract, wait=e)
                e = k.ts(subln, subln, 1.0 - LAM0, None, ALU.mult, wait=t_tab)
                subln_ready = e
            else:
                sink = small[:, 0:8]
                masks = small[:, 8:264]
                bias_ring = [y[:, i, 512:1024] for i in range(4)]
                k.load(masks, C["window_masks"], s_tab, q=k.pool)
                t_tab = k.load(sink, A["sink_c"][0].partition_broadcast(P), s_tab, q=k.pool)
                V["tables"] = [(cos, sin)] * 3
                V["tables_ready"] = t_tab
            if layer == 0:
                k.background = first
            for stream in (1, 0):
                src, tiles, src_ready = ((x, TT_X, x_ready), (cx, TT_C, c_ready))[stream]
                if layer == 1 and stream == 1:
                    normed = ctx_normed
                else:
                    if layer == 0:
                        free = k.pe.last()
                        scaled = [k.normed_tile(src, t, src_ready, y, free) for t in range(tiles)]
                    else:
                        scaled = x_scaled
                    A1, e1 = scale_cols(mod, stream, 8, gains[0], ready)
                    normed = k.modulated(y, tiles, scaled, A1, mod[:, 0:8, stream], [e1, ready], hT, k.pe.last())
                V["want_q"] = layer == 0 or stream == 0
                project_heads(k, layer, A["w_in"][layer], hT, tiles, 0 if stream else T_C,
                              stream == 0, normed, V)
            if layer == 0:
                k.background = None
                k.finish(first)
            QT, KT, VV = V["QT"], V["KT"], V["VV"]
            k.barrier()
            x_mixed, x_scaled = [], []
            for stream in ((1, 0) if layer == 0 else (0,)):
                tiles = TT_C if stream else TT_X
                mix_done = []
                units = []
                full = [(0, 0, 256)] if stream else [(0, 0, 512), (512, 512, 256)]
                S = T_C if stream else S_ALL
                qtok = 0 if stream else T_C

                def stacked(t, c):
                    def f(o, end):
                        e = k.copy_any(hT[:, c, t * P:(t + 1) * P], o, wait=end)
                        mix_done.append(e)
                        return e
                    return f

                def sublayer_norm(t):
                    o = y[:, t, 512:1024]
                    e = k.tt(k.junk[:, 0:512], o, o, ALU.mult, wait=[diff_done, k.junk_free, k.dve.last()])
                    sums = k.cols(4)
                    e = k.dve.put(lambda en: en.tensor_reduce(
                        sums, k.junk[:, 0:512].rearrange("p (h d) -> p h d", d=P), AX.X, ALU.add), wait=e)
                    k.junk_free = e
                    rstd, have = k.inv_rms(sums, 4, P, e)
                    o3 = o.rearrange("p (h d) -> p h d", d=P)
                    e = k.tt(o3, o3, rstd.unsqueeze(2).to_broadcast([P, 4, P]), ALU.mult, wait=have)
                    e = k.tt(o3, o3, subln.unsqueeze(1).to_broadcast([P, 4, P]), ALU.mult,
                             wait=[e, subln_ready])
                    diff_done.append(e)

                def diff_out(t, h):
                    def f(o, end):
                        e = k.copy_any(y[:, t, 512 + h * P:512 + (h + 1) * P], o, wait=end)
                        diff_done.append(e)
                        if h == 3:
                            sublayer_norm(t)
                        return e
                    return f

                diff_done = []
                bias_slot = itertools.cycle(range(4))
                s_bias = [k.counter(f"bias_loaded{layer}{stream}{i}") for i in range(4)] if layer == 1 else None
                for c, t, g in [(c, t, g) for c in range(4) for t in range(tiles) for g in range(2)]:
                        h, kv, pb = 2 * c + g, c // 2, 64 * g
                        q = QT[pb:pb + 64, c, qtok + t * P:qtok + (t + 1) * P]
                        u = {"q": q, "kind": "stack", "pos": g, "finish": stacked(t, c)}
                        if layer == 0:
                            u.update(S=S, segments=full, k=KT[pb:pb + 64, kv, :],
                                     v=[VV[:, c, kv * HD:(kv + 1) * HD] for c in range(S // P)])
                        else:
                            lo, hi = max(0, t - 1), min(TT_X - 1, t + 1)
                            n = hi - lo + 1
                            segs = [(0, 0, 256), (256, T_C + lo * P, min(n, 2) * P)]
                            if n == 3:
                                segs.append((512, T_C + (lo + 2) * P, P))
                            bias = []
                            if t > 0:
                                bias.append((256, P, masks[:, 0:P], t_tab))
                            if t < TT_X - 1:
                                bias.append((256 + (n - 1) * P, P, masks[:, P:2 * P], t_tab))
                            u.update(S=T_C + n * P, segments=segs, k=KT[pb:pb + 64, kv, :], bias=bias,
                                     sink=sink[:, h:h + 1], sink_ready=t_tab,
                                     v=[VV[:, c, kv * HD:(kv + 1) * HD] for c in [0, 1] + [2 + lo + i for i in range(n)]])
                        units.append(u)
                for t, c, g in [(t, c, g) for t in range(tiles) for c in range(4) for g in range(2)]:
                    h, pb = 2 * c + g, 64 * g
                    u = {"q": QT[pb:pb + 64, 4 + c, qtok + t * P:qtok + (t + 1) * P], "S": S, "segments": full,
                         "k": KT[pb:pb + 64, 2 + c, :], "pos": g}
                    if layer == 0:
                        u.update(kind="diff", finish=diff_out(t, c), neg_lam=neg_lam, lam_ready=lam_ready,
                                 v=[VV[:, s, P + c * P:P + (c + 1) * P] for s in range(S // P)])
                    else:
                        u.update(kind="stack", finish=stacked(t, 4 + c), load_bias=(next(bias_slot), h, t),
                                 v=[VV[:, s, P + h * HD:P + (h + 1) * HD] for s in range(S // P)])
                    units.append(u)
                if layer == 1:
                    free = [None] * 4

                    def with_bias(u):
                        i, h, t = u["load_bias"]

                        def start():
                            for rs in range(2):
                                r = 2 * t + rs
                                src = scratch[h * RPB_ROWS + 7 - r:h * RPB_ROWS + 15 - r, :].rearrange(
                                    "r (q c) -> q r c", c=GRID)
                                dst = bias_ring[i][64 * rs:64 * rs + 64, :].rearrange("p (r c) -> p r c", c=GRID)
                                tok = k.load(dst, src, s_bias[i], wait=[free[i], t_scr], q=k.pool)
                            return tok
                        have = start()
                        u["bias"] = [(256, 256, bias_ring[i][:, 0:256], have),
                                     (512, 256, bias_ring[i][:, 256:512], have)]

                        def release(tok):
                            free[i] = tok
                        u["bias_free"] = release
                    u_list = UnitStream(units, with_bias)
                else:
                    u_list = units
                attention(k, u_list, p_ring, pt_ring)
                if layer == 0:
                    mix_done += k.to_features(y, tiles, diff_done, hT, k.pe.last(), range(4, DC))
                g1, e = gate_cols(mod, stream, 16, gains[1], ready)
                g_ready = k.columns_to_rows(g1, 8, gate_row, e, [k.dve.last(), k.pool.last()])
                tr_end = k.pe.last()
                if stream:
                    c_mixed = []
                    project_residual(k, A["w_out"][layer], D, hT, cx, tiles, mix_done, y, tr_end, gate_row[:, :],
                                     g_ready, lambda t, e: c_mixed.append(e))
                    k.barrier()
            new_phase()
            uT = carve(FF // P, T_X)
            y2 = carve(TT_X, D)

            def x_done(t, e):
                x_mixed.append(e)
                if layer == 1:
                    x_scaled.append(k.normed_tile(x, t, e, y, None))

            if layer == 0:
                c_scaled = [k.normed_tile(cx, t, c_mixed[t], y2, None) for t in range(TT_C)]
            project_residual(k, A["w_out"][layer], D, hT, x, TT_X, mix_done, y, tr_end, gate_row[:, :], g_ready,
                             x_done)
            if layer == 0:
                A2, e1 = scale_cols(mod, 1, 32, gains[2], ready)
                normed = k.modulated(y2, TT_C, c_scaled, A2, mod[:, 24:32, 1], [e1, ready], hT, k.pe.last())
                free = k.pe.last()
                x_scaled = [k.normed_tile(x, t, x_mixed[t], y2, free) for t in range(TT_X)]
                g2, e = gate_cols(mod, 1, 40, gains[3], ready)
                g_ready = k.columns_to_rows(g2, 8, gate_row, e, [k.dve.last(), k.pool.last()])
                later = modulation(A["w_mod"][1], 0, 2, mods[:, 1], b_modT[:, 48:96], mod_ready[1])
                k.background = later
                hidden = mlp_up(k, A["w_mlp_in"][layer], hT, TT_C, normed, uT)
                A2, e1 = scale_cols(mod, 0, 32, gains[2], ready)
                normed = k.modulated(y2, TT_X, x_scaled, A2, mod[:, 24:32, 0], [e1, ready], hT, k.pe.last())
                c_out = []
                project_residual(k, A["w_mlp_out"][layer], FF, uT, cx, TT_C, hidden, y, [x_mixed, k.pe.last()],
                                 gate_row[:, :], g_ready, lambda t, e: c_out.append(e))
                k.background = None
                k.finish(later)
            else:
                A2, e1 = scale_cols(mod, 0, 32, gains[2], ready)
                normed = k.modulated(y, TT_X, x_scaled, A2, mod[:, 24:32, 0], [e1, ready], hT, k.pe.last())
            g2, e = gate_cols(mod, 0, 40, gains[3], ready)
            g_ready = k.columns_to_rows(g2, 8, gate_row, e, [k.dve.last(), k.pool.last()])
            if layer == 0:
                later = modulation(A["w_ada_2"][0], 2, 1, mod2[:, :, :], b_adaT, mod2_ready)
                k.background = later
            y_free = k.pe.last()
            hidden = mlp_up(k, A["w_mlp_in"][layer], hT, TT_X, normed, uT)
            if layer == 0:
                c_scaled = [k.normed_tile(cx, t, c_out[t], y2, y_free) for t in range(TT_C)]
                nxt = [mod_ready[1], cols_ready]
                A1, e1 = scale_cols(mods[:, 1], 1, 8, norm_gT[:, 32:40], nxt)
                ctx_normed = k.modulated(y2, TT_C, c_scaled, A1, mods[:, 1, 0:8, 1], [e1, nxt], hT, k.pe.last())
            x_out, x_scaled = [], []

            def x_through(t, e):
                x_out.append(e)
                x_scaled.append(k.normed_tile(x, t, e, y, None))

            project_residual(k, A["w_mlp_out"][layer], FF, uT, x, TT_X, hidden, y, y_free, gate_row[:, :], g_ready,
                             x_through)
            if layer == 0:
                k.background = None
                k.finish(later)

        second_block(k, A, C, out, x, hT, y, gate_row, carve, new_phase,
                     dict(cT=cT, cols_ready=cols_ready, b_adaT=b_adaT, g_mixT=g_mixT, g_ffnT=g_ffnT,
                          conv_qk_wT=conv_qk_wT, conv_qk_bT=conv_qk_bT, conv_hy_wT=conv_hy_wT,
                          conv_hy_bT=conv_hy_bT, b_qkT=b_qkT, b_hxT=b_hxT, mod2=mod2, mod2_ready=mod2_ready,
                          scale_cols=scale_cols, rewind=rewind, cx=cx, scratch_done=t_scr, mod_sums=mod_sums, x_scaled=x_scaled))

        with nc.Block() as block:
            @block.sync
            def _(e):
                k.sp.play(e)

            @block.tensor
            def _(e):
                k.pe.play(e)

            @block.scalar
            def _(e):
                k.act.play(e)

            @block.vector
            def _(e):
                k.dve.play(e)

            @block.gpsimd
            def _(e):
                k.pool.play(e)


class UnitStream:

    def __init__(self, units, prepare):
        self.units, self.prepare, self.made = units, prepare, set()

    def __len__(self):
        return len(self.units)

    def __getitem__(self, i):
        if i not in self.made:
            self.made.add(i)
            if "load_bias" in self.units[i]:
                self.prepare(self.units[i])
        return self.units[i]


def short_conv(k, out, raw, w, b, T, wait):
    e = k.ts(out, raw, w[1], b, ALU.mult, ALU.add, wait=wait)
    e = k.stt(out[:, 1:T], raw[:, 0:T - 1], w[0], out[:, 1:T], ALU.mult, ALU.add, wait=e)
    return k.stt(out[:, 0:T - 1], raw[:, 1:T], w[2], out[:, 0:T - 1], ALU.mult, ALU.add, wait=e)


def group_rms(k, view, groups, width, gain, gain_ready, tmp, ready):
    n = groups * width
    e = k.tt(tmp[:, 0:n], view, view, ALU.mult, wait=[ready, k.dve.last()])
    sums = k.cols(groups)
    e = k.dve.put(lambda en: en.tensor_reduce(sums, tmp[:, 0:n].rearrange("p (h d) -> p h d", d=width),
                                              AX.X, ALU.add), wait=e)
    rstd, have = k.inv_rms(sums, groups, width, e)
    v3 = view.rearrange("p (h d) -> p h d", d=width)
    e = k.tt(v3, v3, rstd.unsqueeze(2).to_broadcast([P, groups, width]), ALU.mult, wait=have)
    return k.tt(view, view, gain, ALU.mult, wait=[e, gain_ready])


def gate_rows(k, qkT, gates, y, cx, gsel, sm, consts, ready, G):
    J, c_ready = consts["J"], consts["ready"]
    NC_ = T_X // P
    R = 2 * MH
    k_tok = y[:, :, MH * MD:2 * MH * MD]
    kt_done = []
    for c in range(NC_):
        b, bank = k.take_bank()
        for h in range(MH):
            end = k.tr(bank[:, h * P:(h + 1) * P], qkT[:, MH + h, c * P:(c + 1) * P], signal=h == MH - 1,
                       wait=[ready, k.bank_free[b]])
        e = k.copy_any(k_tok[:, c, :], bank, wait=end)
        k.bank_free[b] = e
        kt_done.append(e)
    yield
    g4 = gsel.rearrange("p (c n d) r -> p c n d r", n=2, d=2)
    e = k.dve.put(lambda en: en.memset(gsel, 0.0))
    sel = []
    for kind in range(2):
        for d in range(2):
            src = gates[:, :, (2 * d + kind) * 4:(2 * d + kind) * 4 + 4]
            sel.append(k.copy(g4[:, :, kind, d, d * 4:d * 4 + 4], src, wait=[e, ready]))
    row = [cx[0:R, i // 2, i % 2 * T_X:(i % 2 + 1) * T_X] for i in range(4)]
    row += [y[0:R, i, 0:T_X] for i in range(4)]
    W, LF, B, CM, M, E_END, E_INT, E_NM = row
    raw_rows = []
    for kind in range(2):
        b, bank = k.take_bank()
        for c in range(NC_):
            k.mm(bank[0:R, c * P:(c + 1) * P], g4[:, c, kind, 0, :], k.ident[:, :], True, False,
                 wait=[sel, k.bank_free[b], c_ready])
            end = k.mm(bank[0:R, c * P:(c + 1) * P], g4[:, NC_ - 1 - c, kind, 1, :], J, False, True,
                       signal=c == NC_ - 1)
        e = k.copy(row[kind], bank[0:R, :], wait=end)
        k.bank_free[b] = e
        raw_rows.append(e)
    yield
    e = k.stt(B, LF, -1.0, LF, ALU.mult, ALU.max, wait=raw_rows[1])
    e = k.activate(B, B, ACT.Exp, scale=-1.0, wait=e)
    e = k.activate(B, B, ACT.Ln, bias=1.0, wait=e)
    lf = k.stt(LF, LF, 0.0, B, ALU.min, ALU.subtract, wait=e)
    yield
    one = k.dve.put(lambda en: en.memset(E_END, 1.0))
    sc = []
    for c in range(NC_):
        s = slice(c * P, (c + 1) * P)
        sc.append(k.dve.put(lambda en, s=s: en.tensor_tensor_scan(B[:, s], E_END[:, s], LF[:, s], 0.0, ALU.mult,
                                                                  ALU.add), wait=[lf, one]))
    e = k.tt(W, W, B, ALU.subtract, wait=[sc, raw_rows[0]])
    yield
    cm = []
    for c in range(NC_):
        s = slice(c * P, (c + 1) * P)
        cm.append(k.dve.put(lambda en, s=s: en.tensor_tensor_scan(CM[:, s], W[:, s], W[:, s], -3.0e38, ALU.max,
                                                                  ALU.max), wait=e))
    yield
    sm = sm[0:R, :]
    m_in, g_m, a_c, spl, ncml = sm[:, 0:5], sm[:, 8:12], sm[:, 12:16], sm[:, 16:24], sm[:, 24:28]
    last = slice(P - 1, T_X, P)
    e0 = k.dve.put(lambda en: en.memset(m_in[:, 0:1], NEG))
    e1 = k.tt(a_c, B[:, last], CM[:, last], ALU.add, wait=cm)
    ncml_ready = k.ts(ncml, CM[:, last], -1.0, None, ALU.mult, wait=cm)
    e = [e0, e1]
    for c in range(NC_):
        e = k.tt(g_m[:, c:c + 1], B[:, c * P + P - 1:c * P + P], m_in[:, c:c + 1], ALU.add, wait=e)
        e = k.tt(m_in[:, c + 1:c + 2], g_m[:, c:c + 1], a_c[:, c:c + 1], ALU.max, wait=e)
    e1 = k.tt(spl[:, 0:4], g_m, m_in[:, 1:5], ALU.subtract, wait=e)
    e2 = k.tt(spl[:, 4:8], a_c, m_in[:, 1:5], ALU.subtract, wait=e)
    spl_ready = k.activate(spl, spl, ACT.Exp, wait=[e1, e2])
    yield
    m_done, q_done = [], []
    for c in range(NC_):
        s = slice(c * P, (c + 1) * P)
        m_done.append(k.ts(M[:, s], CM[:, s], m_in[:, c:c + 1], None, ALU.max, wait=e))
        q_done.append(k.activate(E_END[:, s], W[:, s], ACT.Exp, bias=ncml[:, c:c + 1], wait=[ncml_ready, sc]))
        q_done.append(k.activate(E_INT[:, s], M[:, s], ACT.Exp, scale=-1.0, bias=m_in[:, c:c + 1],
                                 wait=m_done[-1]))
    e = k.tt(E_NM, B, M, ALU.add, wait=m_done)
    q_done.append(k.activate(E_NM, E_NM, ACT.Exp, scale=-1.0, wait=e))
    G.update(rows=[W, M, E_END, E_INT, E_NM], spl=spl, spl_ready=spl_ready, k_tok=k_tok, kt_done=kt_done,
             done=[q_done, m_done])


def mlstm(k, qkT, vpad, G, cx, y, consts, ready, carve, head_done):
    J, ones, masks = consts["J"], consts["ones"], consts["tri"]
    c_ready = consts["ready"]
    NC_ = T_X // P
    R = 2 * MH
    spl, spl_ready, k_tok, kt_done = G["spl"], G["spl_ready"], G["k_tok"], G["kt_done"]
    Q = G["rows"]
    nq = len(Q)
    craw, colsq = carve(NC_ * nq, R), carve(NC_ * nq, R)
    b, bank = k.take_bank()
    for c in range(NC_):
        for i, q in enumerate(Q):
            end = k.tr(bank[:, (c * nq + i) * R:(c * nq + i + 1) * R], q[:, c * P:(c + 1) * P],
                       wait=[G["done"], k.bank_free[b]], signal=True)
    n = NC_ * nq * R
    e1 = k.copy(craw, bank[:, 0:n].rearrange("p (n r) -> p n r", r=R), wait=end)
    k.bank_free[b] = e1
    e2 = k.copy(colsq[:, :, 0:4], craw[:, :, 0:4], wait=e1)
    b, bank = k.take_bank()
    end = k.mm(bank[:, 0:n // 2].rearrange("p (n r) -> p n r", r=4), J, craw[:, :, 4:8], True, True,
               wait=[e1, k.bank_free[b], c_ready], signal=True)
    cols_done = [e2]
    for c in range(NC_):
        o = (NC_ - 1 - c) * nq
        cols_done.append(k.copy(colsq[:, o:o + nq, 4:8],
                                bank[:, c * nq * 4:(c + 1) * nq * 4].rearrange("p (n r) -> p n r", r=4), wait=end))
    k.bank_free[b] = cols_done[-1]

    def col(c, q, r):
        return colsq[:, c * nq + q, r:r + 1]

    diag = carve(8, 8)[0:R, :, :]
    e = k.tt(diag, spl.unsqueeze(2).to_broadcast([R, 8, 8]),
             k.ident[0:R, 0:R].unsqueeze(1).to_broadcast([R, 8, 8]), ALU.mult, wait=spl_ready)
    sB = carve(8, 8)
    b, bank = k.take_bank()
    end = k.mm(bank[:, 0:64].rearrange("p (n r) -> p n r", r=8), ones[0:R, :], diag, True, True,
               wait=[e, k.bank_free[b], c_ready], signal=True)
    sB_ready = k.copy(sB, bank[:, 0:64].rearrange("p (n r) -> p n r", r=8), wait=end)
    k.bank_free[b] = sB_ready
    DT = carve(2, T_X)
    PT = carve(2, T_X)
    ve = carve(2, NC_ * 129)
    st = carve(2, 3 * 129)
    tmp = carve(2, 129)
    free = [None, None]
    num_free = [None, None]
    y_tok = {}
    tmp_free = [None, None]
    made = {}

    def states(r):
        d, h, i = r // MH, r % MH, r % 2
        b, bank = k.take_bank()
        for c in range(NC_):
            end = k.tr(bank[:, c * P:(c + 1) * P], col(c, 1, r).to_broadcast([P, P]), signal=c == NC_ - 1,
                       wait=[cols_done, k.bank_free[b]])
        e = []
        for c in range(NC_):
            e.append(k.ts(DT[:, i, c * P:(c + 1) * P], bank[:, c * P:(c + 1) * P], col(c, 0, r), 0.0,
                          ALU.subtract, ALU.max, wait=[end, free[i]]))
        k.bank_free[b] = e[-1]
        e = k.activate(DT[:, i, :], DT[:, i, :], ACT.Exp, scale=-1.0, wait=e)
        d3 = DT[:, i, :].rearrange("p (c t) -> p c t", t=P)
        dm = k.tt(d3, d3, masks[:, d, :].unsqueeze(1).to_broadcast([P, NC_, P]), ALU.mult, wait=[e, c_ready],
                  q=k.pool)
        b, bank = k.take_bank()
        for c in range(NC_):
            s = slice(c * P, (c + 1) * P)
            end = k.mm(bank[:, s], qkT[:, MH + h, s], qkT[:, h, s], True, True, signal=c == NC_ - 1,
                       wait=[ready, k.bank_free[b]])
        pt_ready = k.tt(PT[:, i, :], bank, DT[:, i, :], ALU.mult, wait=[end, dm, free[i]])
        k.bank_free[b] = pt_ready
        order = list(range(NC_)) if d == 0 else list(range(NC_ - 1, -1, -1))
        v3 = ve[:, i, :].rearrange("p (c n) -> p c n", n=129)
        s3 = st[:, i, :].rearrange("p (c n) -> p c n", n=129)
        state_ready = None
        have = {}
        for n_, c in enumerate(order):
            if n_ < NC_ - 1:
                a = k.activate(v3[:, c, :], vpad[:, c * MH + h, :], ACT.Copy, scale=col(c, 2, r),
                               wait=[cols_done, ready, free[i]])
                b, bank = k.take_bank()
                end = k.mm(bank[:, 0:129], k_tok[:, c, h * P:(h + 1) * P], v3[:, c, :], True, True,
                           wait=[a, kt_done, k.bank_free[b]], signal=True)
                loc = k.activate(s3[:, n_, :], bank[:, 0:129], ACT.Copy, scale=sB[:, 4 + n_, r:r + 1],
                                 wait=[end, sB_ready, free[i]])
                k.bank_free[b] = loc
                if n_ == 0:
                    nxt = loc
                else:
                    nxt = k.stt(s3[:, n_, :], s3[:, n_ - 1, :], sB[:, n_, r:r + 1], s3[:, n_, :], ALU.mult,
                                ALU.add, wait=[loc, state_ready])
                state_ready = nxt
                have[n_ + 1] = nxt
        made[r] = (pt_ready, have)

    def outputs(r):
        d, h, i = r // MH, r % MH, r % 2
        pt_ready, have = made[r]
        order = list(range(NC_)) if d == 0 else list(range(NC_ - 1, -1, -1))
        s3 = st[:, i, :].rearrange("p (c n) -> p c n", n=129)
        num = cx[:, i, 0:NC_ * 129].rearrange("p (c n) -> p c n", n=129)
        got = []
        for n_, c in enumerate(order):
            b, bank = k.take_bank()
            end = k.mm(bank[:, 0:129], PT[:, i, c * P:(c + 1) * P], vpad[:, c * MH + h, :], True, True,
                       wait=[pt_ready, k.bank_free[b]], signal=True)
            if n_ > 0:
                end = k.mm(bank[:, 256:385], qkT[:, h, c * P:(c + 1) * P], s3[:, n_ - 1, :], True, True,
                           wait=have[n_], signal=True)
                e = k.activate(tmp[:, c % 2, :], bank[:, 256:385], ACT.Copy, scale=col(c, 3, r),
                               wait=[end, tmp_free[c % 2]])
                e = k.tt(num[:, c, :], bank[:, 0:129], tmp[:, c % 2, :], ALU.add, wait=[e, num_free[i]])
                tmp_free[c % 2] = e
            else:
                e = k.copy(num[:, c, :], bank[:, 0:129], wait=[end, num_free[i]])
            k.bank_free[b] = e
            got.append(e)
        free[i] = [got, end]
        den = k.cols(2 * NC_)
        floor = colsq.rearrange("p (c q) r -> p c q r", q=nq)[:, :, 4, r]
        e = k.tt(den[:, 0:NC_], num[:, :, 128], floor, ALU.max, wait=got)
        e = k.stt(den[:, 0:NC_], num[:, :, 128], -1.0, den[:, 0:NC_], ALU.mult, ALU.max, wait=e)
        ratio = k.dve.put(lambda en: en.reciprocal(den[:, NC_:], den[:, 0:NC_]), wait=e)
        for c in range(NC_):
            o = y[:, c, h * P:(h + 1) * P]
            if d == 0:
                e = k.activate(o, num[:, c, 0:128], ACT.Copy, scale=den[:, NC_ + c:NC_ + c + 1], wait=ratio)
            else:
                e = k.stt(o, num[:, c, 0:128], den[:, NC_ + c:NC_ + c + 1], o, ALU.mult, ALU.add,
                          wait=[ratio, y_tok[(c, h)]])
            y_tok[(c, h)] = e
        num_free[i] = [y_tok[(c, h)] for c in range(NC_)]

    states(0)
    for r in range(R):
        if r + 1 < R:
            states(r + 1)
        outputs(r)
        if r >= MH:
            head_done(r - MH, [y_tok[(c, r - MH)] for c in range(NC_)])


def filter_network(k, A, C, z0, arg, turns, hid1, hid2, free, F):
    s_f = k.counter("filter_loaded")
    small, tcol = k.cols(136), k.cols(8)
    z0, w1, w2, fcol = z0[0:33, :], small[0:33, 0:64], small[0:64, 64:128], small[0:64, 128:136]
    arg, turns, hid1, hid2 = arg[0:64, :], turns[0:64, :], hid1[0:64, :], hid2[0:64, :]
    k.load(z0, C["hyena_z"], s_f, wait=free, q=k.pool)
    k.load(w1, A["hy_w1_2"][0], s_f, q=k.pool)
    k.load(w2, A["hy_w2_2"][0], s_f, q=k.pool)
    for i, n in enumerate(("hy_b1_2", "hy_b2_2", "hy_freq_2")):
        k.load(fcol[:, i:i + 1], A[n][0].rearrange("(p a) -> p a", a=1), s_f, q=k.pool)
    t_f = k.load(tcol[:, 0:6], C["hyena_cols"], s_f, q=k.pool)

    def sine_layer(w, z, bias, out, wait):
        b, bank = k.take_bank()
        end = k.mm(bank[0:64, :], w, z, True, True, wait=[wait, t_f, k.bank_free[b]], signal=True)
        e = k.ts(arg, bank[0:64, :], bias, fcol[:, 2:3], ALU.add, ALU.mult, wait=end)
        k.bank_free[b] = e
        e = k.ts(turns, arg, 1.0 / (2.0 * math.pi), ROUND, ALU.mult, ALU.add, wait=e)
        e = k.ts(turns, turns, ROUND, None, ALU.subtract, wait=e)
        for part in TWO_PI:
            e = k.stt(arg, turns, -part, arg, ALU.mult, ALU.add, wait=e)
        e = k.ts(arg, arg, 3.1415925, -3.1415925, ALU.min, ALU.max, wait=e)
        return k.activate(out, arg, ACT.Sin, wait=e)

    e = sine_layer(w1, z0, fcol[:, 0:1], hid1, free)
    yield
    hid_ready = sine_layer(w2, hid1, fcol[:, 1:2], hid2, e)
    F.update(hidden=hid2, ready=[hid_ready, t_f], columns=tcol)


def hyena(k, u_tok, A, C, F, cx, hT, y, gate_row, carve, ready, then):
    N_F = 2 * T_X
    TC = T_X // P
    dft, alt_re, alt_im, alt_g = carve(TC, N_F), carve(TC, P), carve(TC, P), carve(T_X)
    U = carve(2 * TC, HYW)
    Kr, Ki, KrB, bias_row = carve(TC, HYW), y[:, :, HYW:2 * HYW], carve(HYW), carve(HYW)
    s_bias = k.counter("hyena_bias_loaded")
    s_dft = k.counter("dft_loaded")
    tp = "(t p) f -> p t f"
    free = [q.last() for q in (k.pe, k.act, k.dve, k.pool)]
    deltas = cx[:, :, :].rearrange("p t d -> p (t d)")
    t_f = k.load(deltas, A["hy_deltas_2"][0].partition_broadcast(P), k.counter("deltas_loaded"), wait=free)
    d_ready = k.stt(deltas, deltas, -1.0, deltas, ALU.mult, ALU.max, wait=t_f)
    tcol, hid2, hid_ready = F["columns"], F["hidden"], F["ready"]
    s_w3 = k.counter("filter_w3_loaded")
    conv_done = ready
    win, hbuf = k.junk[:, 0:512], k.junk[:, 512:1024]
    w3_free = [None]
    back_end = None
    HS, HDIF = U[:, 0:TC, :], U[:, TC:2 * TC, :]
    w3 = gate_row[0:64, 0:1024]
    sum_done, prev = [], [None]

    def load_filter(order):
        return k.load(w3, A["hy_w3_2"][0, :, order * 1024:(order + 1) * 1024], s_w3,
                      wait=[w3_free, hid_ready])

    def filter_tile(order, c, t_w3, u_free):
        parts = []
        for dr in range(2):
            b, bank = k.take_bank()
            end = k.mm(bank, hid2[:, c * P:(c + 1) * P], w3[:, dr * 512:(dr + 1) * 512], True, True,
                       wait=[t_w3, hid_ready, k.bank_free[b]], signal=True)
            n0 = order * 1024 + dr * 512
            e = k.activate(win, deltas[:, n0:n0 + 512], ACT.Exp, scale=tcol[:, c:c + 1],
                           wait=[d_ready, prev[0], hid_ready])
            e = k.stt((hbuf, HDIF[:, c, :])[dr], win, 0.05, bank, ALU.add, ALU.mult,
                      wait=[e, end, u_free, sum_done[-1:]])
            prev[0] = k.bank_free[b] = e
            parts.append(e)
        w3_free[0] = end
        e = k.tt(HS[:, c, :], hbuf, HDIF[:, c, :], ALU.add, wait=parts)
        sum_done.append([e, k.tt(HDIF[:, c, :], hbuf, HDIF[:, c, :], ALU.subtract, wait=[e, parts])])

    t_w3 = load_filter(0)
    k.load(dft, C["dft"].rearrange(tp, p=P), s_dft)
    k.load(alt_re, C["dft_alt_re"].rearrange(tp, p=P), s_dft)
    k.load(alt_im, C["dft_alt_im"].rearrange(tp, p=P), s_dft)
    t_dft = k.load(alt_g, C["dft_alt_back"], s_dft)
    for c in range(TC):
        filter_tile(0, c, t_w3, None)
    for order in range(2):
        t_bias = k.load(bias_row, A["hy_bias_2"][0, order].partition_broadcast(P), s_bias,
                        wait=conv_done, q=k.pool)
        k_ready = []
        for j in range(2 * TC + 1):
            b, bank = k.take_bank()
            for t in range(TC):
                if j < TC:
                    lhs, rhs = dft[:, t, j * P:(j + 1) * P], HS[:, t, :]
                elif j < 2 * TC:
                    lhs, rhs = dft[:, t, j * P:(j + 1) * P], HDIF[:, t, :]
                else:
                    lhs, rhs = alt_re[:, t, :], HS[:, t, :]
                end = k.mm(bank, lhs, rhs, t == 0, t == TC - 1, signal=t == TC - 1,
                           wait=[sum_done, t_dft, k.bank_free[b]] if t == 0 else ())
            dst = Kr[:, j, :] if j < TC else Ki[:, j - TC, :] if j < 2 * TC else KrB
            scale = tcol[:, 4:5] if j in (0, 2 * TC) else 2.0 / N_F
            e = k.ts(dst, bank, scale, None, ALU.mult, wait=[end, conv_done])
            k.bank_free[b] = e
            k_ready.append(e)
        filters_read = end
        z = [u_tok[:, t, 2 * HYW:3 * HYW] for t in range(TC)]
        u_ready = {}
        Y = hT
        prod = []
        t2 = hbuf
        last = k.dve.last()
        for m in range(TC):
            for j in (m, TC + m):
                b, bank = k.take_bank()
                for t in range(TC):
                    lhs = alt_im[:, t, :] if j == TC else dft[:, t, j * P:(j + 1) * P]
                    end = k.mm(bank, lhs, z[t], t == 0, t == TC - 1, signal=t == TC - 1,
                               wait=[conv_done, k.bank_free[b], t_dft] if t == 0 else ())
                e = k.copy(U[:, j, :], bank, wait=[end, filters_read], q=k.act)
                k.bank_free[b] = e
                u_ready[j] = e
            r, i = U[:, m, :], U[:, TC + m, :]
            krb = KrB if m == 0 else Kr[:, m, :]
            w = [u_ready[m], u_ready[TC + m], k_ready, last]
            a = k.tt(Y[:, m, :], r, Kr[:, m, :], ALU.mult, wait=w + [back_end])
            b_ = k.tt(t2, i, Ki[:, m, :], ALU.mult, wait=w)
            c_ = k.tt(Y[:, m, :], Y[:, m, :], t2, ALU.subtract, wait=[a, b_])
            d_ = k.tt(Y[:, TC + m, :], r, Ki[:, m, :], ALU.mult, wait=w + [back_end])
            e_ = k.tt(win, i, krb, ALU.mult, wait=w)
            f_ = k.tt(Y[:, TC + m, :], Y[:, TC + m, :], win, ALU.add, wait=[d_, e_])
            last = [c_, f_]
            prod += [c_, f_]
        prev[0] = last
        if order == 0:
            t_w3 = load_filter(1)
            sum_done.clear()
            sum_done.append(last)
        new = []
        for t in range(TC):
            b, bank = k.take_bank()
            for j in range(2 * TC):
                lhs = alt_g[:, t * P:(t + 1) * P] if j == TC else dft[:, j % TC, (j // TC) * T_X + t * P:(j // TC) * T_X + (t + 1) * P]
                end = k.mm(bank, lhs, Y[:, j, :], j == 0, j == 2 * TC - 1, signal=j == 2 * TC - 1,
                           wait=[prod, k.bank_free[b]] if j == 0 else ())
            back_read = end
            e = k.tt(z[t], z[t], bias_row, ALU.mult, wait=[end, list(u_ready.values()), t_bias])
            e = k.tt(z[t], z[t], bank, ALU.add, wait=e)
            k.bank_free[b] = e
            dst = z[t] if order == 0 else y[:, t, HYW:2 * HYW]
            new.append(k.tt(dst, z[t], u_tok[:, t, order * HYW:(order + 1) * HYW], ALU.mult,
                            wait=e))
            if order == 1:
                then(t, new[-1])
            else:
                filter_tile(1, t, t_w3, [prod, k.act.last()])
        back_end = back_read
        conv_done = new
    return new


def experts(k, A, y, y_ready, hT, h_ready, A2, B2, B2_ready, consts, carve, finish_tile):
    TC = T_X // P
    HALF = SLAB_N // 2
    aff, ex = carve(TC, N_EXP), carve(TC, N_EXP)
    c_ready = consts["ready"]
    logit_done = []

    def logits(t, n0, nw, bank, end):
        e = k.copy(ex[:, t, :], bank, wait=end)
        logit_done.append(e)
        return e

    k.token_gemm(A["w_router_2"][0], D, [(0, N_EXP)], hT, TC, h_ready, logits)
    mx = k.cols(8)
    e = k.dve.put(lambda en: en.tensor_reduce(mx[:, 0:4], ex, AX.X, ALU.max), wait=logit_done)
    e = k.tt(ex, ex, mx[:, 0:4].unsqueeze(2).to_broadcast([P, TC, N_EXP]), ALU.subtract, wait=e)
    e = k.activate(ex, ex, ACT.Exp, wait=e)
    e = k.dve.put(lambda en: en.tensor_reduce(mx[:, 4:8], ex, AX.X, ALU.add), wait=e)
    e = k.dve.put(lambda en: en.reciprocal(mx[:, 0:4], mx[:, 4:8]), wait=e)
    aff_ready = k.tt(aff, ex, mx[:, 0:4].unsqueeze(2).to_broadcast([P, TC, N_EXP]), ALU.mult, wait=e)
    moe = carve(TC, D)
    counts = carve(2, TC * 3)
    scrap = carve(T_X)
    hot = carve(2, TC * CAP)
    wgt = carve(2, TC * P)
    wT = carve(4, T_X)
    xs = carve(2, DC * CAP)
    hid = carve(2, (FF_E // P) * CAP)
    act_g = carve(2, HALF)
    tok_h = carve(2, HALF)
    ye = carve(4, 2 * HALF)
    zero = k.dve.put(lambda en: en.memset(counts, 0.0))
    hot_free, wgt_free, xs_free, hid_free, g_free, h_free = ([None, None] for _ in range(6))
    wT_free, ye_free = [None] * 4, [None] * 4
    prepared = {}
    wT_ready = {}
    moe_done = {}

    def choose(e_):
        i = e_ % 2
        b, bank = k.take_bank()
        for c in range(TC):
            end = k.tr(bank[:, c * P:(c + 1) * P], aff[:, c, e_:e_ + 1].to_broadcast([P, P]), signal=c == TC - 1,
                       wait=[aff_ready, k.bank_free[b]])
        cnt = counts[:, i, :].rearrange("p (t n) -> p t n", n=3)
        got = []
        for t in range(TC):
            a = aff[:, t, e_:e_ + 1]
            w = [end, zero, k.dve.last()]
            if t:
                e = k.ts(scrap[:, 0:t * P], bank[:, 0:t * P], a, None, ALU.is_ge, ALU.add, wait=w,
                         accum_out=cnt[:, t, 0:1])
                got.append(e)
                w = e
            e = k.ts(scrap[:, t * P:T_X], bank[:, t * P:T_X], a, None, ALU.is_gt, ALU.add, wait=w,
                     accum_out=cnt[:, t, 1:2])
            e2 = k.stt(scrap[:, 0:P], bank[:, t * P:(t + 1) * P], a, consts["before"], ALU.is_equal, ALU.mult,
                       accum_out=cnt[:, t, 2:3], wait=[e, c_ready])
            got += [e, e2]
        k.bank_free[b] = got[-1]
        rank = k.cols(4)
        e = k.dve.put(lambda en: en.tensor_reduce(rank, cnt, AX.X, ALU.add), wait=got)
        hots, wgts = [], []
        for t in range(TC):
            hots.append(k.ts(hot[:, i, t * CAP:(t + 1) * CAP], consts["iota"][:, 0:CAP], rank[:, t:t + 1], None,
                             ALU.is_equal, wait=[e, c_ready, hot_free[i]]))
            wgts.append(k.ts(wgt[:, i, t * P:(t + 1) * P], consts["iota"], rank[:, t:t + 1],
                             aff[:, t, e_:e_ + 1], ALU.is_equal, ALU.mult, wait=[e, c_ready, wgt_free[i]]))
        return hots, wgts

    def gather(e_, hots, wgts):
        i = e_ % 2
        b, bank = k.take_bank()
        for dc in range(DC):
            for t in range(TC):
                end = k.mm(bank[:, dc * CAP:(dc + 1) * CAP], y[:, t, dc * P:(dc + 1) * P],
                           hot[:, i, t * CAP:(t + 1) * CAP], t == 0, t == TC - 1,
                           signal=t == TC - 1 and dc == DC - 1,
                           wait=[hots, y_ready, k.bank_free[b]] if t + dc == 0 else ())
        hot_free[i] = end
        x3 = xs[:, i, :].rearrange("p (d r) -> p d r", r=CAP)
        e = k.tt(x3, bank.rearrange("p (d r) -> p d r", r=CAP), A2.unsqueeze(2).to_broadcast([P, DC, CAP]),
                 ALU.mult, wait=[end, xs_free[i], B2_ready])
        k.bank_free[b] = e
        prepared[e_] = k.tt(x3, x3, B2.unsqueeze(2).to_broadcast([P, DC, CAP]), ALU.add, wait=e)
        b, bank = k.take_bank()
        for t in range(TC):
            end = k.tr(bank[:, t * P:(t + 1) * P], wgt[:, i, t * P:(t + 1) * P], signal=t == TC - 1,
                       wait=[wgts, k.bank_free[b]])
        wgt_free[i] = end
        wT_ready[e_] = k.bank_free[b] = k.copy(wT[:, e_ % 4, :], bank, wait=[end, wT_free[e_ % 4]], q=k.act)

    def scatter(pair, t):
        for half in range(2):
            rows = slice(half * CAP, (half + 1) * CAP)
            b, bank = k.take_bank()
            for n in range(2):
                for e_ in (2 * pair, 2 * pair + 1):
                    end = k.mm(bank[:, n * HALF:(n + 1) * HALF], wT[rows, e_ % 4, t * P:(t + 1) * P],
                               ye[rows, e_ % 4, n * HALF:(n + 1) * HALF], e_ % 2 == 0, e_ % 2 == 1,
                               signal=n + e_ % 2 == 2,
                               wait=[wT_ready[e_], ye_ready[e_], k.bank_free[b]])
            o = moe[:, t, :].rearrange("p (n h d) -> p n h d", n=2, h=2)[:, :, half, :]
            rows_in = bank.rearrange("p (n d) -> p n d", n=2)
            if pair == 0:
                e = k.copy(o, rows_in, wait=end)
            else:
                e = k.tt(o, o, rows_in, ALU.add, wait=[end, moe_done[(t, half)]])
            k.bank_free[b] = e
            moe_done[(t, half)] = e
        if t == TC - 1:
            for e_ in (2 * pair, 2 * pair + 1):
                wT_free[e_ % 4] = ye_free[e_ % 4] = end

    def weights_past(act_T, chunk0, slabs, w, ready):
        b, bank = k.take_bank()
        for n, (k0, n0) in enumerate(slabs):
            slot, slab, loaded = k.load_slab(w, k0, DC, n0, SLAB_N)
            for kc in range(DC):
                f = chunk0 + n * DC + kc
                for half in range(2):
                    end = k.mm(bank[half * CAP:(half + 1) * CAP, 0:HALF], act_T[:, f * CAP:(f + 1) * CAP],
                               slab[:, kc, half * HALF:(half + 1) * HALF], n + kc == 0,
                               n == len(slabs) - 1 and kc == DC - 1, signal=kc == DC - 1 and half == 1,
                               wait=[loaded, ready, k.bank_free[b]] if kc + half == 0 else ())
            k.slab_free[slot] = end
        return b, bank[:, 0:HALF], end

    ye_ready = {}
    gather(0, *choose(0))
    for e_ in range(N_EXP):
        i = e_ % 2
        hid_ready = []

        def to_hidden(s, h, have):
            b, bank = k.take_bank()
            for q in range(2):
                end = k.tr(bank[:, q * P:(q + 1) * P], h[:, q * P:(q + 1) * P], signal=q == 1,
                           wait=[have, k.bank_free[b]])
            h_free[s % 2] = end
            dst = hid[:, i, s * 4 * CAP:(s + 1) * 4 * CAP].rearrange("p (h q r) -> p q h r", h=2, q=2)
            src = bank[:, 0:2 * P].rearrange("p (q h r) -> p q h r", q=2, h=2)
            for q in range(2):
                e = k.copy(dst[:, q], src[:, q], wait=[end, hid_free[i]], q=k.act)
                hid_ready.append(e)
            k.bank_free[b] = e

        chosen = choose(e_ + 1) if e_ + 1 < N_EXP else None
        last = None
        for s in range(FF_E // SLAB_N):
            bg, gate, end_g = weights_past(xs[:, i], 0, [(0, s * SLAB_N)], A["w_gate_2"][0, e_], prepared[e_])
            bu, up, end_u = weights_past(xs[:, i], 0, [(0, s * SLAB_N)], A["w_up_2"][0, e_], prepared[e_])
            g, h = act_g[:, s % 2, :], tok_h[:, s % 2, :]
            e = k.activate(g, gate, ACT.Silu, wait=[end_g, g_free[s % 2]])
            k.bank_free[bg] = e
            e = k.tt(h, g, up, ALU.mult, wait=[e, end_u, h_free[s % 2]])
            k.bank_free[bu] = g_free[s % 2] = e
            if last is not None:
                to_hidden(*last)
            last = (s, h, e)
            if e_ % 2 == 0 and e_:
                scatter(e_ // 2 - 1, s)
        xs_free[i] = end_u
        if chosen:
            gather(e_ + 1, *chosen)
        to_hidden(*last)
        outs = []
        for n in range(2):
            b, bank, end = weights_past(hid[:, i], 0, [(0, n * SLAB_N), (DC * P, n * SLAB_N)],
                                        A["w_down_2"][0, e_], hid_ready)
            e = k.copy(ye[:, e_ % 4, n * HALF:(n + 1) * HALF], bank, wait=[end, ye_free[e_ % 4]], q=k.act)
            k.bank_free[b] = e
            outs.append(e)
        hid_free[i] = end
        ye_ready[e_] = outs
    for t in range(TC):
        scatter(N_EXP // 2 - 1, t)
        finish_tile(t, moe[:, t, :], [moe_done[(t, 0)], moe_done[(t, 1)]])


def second_block(k, A, C, out, x, hT, y, gate_row, carve, new_phase, S):
    ready = S["cols_ready"]
    mod2 = S["mod2"]
    mod_ready = S["mod2_ready"]
    new_phase()
    TC = T_X // P
    consts_t = carve(6, P)
    u_tok = carve(TC, 3 * HYW)
    J, ones, tri, before = consts_t[:, 0, :], consts_t[:, 1, :], consts_t[:, 2:4, :], consts_t[:, 4, :]
    iota = consts_t[:, 5, :]
    s_c = k.counter("mixer_consts_loaded")
    k.load(J, C["flip"], s_c, q=k.pool)
    k.load(tri, C["tri"].rearrange("a p b -> p a b"), s_c, q=k.pool)
    k.load(before, C["before"], s_c, q=k.pool)
    k.load(iota, C["iota"].partition_broadcast(P), s_c, q=k.pool)
    after_u = 6 * P + TC * 3 * HYW
    qkT = carve(2 * MH, T_X)
    vpad = carve(TC * MH, 129)
    o_sig = carve(TC, 512)
    gates = carve(TC, 16)
    gsel, state_max = carve(TC * 4, 8), carve(64)
    after_gates = after_u + sum(int(np.prod(v.shape[1:])) for v in (qkT, vpad, o_sig, gates, gsel, state_max))
    b_row = carve(1040)
    raw = carve(2, T_X)
    conv = carve(2, T_X)
    t_c = k.load(b_row, A["b_in_2"][0, 1024:2064].partition_broadcast(P), s_c, q=k.pool)
    e1 = k.dve.put(lambda e: e.memset(ones, 1.0))
    e2 = k.dve.put(lambda e: e.memset(vpad[:, :, 128:129], 1.0))
    consts = {"J": J, "ones": ones, "tri": tri, "before": before, "iota": iota, "ready": [t_c, e1]}
    gmix, e = S["scale_cols"](mod2, 0, 8, S["g_mixT"], [mod_ready, ready])
    normed = k.modulated(y, TC, S["x_scaled"], gmix, mod2[:, 0:8, 0], [e, mod_ready], hT, k.pe.last())
    state = {"raw_free": [None, None], "conv_free": [None, None], "n": 0}
    W_in = A["w_in_2"][0]

    qk_done = []

    def qk_evac(j, bank, end):
        i = state["n"] % 2
        state["n"] += 1
        r = raw[:, i, :]
        e0 = k.activate(r, bank, ACT.Identity, bias=S["b_qkT"][:, j:j + 1], wait=[end, state["raw_free"][i]])
        w = [S["conv_qk_wT"][:, 8 * n + j:8 * n + j + 1] for n in range(3)]
        e = short_conv(k, conv[:, i, :], r, w, S["conv_qk_bT"][:, j:j + 1], T_X, [e0, state["conv_free"][i]])
        state["raw_free"][i] = e
        e = k.activate(qkT[:, j, :], conv[:, i, :], ACT.Silu, wait=e)
        state["conv_free"][i] = e
        if j >= MH:
            e = k.ts(qkT[:, j, :], qkT[:, j, :], MD ** -0.5, None, ALU.mult, wait=e)
        qk_done.append(e)
        return e0

    k.feature_gemm(W_in, 0, 1024, hT, T_X, normed, qk_evac)
    vo_done = []

    def vo_evac(t, n0, nw, bank, end):
        row = b_row[:, n0 - 1024:n0 - 1024 + nw]
        if n0 == 1024:
            o = vpad[:, t * MH:(t + 1) * MH, 0:128]
            e = k.tt(o, bank.rearrange("p (h d) -> p h d", d=128), row.rearrange("p (h d) -> p h d", d=128),
                     ALU.add, wait=[end, t_c])
        else:
            e = k.tt(o_sig[:, t, :] if n0 == 1536 else gates[:, t, :], bank, row, ALU.add, wait=[end, t_c])
        vo_done.append(e)
        return e

    k.token_gemm(W_in, D, [(1024, 512), (1536, 512), (2048, 16)], hT, TC, normed, vo_evac)
    G, F = {}, {}
    chain = itertools.chain(
        gate_rows(k, qkT, gates, y, S["cx"], gsel, state_max, consts, [qk_done, vo_done], G),
        filter_network(k, A, C, k.junk[:, 0:512], k.junk[:, 512:1024], gate_row[:, 0:512], gate_row[:, 512:1024],
                       S["mod_sums"][:, :], [k.junk_free, k.dve.last(), k.pe.last()], F))
    u_done = []

    def hx_evac(j, bank, end):
        i = state["n"] % 2
        state["n"] += 1
        r = raw[:, i, :]
        e0 = k.activate(r, bank, ACT.Identity, bias=S["b_hxT"][:, j:j + 1], wait=[end, state["raw_free"][i]])
        w = [S["conv_hy_wT"][:, 12 * n + j:12 * n + j + 1] for n in range(3)]
        e = short_conv(k, conv[:, i, :], r, w, S["conv_hy_bT"][:, j:j + 1], T_X, [e0, state["conv_free"][i]])
        state["raw_free"][i] = e
        hx_pending.append((j, i, e))
        next(chain, None)
        if len(hx_pending) > 1:
            hx_transpose(*hx_pending.pop(0))
        return e0

    hx_pending = []

    def hx_transpose(j, i, have):
        b, bank = k.take_bank()
        for t in range(TC):
            end = k.tr(bank[:, t * P:(t + 1) * P], conv[:, i, t * P:(t + 1) * P], signal=t == TC - 1,
                       wait=[have, k.bank_free[b]])
        state["conv_free"][i] = end
        e = k.copy(u_tok[:, :, j * P:(j + 1) * P], bank.rearrange("p (t c) -> p t c", c=P), wait=end, q=k.act)
        k.bank_free[b] = e
        u_done.append(e)

    k.feature_gemm(W_in, 2064, 1536, hT, T_X, normed, hx_evac)
    while hx_pending:
        hx_transpose(*hx_pending.pop(0))
    k.finish(chain)
    k.barrier()
    S["rewind"](after_gates)
    s_g = k.counter("mixer_gains_loaded")
    gain, square = k.junk[:, 0:512], k.junk[:, 512:1024].rearrange("p (t d) -> p t d", d=P)
    t_g = k.load(gain, A["mlstm_norm_g_2"][0].partition_broadcast(P), s_g, wait=F["ready"], q=k.pool)
    sg = [k.activate(o_sig[:, t, :], o_sig[:, t, :], ACT.Sigmoid, wait=vo_done) for t in range(TC)]
    m_done = []

    def head_done(h, ready):
        v = y[:, :, h * P:(h + 1) * P]
        e = k.tt(square, v, v, ALU.mult, wait=[ready, F["ready"], k.dve.last()])
        sums = k.cols(TC)
        e = k.dve.put(lambda en: en.tensor_reduce(sums, square, AX.X, ALU.add), wait=e)
        rstd, have = k.inv_rms(sums, TC, MD, e)
        e = k.tt(v, v, rstd.unsqueeze(2).to_broadcast([P, TC, P]), ALU.mult, wait=have)
        e = k.tt(v, v, gain[:, h * P:(h + 1) * P].unsqueeze(1).to_broadcast([P, TC, P]), ALU.mult, wait=[e, t_g])
        m_done.append(k.tt(v, v, o_sig[:, :, h * P:(h + 1) * P], ALU.mult, wait=[e, sg]))

    mlstm(k, qkT, vpad, G, S["cx"], y, consts, [qk_done, vo_done, e2], carve, head_done)
    k.barrier()
    S["rewind"](after_u)
    s_g2 = k.counter("hyena_gain_loaded")
    t_g2 = []

    def hyena_tile(t, ready):
        if t == 0:
            t_g2.append(k.load(k.junk[:, 0:512], A["hyena_norm_g_2"][0].partition_broadcast(P), s_g2,
                               wait=ready, q=k.pool))
        m_done.append(group_rms(k, y[:, t, 512:1024], 4, P, k.junk[:, 0:512], t_g2, k.junk[:, 512:1024], ready))

    hyena(k, u_tok, A, C, F, S["cx"], hT, y, gate_row, carve, u_done, hyena_tile)
    tr_done = k.to_features(y, TC, m_done, hT, None)
    g_ready = k.columns_to_rows(mod2[:, 16:24, 0], 8, gate_row, mod_ready, None)
    tr_end = k.pe.last()
    res, x_scaled = {t: [] for t in range(TC)}, []

    def out_evac(t, n0, nw, bank, end):
        e = k.tt(y[:, t, n0:n0 + nw], bank, gate_row[:, n0:n0 + nw], ALU.mult, wait=[end, tr_end, g_ready])
        res[t].append(k.tt(x[:, t, n0:n0 + nw], x[:, t, n0:n0 + nw], y[:, t, n0:n0 + nw], ALU.add, wait=e))
        if n0 + nw == D:
            x_scaled.append(k.normed_tile(x, t, res[t], y, None))
        return e

    k.token_gemm(A["w_out_2"][0], D, [(0, 512), (512, 512)], hT, TC, tr_done, out_evac)
    k.barrier()
    S["rewind"](6 * P)
    gffn, e = S["scale_cols"](mod2, 0, 32, S["g_ffnT"], [mod_ready, ready])
    normed = k.modulated(y, TC, x_scaled, gffn, mod2[:, 24:32, 0], [e, mod_ready], hT, k.pe.last())
    y_ready = x_scaled
    g_ready = k.columns_to_rows(mod2[:, 40:48, 0], 8, gate_row, mod_ready, k.dve.last())
    fin_row = k.junk[:, :]
    s_fin = k.counter("final_gain_loaded")
    t_fin = k.load(fin_row, A["g_final_2"].partition_broadcast(P), s_fin, wait=k.junk_free, q=k.pool)
    s_out = k.counter("output_written")
    written = []

    def finish_tile(t, m, ready):
        e = k.tt(m, m, gate_row[:, :], ALU.mult, wait=[ready, g_ready])
        e = k.tt(m, m, x[:, t, :], ALU.add, wait=e)
        sums = k.cols(1)
        e = k.activate(y[:, t, :], m, ACT.Square, accum_out=sums, wait=[e, k.pe.last()])
        rstd, have = k.inv_rms(sums, 1, D, e)
        e = k.stt(m, m, rstd, fin_row, ALU.mult, ALU.mult, wait=[have, t_fin])
        written.append(k.load(out[t * P:(t + 1) * P, :], m, s_out, wait=e))

    experts(k, A, y, y_ready, hT, normed, gffn, mod2[:, 24:32, 0], [e, mod_ready], consts,
                            carve, finish_tile)
    k.sp.hold(written)
    k.sp.hold(S["scratch_done"])


ROUND = 1.5 * 2.0 ** 23
TWO_PI = (6.28125, 0.0019350051879882812, 3.0199159819567e-07)


def tables():
    f = np.float32
    C = {"ident": np.eye(P, dtype=f), "flip": np.eye(P, dtype=f)[::-1].copy()}
    t = np.arange(T_X)
    pos = np.stack([t // GRID, t % GRID], -1).astype(f)
    inv = (f(10000.0) ** (-np.arange(16, dtype=f) / f(16))).astype(f)
    ang = (pos[:, :, None] * inv).astype(f)
    cos, sin = np.cos(ang).astype(f), np.sin(ang).astype(f)
    C["rope_cos"] = np.stack([cos, cos], 2).reshape(T_X, HD)
    C["rope_sin"] = np.stack([-sin, sin], 2).reshape(T_X, HD)
    q, c = np.arange(GRID)[:, None], np.arange(GRID)[None, :]
    start = np.clip(q - 8, 0, GRID - 16)
    valid = (c >= start) & (c < start + 16)
    off = np.clip(c - q, -15, 15) + 15
    hot = np.zeros((32, GRID, GRID), f)
    for d in range(RPB_COLS):
        hot[d] = (off == d) & valid
    hot[31] = np.where(valid, 0.0, NEG)
    C["neighbour_onehot"] = hot.reshape(32, GRID * GRID)
    i, j = np.arange(P)[:, None], np.arange(P)[None, :]
    C["window_masks"] = np.concatenate([np.where(j >= i, 0.0, NEG), np.where(j <= i, 0.0, NEG)], 1).astype(f)
    C["tri"] = np.stack([i <= j, i >= j]).astype(f)
    C["before"] = (j < i).astype(f)
    C["pick"] = (np.arange(P)[:, None] % 32 == np.arange(3)[None, :]).astype(f)
    C["iota"] = (np.arange(P) % CAP).astype(f)
    L = T_X
    tl = np.linspace(0.0, 1.0, L, dtype=f)[:, None]
    w = (f(2.0 * math.pi) * np.arange(L, dtype=f)[:, None] / f(L)).astype(f)
    bands = np.linspace(1e-4, 15, 16, dtype=f)[None, :]
    C["hyena_z"] = np.concatenate([tl, np.cos(bands * w), -np.sin(bands * w)], -1).astype(f).T.copy()
    cols = np.zeros((P, 6), f)
    cols[:, 0:4] = -tl.reshape(4, P).T
    cols[:, 4] = 2.0 / (2 * L)
    cols[0, 4] = 1.0 / (2 * L)
    C["hyena_cols"] = cols
    n = np.arange(L)
    ph = 2.0 * np.pi * ((n[:, None] * n[None, :]) % (2 * L)) / (2 * L)
    re, im = np.cos(ph), -np.sin(ph)
    alt = np.where(n % 2 == 0, 1.0, -1.0)
    C["dft"] = np.concatenate([re, im], 1).astype(f)
    are, aim = re[:, 0:P].copy(), im[:, 0:P].copy()
    are[:, 0] = alt
    aim[:, 0] = alt
    C["dft_alt_re"], C["dft_alt_im"] = are.astype(f), aim.astype(f)
    C["dft_alt_back"] = aim.T.astype(f).copy()
    return C


_INS = ["x", "c", "ctx", "c_ctx", "w_mod", "b_mod", "norm_g", "w_in", "w_out", "w_mlp_in", "w_mlp_out",
        "qk_norm_a", "diff_lambda", "diff_subln", "sink_c", "rpb_d", "c_2", "w_ada_2", "b_ada_2", "g_mix_2",
        "w_in_2", "b_in_2", "conv_qk_w_2", "conv_qk_b_2", "mlstm_norm_g_2", "conv_hy_w_2", "conv_hy_b_2",
        "hy_w1_2", "hy_b1_2", "hy_w2_2", "hy_b2_2", "hy_w3_2", "hy_freq_2", "hy_deltas_2", "hy_bias_2",
        "hyena_norm_g_2", "w_out_2", "g_ffn_2", "w_router_2", "w_gate_2", "w_up_2", "w_down_2", "g_final_2"]


def kernel(**inputs):
    import numpy as _np
    import concourse.bacc as _bacc
    from concourse import mybir as _mybir
    from concourse.bass_utils import run_bass_kernel_spmd as _run

    nc = _bacc.Bacc("TRN2", target_bir_lowering=False, num_devices=1)
    arrays, A, C = {}, {}, {}
    for group, named in ((A, {n: inputs[n] for n in _INS}), (C, tables())):
        for name, value in named.items():
            a = _np.ascontiguousarray(value)
            full = f"in_{name}" if group is A else f"table_{name}"
            arrays[full] = a
            group[name] = nc.dram_tensor(full, a.shape, _mybir.dt.from_np(a.dtype), kind="ExternalInput").ap()
    out = nc.dram_tensor("out", (T_X, D), F32, kind="ExternalOutput").ap()
    build(nc, A, C, out)
    r = _run(nc, [arrays], core_ids=[0])
    return r.results[0]["out"].reshape(1, T_X, D)
```
